# Optimizing a Trainium2 kernel written in Bass

```python
import jax, jax.numpy as jnp
from jax import lax
import numpy as np
import math

D_MODEL = 1024
BATCH = 1
SEQ = 1024
DEPTH = 1

CHUNK = 64
D_POOL = D_MODEL // 2
POOL_WINDOWS = (2, 4, 8, 16)
POOL_GROUPS = len(POOL_WINDOWS)
POOL_GC = D_POOL // POOL_GROUPS
D_MLSTM = D_MODEL // 2
N_HEADS = 4
HEAD_DIM = D_MLSTM // N_HEADS
CONV_K = 4
N_GROUPS = 4
EXPERTS_PER_GROUP = 8
N_EXPERTS = N_GROUPS * EXPERTS_PER_GROUP
TOP_K = 2
D_EXPERT = D_MODEL // 2
MOE_BLOCK = 128
EPS = 1e-6
SPLIT_SIZES = (D_POOL, D_MLSTM, D_MLSTM, D_MLSTM, D_MLSTM, N_HEADS, N_HEADS, D_MODEL, D_MODEL)
N_IN = sum(SPLIT_SIZES)


def rmsnorm(x, g):
    xf = x.astype(jnp.float32)
    y = xf * lax.rsqrt(jnp.mean(xf * xf, axis=-1, keepdims=True) + EPS) * g.astype(jnp.float32)
    return y.astype(x.dtype)

def pool_mixer(u, w_pool, pool_scale):
    B, S, _ = u.shape
    uf = u.astype(jnp.float32)
    cs = jnp.pad(jnp.cumsum(uf, axis=1), ((0, 0), (1, 0), (0, 0)))
    t = jnp.arange(S)
    outs = []
    for g, w in enumerate(POOL_WINDOWS):
        sl = slice(g * POOL_GC, (g + 1) * POOL_GC)
        start = jnp.maximum(t + 1 - w, 0)
        win_sum = cs[:, 1:, sl] - cs[:, start, sl]
        cnt = (t + 1 - start).astype(jnp.float32)
        outs.append(win_sum / cnt[None, :, None] - uf[:, :, sl])
    d = jnp.stack(outs, axis=2)
    y = jnp.einsum('bsgc,gcd->bsgd', d, w_pool.astype(jnp.float32)).reshape(B, S, D_POOL)
    return (y * pool_scale.astype(jnp.float32)).astype(u.dtype)

def causal_conv(u, w):
    S = u.shape[1]
    up = jnp.pad(u, ((0, 0), (CONV_K - 1, 0), (0, 0)))
    return sum(up[:, j:j + S, :] * w[j] for j in range(CONV_K))

def mlstm_chunkwise(q, k, v, i_pre, f_pre):
    B, S, H, Dh = q.shape
    NC, L = S // CHUNK, CHUNK

    def to_chunks(a):
        a = a.astype(jnp.float32).reshape((B, NC, L, H) + a.shape[3:])
        return jnp.moveaxis(a, 3, 1)

    q = to_chunks(q)
    k = to_chunks(k) * (Dh ** -0.5)
    v = to_chunks(v)
    ig = to_chunks(i_pre)
    lf = jax.nn.log_sigmoid(to_chunks(f_pre))
    b = jnp.cumsum(lf, axis=-1)
    b_last = b[..., -1]

    a_log = b_last[..., None] - b + ig
    a_max = jnp.max(a_log, axis=-1)
    w_loc = jnp.exp(a_log - a_max[..., None])
    C_loc = jnp.einsum('bhcld,bhcle->bhcde', w_loc[..., None] * k, v)
    n_loc = jnp.einsum('bhcl,bhcld->bhcd', w_loc, k)

    def step(carry, inp):
        C, n, m = carry
        bl, am, Cl, nl = inp
        m_new = jnp.maximum(bl + m, am)
        s_prev = jnp.exp(bl + m - m_new)
        s_loc = jnp.exp(am - m_new)
        C_new = s_prev[..., None, None] * C + s_loc[..., None, None] * Cl
        n_new = s_prev[..., None] * n + s_loc[..., None] * nl
        return (C_new, n_new, m_new), (C, n, m)

    init = (jnp.zeros((B, H, Dh, Dh), jnp.float32), jnp.zeros((B, H, Dh), jnp.float32),
            jnp.zeros((B, H), jnp.float32))
    xs = (jnp.moveaxis(b_last, 2, 0), jnp.moveaxis(a_max, 2, 0),
          jnp.moveaxis(C_loc, 2, 0), jnp.moveaxis(n_loc, 2, 0))
    _, (C_prev, n_prev, m_prev) = lax.scan(step, init, xs)
    C_prev = jnp.moveaxis(C_prev, 0, 2)
    n_prev = jnp.moveaxis(n_prev, 0, 2)
    m_prev = jnp.moveaxis(m_prev, 0, 2)

    inter_log = b + m_prev[..., None]
    causal = jnp.tril(jnp.ones((L, L), dtype=bool))
    D = b[..., :, None] - b[..., None, :] + ig[..., None, :]
    D = jnp.where(causal, D, -jnp.inf)
    m_t = jnp.maximum(inter_log, jnp.max(D, axis=-1))
    w_inter = jnp.exp(inter_log - m_t)
    s = jnp.einsum('bhctd,bhcsd->bhcts', q, k) * jnp.exp(D - m_t[..., None])
    num = (w_inter[..., None] * jnp.einsum('bhctd,bhcde->bhcte', q, C_prev)
           + jnp.einsum('bhcts,bhcse->bhcte', s, v))
    nq = w_inter * jnp.einsum('bhctd,bhcd->bhct', q, n_prev) + jnp.sum(s, axis=-1)
    den = jnp.maximum(jnp.abs(nq), jnp.exp(-m_t))
    h = num / den[..., None]
    return jnp.moveaxis(h, 1, 3).reshape(B, S, H, Dh)

def head_layernorm(h, g):
    B, S, H, Dh = h.shape
    mu = jnp.mean(h, axis=-1, keepdims=True)
    var = jnp.mean(jnp.square(h - mu), axis=-1, keepdims=True)
    hn = (h - mu) * lax.rsqrt(var + EPS)
    return hn * g.astype(jnp.float32).reshape(H, Dh)

def hybrid_mixer(h, w_in, b_if, conv_q, conv_k, g_head, w_pool, pool_scale, w_br_a, w_br_b, w_out):
    B, S, _ = h.shape
    z = h @ w_in
    idx = [int(c) for c in np.cumsum(SPLIT_SIZES)[:-1]]
    u_pool, q, k, v, o, i_pre, f_pre, ga, gb = jnp.split(z, idx, axis=-1)
    y_a = pool_mixer(u_pool, w_pool, pool_scale) @ w_br_a
    q = jax.nn.silu(causal_conv(q, conv_q)).reshape(B, S, N_HEADS, HEAD_DIM)
    k = jax.nn.silu(causal_conv(k, conv_k)).reshape(B, S, N_HEADS, HEAD_DIM)
    v = v.reshape(B, S, N_HEADS, HEAD_DIM)
    i_pre = i_pre.astype(jnp.float32) + b_if[:N_HEADS].astype(jnp.float32)
    f_pre = f_pre.astype(jnp.float32) + b_if[N_HEADS:].astype(jnp.float32)
    hm = mlstm_chunkwise(q, k, v, i_pre, f_pre)
    hm = head_layernorm(hm, g_head).reshape(B, S, D_MLSTM)
    hm = (jax.nn.sigmoid(o.astype(jnp.float32)) * hm).astype(h.dtype)
    y_b = hm @ w_br_b
    merged = jax.nn.sigmoid(ga) * y_a + jax.nn.sigmoid(gb) * y_b
    return merged @ w_out

def hier_moe(h, w_rg, b_rg, w_re, b_re, w_gate, w_up, w_down):
    B, S, D = h.shape
    T = B * S
    xt = h.reshape(T, D)
    g_logits = (xt @ w_rg).astype(jnp.float32) + b_rg.astype(jnp.float32)
    g_prob = jax.nn.softmax(g_logits, axis=-1)
    g_sel = jnp.argmax(g_logits, axis=-1)
    p_g = jnp.take_along_axis(g_prob, g_sel[:, None], axis=-1)
    e_logits = ((xt @ w_re).astype(jnp.float32) + b_re.astype(jnp.float32)).reshape(
        T, N_GROUPS, EXPERTS_PER_GROUP)
    e_sel = jnp.take_along_axis(e_logits, g_sel[:, None, None], axis=1)[:, 0]
    top_p, top_i = lax.top_k(jax.nn.softmax(e_sel, axis=-1), TOP_K)
    gate = p_g * top_p / jnp.sum(top_p, axis=-1, keepdims=True)
    expert_id = g_sel[:, None] * EXPERTS_PER_GROUP + top_i

    A = T * TOP_K
    flat_e = expert_id.reshape(A)
    flat_tok = jnp.repeat(jnp.arange(T), TOP_K)
    flat_w = gate.reshape(A)
    order = jnp.argsort(flat_e)
    e_s, tok_s, w_s = flat_e[order], flat_tok[order], flat_w[order]
    counts = jnp.bincount(flat_e, length=N_EXPERTS)
    padded = (counts + MOE_BLOCK - 1) // MOE_BLOCK * MOE_BLOCK
    off = jnp.cumsum(counts) - counts
    pend = jnp.cumsum(padded)
    poff = pend - padded
    dest = poff[e_s] + jnp.arange(A) - off[e_s]
    n_rows = A + N_EXPERTS * MOE_BLOCK
    n_blocks = n_rows // MOE_BLOCK
    buf = jnp.zeros((n_rows, D), h.dtype).at[dest].set(xt[tok_s])
    block_e = jnp.clip(jnp.searchsorted(pend, jnp.arange(n_blocks) * MOE_BLOCK, side='right'),
                       0, N_EXPERTS - 1)

    def run_block(args):
        xb, e = args
        hid = jax.nn.silu(xb @ w_gate[e]) * (xb @ w_up[e])
        return hid @ w_down[e]

    yb = lax.map(run_block, (buf.reshape(n_blocks, MOE_BLOCK, D), block_e)).reshape(n_rows, D)
    y = jnp.zeros((T, D), jnp.float32).at[tok_s].add(yb[dest].astype(jnp.float32) * w_s[:, None])
    return y.reshape(B, S, D).astype(h.dtype)

def first_inputs(seed: int = 0) -> dict:
    key = jax.random.key(seed)
    ks = jax.random.split(key, 24)
    nrm = jax.random.normal
    f32 = jnp.float32
    x = nrm(ks[0], (BATCH, SEQ, D_MODEL), f32)
    g_mix = 1.0 + 0.1 * nrm(ks[1], (DEPTH, D_MODEL), f32)
    w_in = nrm(ks[2], (DEPTH, D_MODEL, N_IN), f32) * D_MODEL ** -0.5
    b_i = 0.1 * nrm(ks[3], (DEPTH, N_HEADS), f32)
    b_f = jnp.linspace(3.0, 6.0, N_HEADS, dtype=f32)[None] + 0.1 * nrm(ks[4], (DEPTH, N_HEADS), f32)
    b_if = jnp.concatenate([b_i, b_f], axis=-1)
    conv_q = nrm(ks[5], (DEPTH, CONV_K, D_MLSTM), f32) * CONV_K ** -0.5
    conv_k = nrm(ks[6], (DEPTH, CONV_K, D_MLSTM), f32) * CONV_K ** -0.5
    g_head = 1.0 + 0.1 * nrm(ks[7], (DEPTH, D_MLSTM), f32)
    w_pool = nrm(ks[8], (DEPTH, POOL_GROUPS, POOL_GC, POOL_GC), f32) * POOL_GC ** -0.5
    pool_scale = 1.0 + 0.1 * nrm(ks[9], (DEPTH, D_POOL), f32)
    w_br_a = nrm(ks[10], (DEPTH, D_POOL, D_MODEL), f32) * D_POOL ** -0.5
    w_br_b = nrm(ks[11], (DEPTH, D_MLSTM, D_MODEL), f32) * D_MLSTM ** -0.5
    w_out = nrm(ks[12], (DEPTH, D_MODEL, D_MODEL), f32) * D_MODEL ** -0.5
    g_ffn = 1.0 + 0.1 * nrm(ks[13], (DEPTH, D_MODEL), f32)
    w_rg = nrm(ks[14], (DEPTH, D_MODEL, N_GROUPS), f32) * D_MODEL ** -0.5
    b_rg = 0.01 * nrm(ks[15], (DEPTH, N_GROUPS), f32)
    w_re = nrm(ks[16], (DEPTH, D_MODEL, N_EXPERTS), f32) * D_MODEL ** -0.5
    b_re = 0.01 * nrm(ks[17], (DEPTH, N_EXPERTS), f32)
    w_e_gate = nrm(ks[18], (DEPTH, N_EXPERTS, D_MODEL, D_EXPERT), f32) * D_MODEL ** -0.5
    w_e_up = nrm(ks[19], (DEPTH, N_EXPERTS, D_MODEL, D_EXPERT), f32) * D_MODEL ** -0.5
    w_e_down = nrm(ks[20], (DEPTH, N_EXPERTS, D_EXPERT, D_MODEL), f32) * D_EXPERT ** -0.5
    g_final = 1.0 + 0.1 * nrm(ks[21], (D_MODEL,), f32)
    return {"x": x, "g_mix": g_mix, "w_in": w_in, "b_if": b_if, "conv_q": conv_q,
            "conv_k": conv_k, "g_head": g_head, "w_pool": w_pool, "pool_scale": pool_scale,
            "w_br_a": w_br_a, "w_br_b": w_br_b, "w_out": w_out, "g_ffn": g_ffn,
            "w_rg": w_rg, "b_rg": b_rg, "w_re": w_re, "b_re": b_re, "w_e_gate": w_e_gate,
            "w_e_up": w_e_up, "w_e_down": w_e_down, "g_final": g_final}

def first_block(x, g_mix, w_in, b_if, conv_q, conv_k, g_head, w_pool, pool_scale, w_br_a, w_br_b,
              w_out, g_ffn, w_rg, b_rg, w_re, b_re, w_e_gate, w_e_up, w_e_down, g_final):
    for l in range(DEPTH):
        x = x + hybrid_mixer(rmsnorm(x, g_mix[l]), w_in[l], b_if[l], conv_q[l], conv_k[l],
                             g_head[l], w_pool[l], pool_scale[l], w_br_a[l], w_br_b[l], w_out[l])
        x = x + hier_moe(rmsnorm(x, g_ffn[l]), w_rg[l], b_rg[l], w_re[l], b_re[l],
                         w_e_gate[l], w_e_up[l], w_e_down[l])
    return rmsnorm(x, g_final)


DEPTH_2 = 2

HEAD_DIM_2 = 64
BLOCK = 128
A_HEADS = 8
A_KV_HEADS = 2
A_WINDOW = 128
B_HEADS = 8
B_CONFIGS = ((128, 1), (512, 4), (2048, 16))
NUM_BUCKETS = 32
MAX_DISTANCE = 2048
C_HEADS = 16
C_Q_RANK = 256
C_KV_RANK = 128
C_NOPE = 64
C_ROPE = 32
C_V = 64
ROPE_THETA = 10000.0

A_WIDTH = A_HEADS * HEAD_DIM_2
A_KV_WIDTH = A_KV_HEADS * HEAD_DIM_2
B_WIDTH = B_HEADS * HEAD_DIM_2
AB_WIDTH = A_WIDTH + B_WIDTH
AB_IN = A_WIDTH + 2 * A_KV_WIDTH + 3 * B_WIDTH + AB_WIDTH
C_WIDTH = C_HEADS * C_V
C_IN = C_Q_RANK + C_KV_RANK + C_ROPE + C_WIDTH
N_AB = (DEPTH_2 + 1) // 2
N_C = DEPTH_2 // 2


def rmsnorm_2(x, w):
    xf = x.astype(jnp.float32)
    y = xf * lax.rsqrt(jnp.mean(xf * xf, axis=-1, keepdims=True) + EPS)
    return (y * w.astype(jnp.float32)).astype(x.dtype)

def t5_bucket(dist):
    max_exact = NUM_BUCKETS // 2
    d = jnp.maximum(dist, 1).astype(jnp.float32)
    large = max_exact + (jnp.log(d / max_exact) / math.log(MAX_DISTANCE / max_exact)
                         * (NUM_BUCKETS - max_exact)).astype(jnp.int32)
    large = jnp.minimum(large, NUM_BUCKETS - 1)
    return jnp.where(dist < max_exact, dist, large)

def band_bias(rel_bias_h, dilation, window):
    i = jnp.arange(BLOCK)[:, None]
    j = jnp.arange(2 * BLOCK)[None, :]
    dist = i + BLOCK - j
    in_band = (dist >= 0) & (dist <= window)
    bucket = t5_bucket(jnp.maximum(dist, 0) * dilation)
    bias = jnp.transpose(rel_bias_h[bucket].astype(jnp.float32), (2, 0, 1))
    return bias, in_band

def banded_attention(q, k, v, bias, in_band, sink=None):
    n, length, hq, dh = q.shape
    hkv = k.shape[2]
    g = hq // hkv
    nb = -(-length // BLOCK)
    padw = ((0, 0), (0, nb * BLOCK - length), (0, 0), (0, 0))
    qb = jnp.pad(q, padw).reshape(n, nb, BLOCK, hkv, g, dh)
    kb = jnp.pad(k, padw).reshape(n, nb, BLOCK, hkv, dh)
    vb = jnp.pad(v, padw).reshape(n, nb, BLOCK, hkv, dh)

    def with_prev(t):
        prev = jnp.pad(t, ((0, 0), (1, 0), (0, 0), (0, 0), (0, 0)))[:, :-1]
        return jnp.concatenate([prev, t], axis=2)

    kk, vv = with_prev(kb), with_prev(vb)
    s = jnp.einsum('nbqhgd,nbkhd->nbhgqk', qb, kk).astype(jnp.float32) * (dh ** -0.5)
    s = s + bias.reshape(hkv, g, BLOCK, 2 * BLOCK)
    kpos = (jnp.arange(nb)[:, None] - 1) * BLOCK + jnp.arange(2 * BLOCK)[None, :]
    mask = in_band[None] & (kpos >= 0)[:, None, :]
    s = jnp.where(mask[None, :, None, None], s, -jnp.inf)
    m = jnp.max(s, axis=-1, keepdims=True)
    if sink is not None:
        sk = sink.astype(jnp.float32).reshape(1, 1, hkv, g, 1, 1)
        m = jnp.maximum(m, sk)
    p = jnp.exp(s - m)
    denom = jnp.sum(p, axis=-1, keepdims=True)
    if sink is not None:
        denom = denom + jnp.exp(sk - m)
    o = jnp.einsum('nbhgqk,nbkhd->nbqhgd', (p / denom).astype(v.dtype), vv)
    o = o.reshape(n, nb * BLOCK, hq, dh)[:, :length]
    lse = (m + jnp.log(denom))[..., 0]
    lse = jnp.transpose(lse, (0, 1, 4, 2, 3)).reshape(n, nb * BLOCK, hq)[:, :length]
    return o, lse

def to_strided(t, d):
    b, s = t.shape[:2]
    sp = -(-s // d) * d
    t = jnp.pad(t, ((0, 0), (0, sp - s)) + ((0, 0),) * (t.ndim - 2))
    t = jnp.moveaxis(t.reshape((b, sp // d, d) + t.shape[2:]), 2, 1)
    return t.reshape((b * d, sp // d) + t.shape[3:])

def from_strided(t, b, s, d):
    length = t.shape[1]
    t = jnp.moveaxis(t.reshape((b, d, length) + t.shape[2:]), 1, 2)
    return t.reshape((b, length * d) + t.shape[3:])[:, :s]

def swa_dilated_layer(h, w_in, sinks, w_out, rel_bias):
    b, s, _ = h.shape
    splits = list(np.cumsum([A_WIDTH, A_KV_WIDTH, A_KV_WIDTH, B_WIDTH, B_WIDTH, B_WIDTH]))
    qa, ka, va, qb, kb, vb, z = jnp.split(h @ w_in, splits, axis=-1)
    qa = qa.reshape(b, s, A_HEADS, HEAD_DIM_2)
    ka = ka.reshape(b, s, A_KV_HEADS, HEAD_DIM_2)
    va = va.reshape(b, s, A_KV_HEADS, HEAD_DIM_2)
    qb, kb, vb = (t.reshape(b, s, B_HEADS, HEAD_DIM_2) for t in (qb, kb, vb))

    bias_a, band_a = band_bias(rel_bias[:, :A_HEADS], 1, A_WINDOW)
    oa, _ = banded_attention(qa, ka, va, bias_a, band_a, sinks)

    outs, lses = [], []
    for window, dil in B_CONFIGS:
        bias_b, band_b = band_bias(rel_bias[:, A_HEADS:], dil, window // dil)
        o, lse = banded_attention(to_strided(qb, dil), to_strided(kb, dil),
                                  to_strided(vb, dil), bias_b, band_b)
        outs.append(from_strided(o, b, s, dil))
        lses.append(from_strided(lse, b, s, dil))
    wts = jax.nn.softmax(jnp.stack(lses), axis=0)
    ob = jnp.sum(wts[..., None] * jnp.stack(outs).astype(jnp.float32), axis=0).astype(h.dtype)

    o = jnp.concatenate([oa.reshape(b, s, A_WIDTH), ob.reshape(b, s, B_WIDTH)], axis=-1)
    return (o * jax.nn.silu(z)) @ w_out

def rope(t, cos, sin):
    half = t.shape[-1] // 2
    t1, t2 = t[..., :half], t[..., half:]
    return jnp.concatenate([t1 * cos - t2 * sin, t1 * sin + t2 * cos], axis=-1).astype(t.dtype)

def mla_layer(h, positions, w_in, q_norm, w_qb, kv_norm, w_kvb, w_out):
    b, s, _ = h.shape
    splits = list(np.cumsum([C_Q_RANK, C_KV_RANK, C_ROPE]))
    c_q, c_kv, k_pe, z = jnp.split(h @ w_in, splits, axis=-1)
    q = (rmsnorm_2(c_q, q_norm) @ w_qb).reshape(b, s, C_HEADS, C_NOPE + C_ROPE)
    q_nope, q_pe = q[..., :C_NOPE], q[..., C_NOPE:]
    kv = (rmsnorm_2(c_kv, kv_norm) @ w_kvb).reshape(b, s, C_HEADS, C_NOPE + C_V)
    k_nope, v = kv[..., :C_NOPE], kv[..., C_NOPE:]

    inv_freq = ROPE_THETA ** (-jnp.arange(0, C_ROPE, 2, dtype=jnp.float32) / C_ROPE)
    ang = positions.astype(jnp.float32)[..., None] * inv_freq
    cos, sin = jnp.cos(ang)[:, :, None], jnp.sin(ang)[:, :, None]
    q_pe = rope(q_pe, cos, sin)
    k_pe = rope(k_pe[:, :, None], cos, sin)[:, :, 0]

    scale = (C_NOPE + C_ROPE) ** -0.5
    nb = s // BLOCK
    kpos = jnp.arange(s)

    def to_blocks(t):
        return jnp.moveaxis(t.reshape((b, nb, BLOCK) + t.shape[2:]), 1, 0)

    def attend_block(args):
        qn, qp, blk = args
        sc = (jnp.einsum('bqhd,bkhd->bhqk', qn, k_nope)
              + jnp.einsum('bqhr,bkr->bhqk', qp, k_pe)).astype(jnp.float32) * scale
        qpos = blk * BLOCK + jnp.arange(BLOCK)
        sc = jnp.where(kpos[None, :] <= qpos[:, None], sc, -jnp.inf)
        p = jax.nn.softmax(sc, axis=-1).astype(v.dtype)
        return jnp.einsum('bhqk,bkhd->bqhd', p, v)

    o = lax.map(attend_block, (to_blocks(q_nope), to_blocks(q_pe), jnp.arange(nb)))
    o = jnp.moveaxis(o, 0, 1).reshape(b, s, C_WIDTH)
    return (o * jax.nn.silu(z)) @ w_out

def second_inputs(seed: int = 0) -> dict:
    key = jax.random.key(seed)
    ks = jax.random.split(key, 16)
    f32 = jnp.float32

    def dense(k, shape):
        return jax.random.normal(k, shape, f32) * shape[-2] ** -0.5

    def gain(k, shape):
        return 1.0 + 0.02 * jax.random.normal(k, shape, f32)

    return {
        "x": jax.random.normal(ks[0], (BATCH, SEQ, D_MODEL), f32),
        "positions": jnp.tile(jnp.arange(SEQ, dtype=jnp.int32)[None, :], (BATCH, 1)),
        "norm_w": gain(ks[1], (DEPTH_2, D_MODEL)),
        "rel_bias": 0.5 * jax.random.normal(ks[2], (NUM_BUCKETS, A_HEADS + B_HEADS), f32),
        "ab_w_in": dense(ks[3], (N_AB, D_MODEL, AB_IN)),
        "ab_sinks": jax.random.normal(ks[4], (N_AB, A_HEADS), f32),
        "ab_w_out": dense(ks[5], (N_AB, AB_WIDTH, D_MODEL)),
        "c_w_in": dense(ks[6], (N_C, D_MODEL, C_IN)),
        "c_q_norm": gain(ks[7], (N_C, C_Q_RANK)),
        "c_w_qb": dense(ks[8], (N_C, C_Q_RANK, C_HEADS * (C_NOPE + C_ROPE))),
        "c_kv_norm": gain(ks[9], (N_C, C_KV_RANK)),
        "c_w_kvb": dense(ks[10], (N_C, C_KV_RANK, C_HEADS * (C_NOPE + C_V))),
        "c_w_out": dense(ks[11], (N_C, C_WIDTH, D_MODEL)),
        "final_norm": gain(ks[12], (D_MODEL,)),
    }

def second_block(x, positions, norm_w, rel_bias, ab_w_in, ab_sinks, ab_w_out,
              c_w_in, c_q_norm, c_w_qb, c_kv_norm, c_w_kvb, c_w_out, final_norm):
    for layer in range(DEPTH_2):
        h = rmsnorm_2(x, norm_w[layer])
        i = layer // 2
        if layer % 2 == 0:
            y = swa_dilated_layer(h, ab_w_in[i], ab_sinks[i], ab_w_out[i], rel_bias)
        else:
            y = mla_layer(h, positions, c_w_in[i], c_q_norm[i], c_w_qb[i],
                          c_kv_norm[i], c_w_kvb[i], c_w_out[i])
        x = x + y
    return rmsnorm_2(x, final_norm)


def setup_inputs(seed=0):
    out = dict(first_inputs(seed))
    for name, value in second_inputs(seed + 1).items():
        if name != "x":
            out[name + "_2"] = value
    return out


def reference(
    x, g_mix, w_in, b_if, conv_q, conv_k, g_head, w_pool, pool_scale, w_br_a, w_br_b, w_out,
    g_ffn, w_rg, b_rg, w_re, b_re, w_e_gate, w_e_up, w_e_down, g_final, positions_2, norm_w_2,
    rel_bias_2, ab_w_in_2, ab_sinks_2, ab_w_out_2, c_w_in_2, c_q_norm_2, c_w_qb_2, c_kv_norm_2,
    c_w_kvb_2, c_w_out_2, final_norm_2,
):
    x = first_block(
        x, g_mix, w_in, b_if, conv_q, conv_k, g_head, w_pool, pool_scale, w_br_a, w_br_b, w_out,
        g_ffn, w_rg, b_rg, w_re, b_re, w_e_gate, w_e_up, w_e_down, g_final,
    )
    return second_block(
        x, positions_2, norm_w_2, rel_bias_2, ab_w_in_2, ab_sinks_2, ab_w_out_2, c_w_in_2,
        c_q_norm_2, c_w_qb_2, c_kv_norm_2, c_w_kvb_2, c_w_out_2, final_norm_2,
    )


_drawn_inputs = setup_inputs


def setup_inputs(seed=0):
    import zlib

    import numpy as np

    out = dict(_drawn_inputs(seed))
    spreads = {}
    factors = {'b_rg': 8.0,
     'b_re': 6.155,
     'norm_w_2': 8.0,
     'ab_sinks_2': 64.0,
     'c_q_norm_2': 8.0,
     'c_kv_norm_2': 8.0,
     'final_norm_2': 8.018}
    for name, (base, spread) in spreads.items():
        noise = np.random.default_rng([zlib.crc32(name.encode()), seed]).standard_normal(out[name].shape)
        drawn = base * np.exp(spread * noise) if base else spread * noise
        out[name] = __import__('jax').numpy.asarray(drawn.astype(out[name].dtype))
    for name, factor in factors.items():
        out[name] = (out[name] * factor).astype(out[name].dtype)
    return out
```

```python
import math
from contextlib import ExitStack

import numpy as np

import concourse.bass as bass
from concourse import mybir

ALU = mybir.AluOpType
ACT = mybir.ActivationFunctionType
AX = mybir.AxisListType
F32 = mybir.dt.float32
F32R = mybir.dt.float32r
I32 = mybir.dt.int32

P = 128
S = 1024
D = 1024
NT = S // P
KT = D // P
HALF = 512
NH = S // HALF
EPS = 1e-6

D_POOL = D // 2
D_ML = D // 2
HEADS = 4
DH = D_ML // HEADS
POOL_WINDOWS = (2, 4, 8, 16)
PAD = max(POOL_WINDOWS)
CONV_K = 4
COL_POOL = 0
COL_Q = D_POOL
COL_K = COL_Q + D_ML
COL_V = COL_K + D_ML
COL_O = COL_V + D_ML
COL_I = COL_O + D_ML
COL_GA = COL_I + 2 * HEADS
COL_GB = COL_GA + D
NC = S // P
NEG = -1.0e30

GROUPS = 4
PER_GROUP = 8
EXPERTS = GROUPS * PER_GROUP
TOP_K = 2
D_EXP = D // 2
FT = D_EXP // P
BLOCKS = S * TOP_K // P + EXPERTS
SLOTS_B = BLOCKS + 1

HD = 64
A_HEADS, A_KV, B_HEADS = 8, 2, 8
A_WIDTH, A_KVW, B_WIDTH = A_HEADS * HD, A_KV * HD, B_HEADS * HD
COL_QA, COL_KA = 0, A_WIDTH
COL_VA = COL_KA + A_KVW
COL_QB = COL_VA + A_KVW
COL_KB, COL_VB = COL_QB + B_WIDTH, COL_QB + 2 * B_WIDTH
COL_Z = COL_QB + 3 * B_WIDTH
DILATIONS = (1, 4, 16)
BUCKETS, MAX_DISTANCE = 32, 2048
BAND = 384
SC_AB = HD ** -0.5

C_HEADS, C_QR, C_KVR, C_NOPE, C_ROPE, C_V = 16, 256, 128, 64, 32, 64
C_LAT = C_QR + C_KVR + C_ROPE
C_QK = C_NOPE + C_ROPE
C_SCALE = C_QK ** -0.5
QR_T = C_QR // P
ROPE_HALF = C_ROPE // 2
ROPE_THETA = 10000.0
TWO_PI = 2.0 * math.pi
TWO_PI_1 = 6.28125
TWO_PI_2 = float(np.float32(round((TWO_PI - TWO_PI_1) * 2 ** 21)) / np.float32(2 ** 21))
TWO_PI_3 = TWO_PI - TWO_PI_1 - TWO_PI_2
ROUND = 1.5 * 2 ** 23
PI_BELOW = 3.1415925


def inverse_frequencies():
    return np.power(np.float32(ROPE_THETA), -np.arange(0, C_ROPE, 2, dtype=np.float32) / np.float32(C_ROPE))


def window_reciprocals():
    t = np.arange(PAD)
    return np.stack([1.0 / np.minimum(t + 1, w) for w in POOL_WINDOWS]).astype(np.float32)


def bucket_onehot():
    dist = 255 - np.arange(BAND)
    inside = (dist >= 0) & (dist <= P)
    out = np.zeros((BUCKETS + 1, len(DILATIONS), BAND), np.float32)
    exact = BUCKETS // 2
    for c, dilation in enumerate(DILATIONS):
        d = np.maximum(dist, 0) * dilation
        far = np.maximum(d, 1).astype(np.float32) / np.float32(exact)
        large = exact + (np.log(far) / np.float32(math.log(MAX_DISTANCE / exact)) * np.float32(BUCKETS - exact)).astype(np.int32)
        bucket = np.where(d < exact, d, np.minimum(large, BUCKETS - 1))
        for x in range(BAND):
            out[bucket[x] if inside[x] else BUCKETS, c, x] = 1.0
    return out


class Scope:

    def __init__(self, nc, ctx, tag):
        self.nc, self.ctx, self.tag, self.sems = nc, ctx, tag, []
        ctx.callback(self.clear)

    def clear(self):
        self.nc.clear_and_free_semaphores(self.sems)
        self.nc.all_engine_barrier()

    def sb(self, name, shape, dt=F32):
        return self.ctx.enter_context(self.nc.sbuf_tensor(f"{self.tag}_{name}", shape, dt))

    def sem(self, name):
        self.sems.append(self.nc.alloc_semaphore(f"{self.tag}_{name}"))
        return self.sems[-1]


class Chain:

    def __init__(self, engine, sem):
        self.engine, self.sem, self.n = engine, sem, 0

    def __call__(self, instruction):
        self.n += 1
        instruction.then_inc(self.sem, 1)
        self.engine.wait_ge(self.sem, self.n)


def multiply_split(pe, out, a, b, start, stop):
    pe.matmul(out, a[0], b[0], start=start, stop=False)
    pe.matmul(out, a[0], b[1], start=False, stop=False)
    return pe.matmul(out, a[1], b[0], start=False, stop=stop)


def low_part(dve, low, x, high):
    return dve.tensor_tensor(low, x, high.bitcast(F32), ALU.subtract)


def tiled_rows(ap):
    return ap.rearrange("(k p) n -> p k n", p=P)


def make_constants(nc, K, dram):
    with ExitStack() as ctx:
        sc = Scope(nc, ctx, "const")
        filled, made = sc.sem("filled"), sc.sem("made")
        with nc.Block() as block:
            @block.gpsimd
            def _(pool):
                pool.memset(K["ident"][:, :], 0.0).then_inc(filled, 1)
                pool.memset(K["ones"][:, :], 1.0).then_inc(filled, 1)
                pool.memset(K["neg_after"][:, :], 0.0).then_inc(filled, 1)
                pool.memset(K["neg_before"][:, :], 0.0).then_inc(filled, 1)
                pool.memset(K["sel_neg"][:, :, :], 0.0).then_inc(filled, 1)
                pool.memset(K["sel_one"][:, :, :], 0.0).then_inc(filled, 1)
                pool.memset(K["earlier"][:, :], 1.0).then_inc(filled, 1)
                pool.wait_ge(filled, 7)
                pool.affine_select(out=K["ident"][:, :], in_=K["ident"][:, :], compare_op=ALU.not_equal, fill=1.0,
                                   base=0, pattern=[[-1, P]], channel_multiplier=1).then_inc(made, 1)
                pool.affine_select(out=K["neg_after"][:, :], in_=K["neg_after"][:, :], compare_op=ALU.is_ge, fill=NEG,
                                   base=0, pattern=[[-1, P]], channel_multiplier=1).then_inc(made, 1)
                pool.affine_select(out=K["neg_before"][:, :], in_=K["neg_before"][:, :], compare_op=ALU.is_ge,
                                   fill=NEG, base=0, pattern=[[1, P]], channel_multiplier=-1).then_inc(made, 1)
                pool.affine_select(out=K["earlier"][:, :], in_=K["earlier"][:, :], compare_op=ALU.is_gt, fill=0.0,
                                   base=0, pattern=[[1, P]], channel_multiplier=-1).then_inc(made, 1)
                pool.affine_select(out=K["sel_neg"][:, :, :], in_=K["sel_neg"][:, :, :], compare_op=ALU.not_equal,
                                   fill=-1.0, base=0, pattern=[[-1, HEADS], [0, P]], channel_multiplier=1).then_inc(made, 1)
                pool.affine_select(out=K["sel_one"][:, :, :], in_=K["sel_one"][:, :, :], compare_op=ALU.not_equal,
                                   fill=1.0, base=0, pattern=[[-1, HEADS], [0, P]], channel_multiplier=1).then_inc(made, 1)
                pool.wait_ge(made, 6)


def load_x(nc, K, x):
    with ExitStack() as ctx:
        sc = Scope(nc, ctx, "load")
        loaded = sc.sem("loaded")
        with nc.Block() as block:
            @block.sync
            def _(sp):
                for t in range(0, NT, 2):
                    sp.dma_start(K["X"][:, t, :], x[t * P:(t + 1) * P, :]).then_inc(loaded, 16)

            @block.scalar
            def _(act):
                for t in range(1, NT, 2):
                    act.dma_start(K["X"][:, t, :], x[t * P:(t + 1) * P, :]).then_inc(loaded, 16)
                act.wait_ge(loaded, 16 * NT)


def norm_transpose(nc, K, g, tag, h_dram=None):
    by_row = h_dram is not None
    X, hT, ps, ident = K["X"], K["hT"], K["ps"], K["ident"]
    with ExitStack() as ctx:
        sc = Scope(nc, ctx, tag)
        gcol = sc.sb("gcol", [P, KT])
        squares = sc.sb("squares", [P, 2, D])
        ss = sc.sb("ss", [P, NT])
        var = sc.sb("var", [P, NT])
        std = sc.sb("std", [P, NT])
        rs = sc.sb("rs", [P, NT])
        h = sc.sb("h", [P, NT, D])
        grow = sc.sb("grow", [P, D])
        stored = sc.sem("stored")
        g_loaded, summed, var_ready, std_ready = sc.sem("g_loaded"), sc.sem("summed"), sc.sem("var_ready"), sc.sem("std_ready")
        h_ready, turned, out_act, out_dve = sc.sem("h_ready"), sc.sem("turned"), sc.sem("out_act"), sc.sem("out_dve")
        chain = sc.sem("chain")
        units = [(half, k) for half in range(NH) for k in range(KT)]
        with nc.Block() as block:
            @block.sync
            def _(sp):
                if by_row:
                    sp.dma_start(grow[:, :], g.partition_broadcast(P)).then_inc(g_loaded, 16)
                    for t in range(NT):
                        sp.wait_ge(h_ready, t + 1)
                        sp.dma_start(h_dram[t * P:(t + 1) * P, :], h[:, t, :]).then_inc(stored, 16)
                    sp.wait_ge(stored, 16 * NT)
                else:
                    sp.dma_start(gcol[:, :], g.rearrange("(k p) -> p k", p=P)).then_inc(g_loaded, 16)

            @block.scalar
            def _(act):
                for t in range(NT):
                    if t >= 2:
                        act.wait_ge(summed, t - 1)
                    act.activation(squares[:, t % 2, :], X[:, t, :], ACT.Square, accum_out=ss[:, t:t + 1]).then_inc(summed, 1)
                act.wait_ge(var_ready, 1)
                act.activation(std[:, :], var[:, :], ACT.Sqrt).then_inc(std_ready, 1)
                act.wait_ge(g_loaded, 16)
                for u, (half, k) in enumerate(units):
                    if u % 2 == 0:
                        act.wait_ge(turned, u + 1)
                        act.activation(hT[:, k, half * HALF:(half + 1) * HALF], ps[:, u % 8, :], ACT.Copy,
                                       scale=1.0 if by_row else gcol[:, k:k + 1]).then_inc(out_act, 1)

            @block.vector
            def _(dve):
                link = Chain(dve, chain)
                dve.wait_ge(summed, NT)
                dve.tensor_scalar(var[:, :], ss[:, :], 1.0 / D, EPS, ALU.mult, ALU.add).then_inc(var_ready, 1)
                dve.wait_ge(std_ready, 1)
                link(dve.reciprocal(rs[:, :], std[:, :]))
                dve.wait_ge(g_loaded, 16)
                for t in range(NT):
                    if by_row:
                        dve.scalar_tensor_tensor(out=h[:, t, :], in0=X[:, t, :], scalar=rs[:, t:t + 1], in1=grow[:, :],
                                                 op0=ALU.mult, op1=ALU.mult).then_inc(h_ready, 1)
                    else:
                        dve.tensor_scalar(h[:, t, :], X[:, t, :], rs[:, t:t + 1], None, ALU.mult).then_inc(h_ready, 1)
                for u, (half, k) in enumerate(units):
                    if u % 2 == 1:
                        dve.wait_ge(turned, u + 1)
                        dve.tensor_scalar(hT[:, k, half * HALF:(half + 1) * HALF], ps[:, u % 8, :],
                                          1.0 if by_row else gcol[:, k:k + 1], None, ALU.mult).then_inc(out_dve, 1)

            @block.tensor
            def _(pe):
                for u, (half, k) in enumerate(units):
                    pe.wait_ge(h_ready, (half + 1) * NT // NH)
                    if u >= 8:
                        pe.wait_ge(out_act if u % 2 == 0 else out_dve, (u - 8) // 2 + 1)
                    for j in range(4):
                        mm = pe.transpose(ps[:, u % 8, j * P:(j + 1) * P], h[:, half * 4 + j, k * P:(k + 1) * P], ident[:, :])
                    mm.then_inc(turned, 1)


def mixer_projections(nc, K, M, w_in, b_if, conv_q, conv_k, w_pool, pool_scale, invcnt):
    hT, ps = K["hT"], K["ps"]
    SLOTS = 6
    with ExitStack() as ctx:
        sc = Scope(nc, ctx, "proj")
        w = K["X"][:, 0:SLOTS, :].rearrange("p s (k n) -> p s k n", n=P)
        wif = sc.sb("wif", [P, KT, 2 * HEADS])
        raw = sc.sb("raw", [P, 2, PAD + S])
        acc = sc.sb("acc", [P, 2, PAD + S])
        cw = sc.sb("cw", [P, 2, HEADS, CONV_K])
        wp = sc.sb("wp", [P, 4, P])
        pscale = sc.sb("pscale", [P, 4])
        icnt = sc.sb("icnt", [P, 4, PAD])
        bi = sc.sb("bi", [HEADS, 2])
        ig, fg, e1, e2 = [M["yT"][0:HEADS, i, :].rearrange("p (c t) -> p c t", t=P) for i in range(4)]
        bb = M["og"][0:HEADS, 0:2, :].rearrange("p a (c t) -> p a c t", t=P)
        cm = M["og"][0:HEADS, 2:4, :].rearrange("p a (c t) -> p a c t", t=P)
        small = sc.sb("small", [HEADS, 4, NC])
        loaded = [sc.sem(f"w{i}") for i in range(SLOTS)]
        consts, evac, made, slot_free = sc.sem("consts"), sc.sem("evac"), sc.sem("made"), sc.sem("slot_free")
        conv_done, silu_done, pool_done, chain = sc.sem("conv_done"), sc.sem("silu_done"), sc.sem("pool_done"), sc.sem("chain")
        gate_dve, gate_act, rows = sc.sem("gate_dve"), sc.sem("gate_act"), sc.sem("rows")
        achain = sc.sem("achain")
        tiles = []
        for h in range(HEADS):
            tiles += [("q", h, COL_Q + h * P), ("k", h, COL_K + h * P)]
        tiles += [("v", j, COL_V + j * P) for j in range(4)]
        tiles += [("p", g, COL_POOL + g * P) for g in range(4)]
        tiles += [("o", h, COL_O + h * P) for h in range(HEADS)]
        V0 = 8
        UQ = 4
        UV = UQ + 2 * V0
        UP = UV + NT
        UO = UP + 8
        UY = UO + 8
        consts_n = 16 * 15

        with nc.Block() as block:
            @block.sync
            def _(sp):
                sp.dma_start(wif[:, :, :], tiled_rows(w_in[:, COL_I:COL_I + 2 * HEADS])).then_inc(consts, 16)
                for n, (kind, j, col) in enumerate(tiles):
                    if n >= SLOTS:
                        sp.wait_ge(slot_free, n - SLOTS + 1)
                    sp.dma_start(w[:, n % SLOTS, :, :], tiled_rows(w_in[:, col:col + P])).then_inc(loaded[n % SLOTS], 16)

            @block.tensor
            def _(pe):
                pe.wait_ge(consts, consts_n)
                u = 0
                for part in range(2):
                    for half in range(NH):
                        for k in range(KT):
                            mm = pe.matmul(ps[0:HEADS, u % 8, :], wif[:, k, part * HEADS:(part + 1) * HEADS],
                                           hT[:, k, half * HALF:(half + 1) * HALF], start=(k == 0), stop=(k == KT - 1))
                        mm.then_inc(made, 1)
                        u += 1
                for n, (kind, j, col) in enumerate(tiles):
                    if kind == "v":
                        if j < 3:
                            continue
                        for i in range(4):
                            pe.wait_ge(loaded[(V0 + i) % SLOTS], 16 * ((V0 + i) // SLOTS + 1))
                        s0 = V0 % SLOTS
                        for t in range(NT):
                            pe.wait_ge(evac, u - 7)
                            for k in range(KT):
                                mm = pe.matmul(ps[:, u % 8, :], hT[:, k, t * P:(t + 1) * P], w[:, s0:s0 + 4, k, :],
                                               start=(k == 0), stop=(k == KT - 1))
                            mm.then_inc(made, 1)
                            u += 1
                        pe.wait_ge(made, u)
                        pe.sem_inc(slot_free, 4)
                        continue
                    pe.wait_ge(loaded[n % SLOTS], 16 * (n // SLOTS + 1))
                    for half in range(NH):
                        if u >= 8:
                            pe.wait_ge(evac, u - 7)
                        for k in range(KT):
                            mm = pe.matmul(ps[:, u % 8, :], w[:, n % SLOTS, k, :], hT[:, k, half * HALF:(half + 1) * HALF],
                                           start=(k == 0), stop=(k == KT - 1))
                        mm.then_inc(made, 1)
                        u += 1
                    pe.wait_ge(made, u)
                    pe.sem_inc(slot_free, 1)
                assert u == UY
                for g in range(4):
                    pe.wait_ge(pool_done, g + 1)
                    for half in range(NH):
                        pe.wait_ge(evac, u - 7)
                        pe.matmul(ps[:, u % 8, :], wp[:, g, :], M["dT"][:, g, half * HALF:(half + 1) * HALF],
                                  start=True, stop=True).then_inc(made, 1)
                        u += 1
                pe.wait_ge(rows, 1)
                pe.wait_ge(evac, u)
                for c in range(NC):
                    mm = pe.transpose(ps[:, c // 4, (c % 4) * P:(c % 4 + 1) * P], M["R"][:, c * P:(c + 1) * P], K["ident"][:, :])
                for h in range(HEADS):
                    mm = pe.matmul(ps[:, 2, h * NC:(h + 1) * NC], K["sel_one"][:, h, :], small[:, 3, :], start=True, stop=True,
                                   skip_group_check=True)
                mm.then_inc(made, 1)

            @block.scalar
            def _(act):
                for which, taps in enumerate((conv_q, conv_k)):
                    for h in range(HEADS):
                        act.dma_start(cw[:, which, h, :], taps[:, h * DH:(h + 1) * DH].rearrange("j p -> p j")).then_inc(consts, 16)
                act.dma_start(wp[:, :, :], w_pool.rearrange("g c d -> c g d")).then_inc(consts, 16)
                act.dma_start(pscale[:, :], pool_scale.rearrange("(g p) -> p g", p=P)).then_inc(consts, 16)
                act.dma_start(icnt[:, :, :], invcnt.partition_broadcast(P)).then_inc(consts, 16)
                act.dma_start(bi[:, 0:1], b_if[0:HEADS].rearrange("(h a) -> h a", a=1)).then_inc(consts, 16)
                act.dma_start(bi[:, 1:2], b_if[HEADS:2 * HEADS].rearrange("(h a) -> h a", a=1)).then_inc(consts, 16)
                act.dma_start(M["ghead"][:, :], M["g_head_dram"].rearrange("(h p) -> p h", p=P)).then_inc(consts, 16)
                act.wait_ge(consts, consts_n)
                for u in range(4):
                    half = u % 2
                    dst = (ig, fg)[u // 2]
                    act.wait_ge(made, u + 1)
                    act.activation(dst[:, half * 4:half * 4 + 4, :], ps[0:HEADS, u % 8, :].rearrange("p (c t) -> p c t", t=P),
                                   ACT.Identity, bias=bi[:, u // 2:u // 2 + 1]).then_inc(evac, 1)
                link = Chain(act, achain)
                act.wait_ge(gate_dve, 1)
                link(act.activation(e1[:, :, :], e1[:, :, :], ACT.Exp, scale=-1.0))
                act.activation(e1[:, :, :], e1[:, :, :], ACT.Ln, bias=1.0).then_inc(gate_act, 1)
                for n in range(V0):
                    for half in range(NH):
                        u = UQ + 2 * n + half
                        act.wait_ge(made, u + 1)
                        if n >= 2:
                            act.wait_ge(conv_done, n - 1)
                        act.activation(raw[:, n % 2, PAD + half * HALF:PAD + (half + 1) * HALF], ps[:, u % 8, :],
                                       ACT.Copy).then_inc(evac, 1)
                    if n == 0:
                        act.wait_ge(gate_dve, 2)
                        act.activation(M["R"][32:32 + HEADS, :], e1[:, :, :].rearrange("p c t -> p (c t)"), ACT.Exp, scale=-1.0).then_inc(gate_act, 1)
                        act.activation(M["R"][64:64 + HEADS, :], e2[:, :, :].rearrange("p c t -> p (c t)"), ACT.Exp).then_inc(gate_act, 1)
                        act.activation(M["R"][96:96 + HEADS, :], fg[:, :, :].rearrange("p c t -> p (c t)"), ACT.Exp).then_inc(gate_act, 1)
                        act.activation(small[:, 3, :], small[:, 2, :], ACT.Exp).then_inc(gate_act, 1)
                        act.wait_ge(gate_act, 5)
                        act.sem_inc(rows, 1)
                    if n >= 1:
                        act.wait_ge(conv_done, n)
                        m = n - 1
                        dst = M["qT"] if m % 2 == 0 else M["kT"]
                        act.activation(dst[:, m // 2, :], acc[:, m % 2, 0:S], ACT.Silu).then_inc(silu_done, 1)
                act.wait_ge(conv_done, V0)
                act.activation(M["kT"][:, HEADS - 1, :], acc[:, 1, 0:S], ACT.Silu).then_inc(silu_done, 1)
                for t in range(NT):
                    u = UV + t
                    act.wait_ge(made, u + 1)
                    act.activation(M["v"][:, t, :, 0:DH], ps[:, u % 8, :].rearrange("p (h e) -> p h e", e=DH), ACT.Copy).then_inc(evac, 1)
                for g in range(4):
                    for half in range(NH):
                        u = UP + 2 * g + half
                        act.wait_ge(made, u + 1)
                        if g >= 2:
                            act.wait_ge(pool_done, g - 1)
                        act.activation(raw[:, g % 2, PAD + half * HALF:PAD + (half + 1) * HALF], ps[:, u % 8, :],
                                       ACT.Copy).then_inc(evac, 1)
                for h in range(HEADS):
                    for half in range(NH):
                        u = UO + 2 * h + half
                        act.wait_ge(made, u + 1)
                        act.activation(M["og"][:, h, half * HALF:(half + 1) * HALF], ps[:, u % 8, :], ACT.Sigmoid).then_inc(evac, 1)
                for g in range(4):
                    for half in range(NH):
                        u = UY + 2 * g + half
                        act.wait_ge(made, u + 1)
                        act.activation(M["yT"][:, g, half * HALF:(half + 1) * HALF], ps[:, u % 8, :], ACT.Copy,
                                       scale=pscale[:, g:g + 1]).then_inc(evac, 1)
                act.wait_ge(made, UY + 9)
                for j in range(2):
                    act.activation(M["RT"][:, 4 * j:4 * j + 4, :], ps[:, j, :].rearrange("p (c r) -> p c r", r=P), ACT.Copy).then_inc(achain, 1)
                act.activation(M["SP"][:, :, :], ps[:, 2, 0:HEADS * NC].rearrange("p (h c) -> p h c", c=NC), ACT.Copy).then_inc(achain, 1)

            @block.vector
            def _(dve):
                link = Chain(dve, chain)
                dve.memset(raw[:, 0, 0:PAD], 0.0).then_inc(chain, 1)
                dve.memset(raw[:, 1, 0:PAD], 0.0).then_inc(chain, 1)
                dve.memset(acc[:, 0, 0:PAD], 0.0).then_inc(chain, 1)
                dve.memset(acc[:, 1, 0:PAD], 0.0).then_inc(chain, 1)
                dve.memset(M["v"][:, :, :, DH:DH + 1], 1.0).then_inc(chain, 1)
                link.n = 5
                link(dve.memset(M["R"][:, :], 0.0))
                dve.wait_ge(evac, 4)
                link(dve.scalar_tensor_tensor(out=e1[:, :, :], in0=fg[:, :, :], scalar=-1.0, in1=fg[:, :, :], op0=ALU.mult, op1=ALU.max))
                dve.tensor_scalar(e2[:, :, :], fg[:, :, :], 0.0, None, ALU.min).then_inc(gate_dve, 1)
                dve.wait_ge(gate_act, 1)
                dve.wait_ge(gate_dve, 1)
                link(dve.tensor_tensor(bb[:, 0, :, :], e2[:, :, :], e1[:, :, :], ALU.subtract))
                cur = 0
                for step in (1, 2, 4, 8, 16, 32, 64):
                    link(dve.tensor_copy(bb[:, 1 - cur, :, 0:step], bb[:, cur, :, 0:step]))
                    link(dve.tensor_tensor(bb[:, 1 - cur, :, step:], bb[:, cur, :, step:], bb[:, cur, :, 0:P - step], ALU.add))
                    cur = 1 - cur
                b = bb[:, cur, :, :]
                U = M["U"]
                link(dve.tensor_tensor(U[:, :, :], ig[:, :, :], b, ALU.subtract))
                link(dve.tensor_copy(cm[:, 0, :, :], U[:, :, :]))
                cur = 0
                for step in (1, 2, 4, 8, 16, 32, 64):
                    link(dve.tensor_copy(cm[:, 1 - cur, :, 0:step], cm[:, cur, :, 0:step]))
                    link(dve.tensor_tensor(cm[:, 1 - cur, :, step:], cm[:, cur, :, step:], cm[:, cur, :, 0:P - step], ALU.max))
                    cur = 1 - cur
                cmx = cm[:, cur, :, :]
                prev = small[:, 0, :]
                link(dve.memset(small[:, :, :], 0.0))
                for c in range(NC - 1):
                    link(dve.scalar_tensor_tensor(out=small[:, 0, c + 1:c + 2], in0=small[:, 0, c:c + 1], scalar=cmx[:, c, P - 1:P],
                                                  in1=b[:, c, P - 1:P], op0=ALU.max, op1=ALU.add))
                G = M["G"]
                prev_all = small[:, 0, :].rearrange("p (c a) -> p c a", a=1).to_broadcast([HEADS, NC, P])
                link(dve.tensor_tensor(G[:, :, :], cmx, prev_all, ALU.max))
                link(dve.tensor_copy(small[:, 1, :], G[:, :, P - 1:P].rearrange("p c a -> p (c a)")))
                last_all = small[:, 1, :].rearrange("p (c a) -> p c a", a=1).to_broadcast([HEADS, NC, P])
                link(dve.tensor_copy(M["R"][0:HEADS, :], U[:, :, :].rearrange("p c t -> p (c t)")))
                link(dve.tensor_tensor(e1[:, :, :], b, G[:, :, :], ALU.add))
                link(dve.tensor_tensor(e2[:, :, :], prev_all, G[:, :, :], ALU.subtract))
                link(dve.tensor_tensor(fg[:, :, :], U[:, :, :], last_all, ALU.subtract))
                dve.tensor_tensor(small[:, 2, :], small[:, 0, :], small[:, 1, :], ALU.subtract).then_inc(gate_dve, 1)
                dve.wait_ge(consts, consts_n)
                for n in range(V0):
                    kind = n % 2
                    h = n // 2
                    dve.wait_ge(evac, UQ + 2 * n + 2)
                    if n >= 2:
                        dve.wait_ge(silu_done, n - 1)
                    for j in range(CONV_K):
                        src = raw[:, n % 2, PAD - CONV_K + 1 + j:PAD - CONV_K + 1 + j + S]
                        dst = acc[:, n % 2, 0:S]
                        tap = cw[:, kind, h, j:j + 1]
                        if j == 0:
                            link(dve.tensor_scalar(dst, src, tap, None, ALU.mult))
                        elif j < CONV_K - 1:
                            link(dve.scalar_tensor_tensor(out=dst, in0=src, scalar=tap, in1=dst, op0=ALU.mult, op1=ALU.add))
                        else:
                            dve.scalar_tensor_tensor(out=dst, in0=src, scalar=tap, in1=dst, op0=ALU.mult, op1=ALU.add).then_inc(conv_done, 1)
                dve.wait_ge(silu_done, V0)
                link(dve.memset(acc[:, :, 0:PAD], 0.0))
                for g, win in enumerate(POOL_WINDOWS):
                    dve.wait_ge(evac, UP + 2 * g + 2)
                    u_in = raw[:, g % 2, :]
                    cur, width, flip = u_in, 1, 0
                    while width < win:
                        nxt = acc[:, flip, :]
                        link(dve.tensor_tensor(nxt[:, PAD:], cur[:, PAD:], cur[:, PAD - width:PAD + S - width], ALU.add))
                        cur, width, flip = nxt, 2 * width, 1 - flip
                    dT = M["dT"]
                    link(dve.scalar_tensor_tensor(out=dT[:, g, :], in0=cur[:, PAD:], scalar=1.0 / win, in1=u_in[:, PAD:], op0=ALU.mult, op1=ALU.subtract))
                    link(dve.tensor_tensor(icnt[:, g, :], icnt[:, g, :], cur[:, PAD:2 * PAD], ALU.mult))
                    dve.tensor_tensor(dT[:, g, 0:PAD], icnt[:, g, :], u_in[:, PAD:2 * PAD], ALU.subtract).then_inc(pool_done, 1)


def mlstm(nc, K, M):
    ps, ident = K["ps"], K["ident"]
    qT, kT, v, U, G, RT, SP = M["qT"], M["kT"], M["v"], M["U"], M["G"], M["RT"], M["SP"]
    SCALE = DH ** -0.5
    E = DH + 1
    with ExitStack() as ctx:
        sc = Scope(nc, ctx, "ml")
        C = sc.sb("C", [P, HEADS, E])
        ex = sc.sb("ex", [P, HEADS, P])
        pt = sc.sb("pt", [P, HEADS, P])
        kw = sc.sb("kw", [P, HEADS, P])
        inter = sc.sb("inter", [P, HEADS, E])
        num = sc.sb("num", [P, HEADS, E])
        den = sc.sb("den", [P, 2, HEADS])
        stats = sc.sb("stats", [P, HEADS, 6])
        mv = sc.sb("mv", [P, NC, HEADS, 2])
        std, rstd = sc.sb("std", [P, NC, HEADS]), sc.sb("rstd", [P, NC, HEADS])
        hm = sc.sb("hm", [P, NC, HEADS, DH])
        scores, gb, kt_done, e_ready, e_done, p_done, kw_done = [sc.sem(x) for x in
            ("scores", "gb", "kt_done", "e_ready", "e_done", "p_done", "kw_done")]
        inter_done, inter_out, intra_done, state_done, c_new, num_done, chain, achain = [sc.sem(x) for x in
            ("inter_done", "inter_out", "intra_done", "state_done", "c_new", "num_done", "chain", "achain")]
        var_ready, std_ready, hn_ready, turned, out_sem = [sc.sem(x) for x in ("var_ready", "std_ready", "hn_ready", "turned", "out")]

        def pair(bank, j):
            return ps[:, bank, j * E:(j + 1) * E]

        with nc.Block() as block:
            @block.tensor
            def _(pe):
                pe.wait_ge(c_new, 1)
                for c in range(NC):
                    cols = slice(c * P, (c + 1) * P)
                    if c:
                        pe.wait_ge(e_ready, c)
                    for h in range(HEADS):
                        mm = pe.matmul(ps[:, 1, h * P:(h + 1) * P], K["sel_neg"][:, h, :], G[:, c, :], start=True, stop=True, skip_group_check=True)
                    mm.then_inc(gb, 1)
                    if c:
                        pe.wait_ge(p_done, c)
                    for h in range(HEADS):
                        mm = pe.matmul(ps[:, 0, h * P:(h + 1) * P], kT[:, h, cols], qT[:, h, cols], start=True, stop=True, skip_group_check=True)
                    mm.then_inc(scores, 1)
                    if c:
                        pe.wait_ge(c_new, c + 1)
                    for h in range(HEADS):
                        mm = pe.transpose(ps[:, 2, h * P:(h + 1) * P], kT[:, h, cols], ident[:, :])
                    mm.then_inc(kt_done, 1)
                    if c:
                        pe.wait_ge(inter_out, c)
                    for h in range(HEADS):
                        mm = pe.matmul(pair(3 + h // 2, h % 2), qT[:, h, cols], C[:, h, :], start=True, stop=True, skip_group_check=True)
                    mm.then_inc(inter_done, 1)
                    pe.wait_ge(p_done, c + 1)
                    if c:
                        pe.wait_ge(num_done, c)
                    for h in range(HEADS):
                        mm = pe.matmul(pair(5 + h // 2, h % 2), pt[:, h, :], v[:, c, h, :], start=True, stop=True, skip_group_check=True)
                    mm.then_inc(intra_done, 1)
                    pe.wait_ge(kw_done, c + 1)
                    for h in range(HEADS):
                        mm = pe.matmul(pair((7, 2)[h // 2], h % 2), kw[:, h, :], v[:, c, h, :], start=True, stop=True, skip_group_check=True)
                    mm.then_inc(state_done, 1)
                pe.wait_ge(hn_ready, 1)
                for u in range(8):
                    h, half = u // 2, u % 2
                    for j in range(4):
                        mm = pe.transpose(ps[:, u, j * P:(j + 1) * P], hm[:, half * 4 + j, h, :], ident[:, :])
                    mm.then_inc(turned, 1)

            @block.scalar
            def _(act):
                act.wait_ge(c_new, 1)
                for c in range(NC):
                    act.wait_ge(e_ready, c + 1)
                    for h in range(HEADS):
                        i = act.activation(ex[:, h, :], ex[:, h, :], ACT.Exp, bias=RT[:, c, h:h + 1])
                    i.then_inc(e_done, 1)
                    act.wait_ge(kt_done, c + 1)
                    if c:
                        act.wait_ge(state_done, c)
                    for h in range(HEADS):
                        i = act.activation(kw[:, h, :], ps[:, 2, h * P:(h + 1) * P], ACT.Copy, scale=RT[:, c, 96 + h:97 + h])
                    i.then_inc(kw_done, 1)
                    act.wait_ge(inter_done, c + 1)
                    if c:
                        act.wait_ge(num_done, c)
                    for h in range(HEADS):
                        i = act.activation(inter[:, h, :], pair(3 + h // 2, h % 2), ACT.Copy, scale=RT[:, c, 64 + h:65 + h])
                    i.then_inc(inter_out, 1)
                act.wait_ge(var_ready, 1)
                act.activation(std[:, :, :], std[:, :, :], ACT.Sqrt).then_inc(std_ready, 1)
                for u in range(8):
                    h, half = u // 2, u % 2
                    act.wait_ge(turned, u + 1)
                    act.activation(M["hmT"][:, h, half * HALF:(half + 1) * HALF], ps[:, u, :], ACT.Copy, scale=M["ghead"][:, h:h + 1]).then_inc(out_sem, 1)

            @block.vector
            def _(dve):
                link = Chain(dve, chain)
                link(dve.tensor_scalar(RT[:, :, 96:96 + HEADS], RT[:, :, 96:96 + HEADS], SCALE, None, ALU.mult))
                dve.memset(C[:, :, :], 0.0).then_inc(c_new, 1)
                dve.wait_ge(c_new, 1)
                mask = K["neg_before"][:, :].rearrange("p (a t) -> p a t", a=1).to_broadcast([P, HEADS, P])
                for c in range(NC):
                    dve.wait_ge(gb, c + 1)
                    if c:
                        dve.wait_ge(p_done, c)
                    dve.tensor_tensor(ex[:, :, :], ps[:, 1, :].rearrange("p (h t) -> p h t", t=P), mask, ALU.add).then_inc(e_ready, 1)
                    dve.wait_ge(e_done, c + 1)
                    dve.wait_ge(scores, c + 1)
                    if c:
                        dve.wait_ge(intra_done, c)
                    dve.scalar_tensor_tensor(out=pt[:, :, :], in0=ps[:, 0, :].rearrange("p (h t) -> p h t", t=P), scalar=SCALE, in1=ex[:, :, :],
                                             op0=ALU.mult, op1=ALU.mult).then_inc(p_done, 1)
                    dve.wait_ge(inter_out, c + 1)
                    dve.wait_ge(intra_done, c + 1)
                    for j in range(2):
                        i = dve.tensor_tensor(num[:, 2 * j:2 * j + 2, :], ps[:, 5 + j, 0:2 * E].rearrange("p (h e) -> p h e", e=E),
                                              inter[:, 2 * j:2 * j + 2, :], ALU.add)
                        if j == 0:
                            link(i)
                    i.then_inc(num_done, 1)
                    dve.wait_ge(num_done, c + 1)
                    dve.wait_ge(state_done, c + 1)
                    for h in range(HEADS):
                        i = dve.scalar_tensor_tensor(out=C[:, h, :], in0=C[:, h, :], scalar=SP[:, h, c:c + 1],
                                                     in1=pair((7, 2)[h // 2], h % 2), op0=ALU.mult, op1=ALU.add)
                        if h < HEADS - 1:
                            i.then_inc(chain, 1)
                            link.n += 1
                    i.then_inc(c_new, 1)
                    nq = num[:, :, DH:E].rearrange("p h a -> p (h a)")
                    link(dve.scalar_tensor_tensor(out=den[:, 0, :], in0=nq, scalar=-1.0, in1=nq, op0=ALU.mult, op1=ALU.max))
                    link(dve.tensor_tensor(den[:, 0, :], den[:, 0, :], RT[:, c, 32:32 + HEADS], ALU.max))
                    link(dve.reciprocal(den[:, 1, :], den[:, 0, :]))
                    for h in range(HEADS):
                        i = dve.tensor_scalar(hm[:, c, h, :], num[:, h, 0:DH], den[:, 1, h:h + 1], None, ALU.mult)
                        i.then_inc(chain, 1)
                        link.n += 1
                    dve.wait_ge(chain, link.n)
                    for h in range(HEADS):
                        dve.bn_stats(stats[:, h, :], hm[:, c, h, :]).then_inc(chain, 1)
                        link.n += 1
                    dve.wait_ge(chain, link.n)
                    for h in range(HEADS):
                        dve.bn_aggr(mv[:, c, h, :], stats[:, h, :]).then_inc(chain, 1)
                        link.n += 1
                    dve.wait_ge(chain, link.n)
                dve.tensor_scalar(std[:, :, :], mv[:, :, :, 1:2].rearrange("p c h a -> p c (h a)"), EPS, None, ALU.add).then_inc(var_ready, 1)
                dve.wait_ge(std_ready, 1)
                link(dve.reciprocal(rstd[:, :, :], std[:, :, :]))
                for c in range(NC):
                    for h in range(HEADS):
                        i = dve.tensor_scalar(hm[:, c, h, :], hm[:, c, h, :], mv[:, c, h, 0:1], rstd[:, c, h:h + 1], ALU.subtract, ALU.mult)
                        i.then_inc(chain, 1)
                        link.n += 1
                dve.wait_ge(chain, link.n)
                dve.sem_inc(hn_ready, 1)
                for h in range(HEADS):
                    dve.wait_ge(out_sem, 2 * h + 2)
                    dve.tensor_tensor(M["hmT"][:, h, :], M["hmT"][:, h, :], M["og"][:, h, :], ALU.mult).then_inc(chain, 1)


def mixer_merge(nc, K, M, w_in, w_br_a, w_br_b, m, y_dram):
    hT, ps = K["hT"], K["ps"]
    with ExitStack() as ctx:
        sc = Scope(nc, ctx, "merge")
        wg = sc.sb("wg", [P, 2, 2, KT, P])
        wb = sc.sb("wb", [P, 2, 2, 4, P])
        sg = sc.sb("sg", [P, 4, HALF])
        part = sc.sb("part", [P, 2, HALF])
        loaded = [sc.sem(f"w{i}") for i in range(2)]
        done, sig, out_sem, chain = sc.sem("done"), sc.sem("sig"), sc.sem("out"), sc.sem("chain")
        zeroed = sc.sem("zeroed")
        chain_pool = sc.sem("chain_pool")
        zero = sc.sb("zero", [P, D])
        with nc.Block() as block:
            @block.sync
            def _(sp):
                for j in range(KT):
                    if j >= 2:
                        sp.wait_ge(done, 2 * 4 * (j - 1))
                    s = j % 2
                    for which, col in enumerate((COL_GA, COL_GB)):
                        sp.dma_start(wg[:, s, which, :, :], tiled_rows(w_in[:, col + j * P:col + (j + 1) * P])).then_inc(loaded[s], 16)
                    for which, src in enumerate((w_br_a, w_br_b)):
                        sp.dma_start(wb[:, s, which, :, :], tiled_rows(src[:, j * P:(j + 1) * P])).then_inc(loaded[s], 16)

            @block.gpsimd
            def _(pool):
                pool.memset(zero[:, :], 0.0).then_inc(chain_pool, 1)
                pool.wait_ge(chain_pool, 1)
                for b in range(SLOTS_B):
                    pool.dma_start(y_dram[b * P:(b + 1) * P, :], zero[:, :]).then_inc(zeroed, 16)
                pool.wait_ge(zeroed, 16 * SLOTS_B)

            @block.tensor
            def _(pe):
                for j in range(KT):
                    s = j % 2
                    pe.wait_ge(loaded[s], 64 * (j // 2 + 1))
                    for half in range(NH):
                        r = 2 * j + half
                        base = 4 * (r % 2)
                        if r >= 2:
                            pe.wait_ge(out_sem, r - 1)
                        cols = slice(half * HALF, (half + 1) * HALF)
                        for which in range(2):
                            for k in range(KT):
                                mm = pe.matmul(ps[:, base + which, :], wg[:, s, which, k, :], hT[:, k, cols], start=(k == 0), stop=(k == KT - 1))
                            mm.then_inc(done, 1)
                            src = (M["yT"], M["hmT"])[which]
                            for k in range(4):
                                mm = pe.matmul(ps[:, base + 2 + which, :], wb[:, s, which, k, :], src[:, k, cols], start=(k == 0), stop=(k == 3))
                            mm.then_inc(done, 1)

            @block.scalar
            def _(act):
                for r in range(2 * KT):
                    for which in range(2):
                        act.wait_ge(done, 4 * r + 2 * which + 1)
                        if r >= 2:
                            act.wait_ge(out_sem, r - 1)
                        act.activation(sg[:, 2 * (r % 2) + which, :], ps[:, 4 * (r % 2) + which, :], ACT.Sigmoid).then_inc(sig, 1)

            @block.vector
            def _(dve):
                link = Chain(dve, chain)
                for r in range(2 * KT):
                    j, half = r // 2, r % 2
                    for which in range(2):
                        dve.wait_ge(sig, 2 * r + which + 1)
                        dve.wait_ge(done, 4 * r + 2 * which + 2)
                        link(dve.tensor_tensor(part[:, which, :], ps[:, 4 * (r % 2) + 2 + which, :], sg[:, 2 * (r % 2) + which, :], ALU.mult))
                    cols = slice(half * HALF, (half + 1) * HALF)
                    dve.tensor_tensor(part[:, 0, :], part[:, 0, :], part[:, 1, :], ALU.add).then_inc(out_sem, 1)
                    dve.wait_ge(out_sem, r + 1)
                    link(dve.tensor_copy(m[:, 0, j, cols], part[:, 0, :]))
                    link(low_part(dve, m[:, 1, j, cols], part[:, 0, :], m[:, 0, j, cols]))


def project_add(nc, K, mT, w_out, tag, x_dram=None, halves=None):
    X, ps = K["X"], K["ps"]
    N = HALF // 2
    KH = KT // 2
    with ExitStack() as ctx:
        sc = Scope(nc, ctx, tag)
        m = halves if halves is not None else sc.sb("m", [P, 2, KT, S], F32R)
        raw = sc.sb("raw", [P, 2, KH, N])
        w = sc.sb("w", [P, 2, 2, KT, N], F32R)
        loaded = [sc.sem(f"w{i}") for i in range(2)]
        done, out_sem, x_loaded = sc.sem("done"), sc.sem("out"), sc.sem("x_loaded")
        w_high, w_split, m_high, m_split = sc.sem("w_high"), sc.sem("w_split"), sc.sem("m_high"), sc.sem("m_split")
        CHUNKS = D // N
        with nc.Block() as block:
            @block.sync
            def _(sp):
                for p in range(2 * CHUNKS):
                    if p >= 2:
                        sp.wait_ge(w_split, p - 1)
                    n, kh = p // 2, p % 2
                    sp.dma_start(raw[:, p % 2, :, :], tiled_rows(w_out[kh * KH * P:(kh + 1) * KH * P, n * N:(n + 1) * N])).then_inc(loaded[p % 2], 16)
                if x_dram is not None:
                    sp.wait_ge(x_loaded, 16 * NT)

            @block.scalar
            def _(act):
                if x_dram is not None:
                    for t in range(NT):
                        act.dma_start(X[:, t, :], x_dram[t * P:(t + 1) * P, :]).then_inc(x_loaded, 16)
                for n in range(CHUNKS):
                    if n >= 2:
                        act.wait_ge(done, NT * (n - 1))
                    for kh in range(2):
                        p = 2 * n + kh
                        act.wait_ge(loaded[p % 2], 16 * (p // 2 + 1))
                        act.activation(w[:, n % 2, 0, kh * KH:(kh + 1) * KH, :], raw[:, p % 2, :, :], ACT.Copy).then_inc(w_high, 1)
                    if n == 0 and halves is None:
                        for t in range(NT):
                            act.activation(m[:, 0, :, t * P:(t + 1) * P], mT[:, :, t * P:(t + 1) * P], ACT.Copy).then_inc(m_high, 1)

            @block.vector
            def _(dve):
                def split(n):
                    for kh in range(2):
                        p = 2 * n + kh
                        dve.wait_ge(w_high, p + 1)
                        low_part(dve, w[:, n % 2, 1, kh * KH:(kh + 1) * KH, :], raw[:, p % 2, :, :],
                                 w[:, n % 2, 0, kh * KH:(kh + 1) * KH, :]).then_inc(w_split, 1)

                split(0)
                if halves is None:
                    for t in range(NT):
                        cols = slice(t * P, (t + 1) * P)
                        dve.wait_ge(m_high, t + 1)
                        low_part(dve, m[:, 1, :, cols], mT[:, :, cols], m[:, 0, :, cols]).then_inc(m_split, 1)
                if x_dram is not None:
                    dve.wait_ge(x_loaded, 16 * NT)
                for n in range(CHUNKS):
                    if n + 1 < CHUNKS:
                        split(n + 1)
                    for t in range(NT):
                        u = n * NT + t
                        dve.wait_ge(done, u + 1)
                        dve.tensor_tensor(X[:, t, n * N:(n + 1) * N], X[:, t, n * N:(n + 1) * N], ps[:, u % 8, 0:N], ALU.add).then_inc(out_sem, 1)

            @block.tensor
            def _(pe):
                for n in range(CHUNKS):
                    pe.wait_ge(w_split, 2 * n + 2)
                    for t in range(NT):
                        u = n * NT + t
                        if n == 0 and halves is None:
                            pe.wait_ge(m_split, t + 1)
                        if u >= 8:
                            pe.wait_ge(out_sem, u - 7)
                        for k in range(KT):
                            mm = multiply_split(pe, ps[:, u % 8, 0:N], (m[:, 0, k, t * P:(t + 1) * P], m[:, 1, k, t * P:(t + 1) * P]),
                                                (w[:, n % 2, 0, k, :], w[:, n % 2, 1, k, :]), k == 0, k == KT - 1)
                        mm.then_inc(done, 1)


def norm_rows(nc, K, g, tag, out=None):
    X = K["X"]
    with ExitStack() as ctx:
        sc = Scope(nc, ctx, tag)
        grow = sc.sb("grow", [P, D])
        squares = sc.sb("squares", [P, 2, D])
        ss, var, std, rs = [sc.sb(n, [P, NT]) for n in ("ss", "var", "std", "rs")]
        g_loaded, summed, var_ready, std_ready, done, chain, stored = [sc.sem(n) for n in
            ("g_loaded", "summed", "var_ready", "std_ready", "done", "chain", "stored")]
        with nc.Block() as block:
            @block.sync
            def _(sp):
                sp.dma_start(grow[:, :], g.partition_broadcast(P)).then_inc(g_loaded, 16)
                if out is not None:
                    for t in range(NT):
                        sp.wait_ge(done, t + 1)
                        sp.dma_start(out[t * P:(t + 1) * P, :], X[:, t, :]).then_inc(stored, 16)
                    sp.wait_ge(stored, 16 * NT)

            @block.scalar
            def _(act):
                for t in range(NT):
                    if t >= 2:
                        act.wait_ge(summed, t - 1)
                    act.activation(squares[:, t % 2, :], X[:, t, :], ACT.Square, accum_out=ss[:, t:t + 1]).then_inc(summed, 1)
                act.wait_ge(var_ready, 1)
                act.activation(std[:, :], var[:, :], ACT.Sqrt).then_inc(std_ready, 1)

            @block.vector
            def _(dve):
                link = Chain(dve, chain)
                dve.wait_ge(summed, NT)
                dve.tensor_scalar(var[:, :], ss[:, :], 1.0 / D, EPS, ALU.mult, ALU.add).then_inc(var_ready, 1)
                dve.wait_ge(std_ready, 1)
                link(dve.reciprocal(rs[:, :], std[:, :]))
                dve.wait_ge(g_loaded, 16)
                for t in range(NT):
                    dve.scalar_tensor_tensor(out=X[:, t, :], in0=X[:, t, :], scalar=rs[:, t:t + 1], in1=grow[:, :],
                                             op0=ALU.mult, op1=ALU.mult).then_inc(done, 1)


def route(nc, K, R, w_rg, b_rg, w_re, b_re, slot_tok):
    hT, ps = K["hT"], K["ps"]
    NL = GROUPS + EXPERTS
    with ExitStack() as ctx:
        sc = Scope(nc, ctx, "route")
        wr = sc.sb("wr", [P, KT, NL])
        brow = sc.sb("brow", [P, NL])
        L = sc.sb("L", [P, NT, NL])
        gi = sc.sb("gi", [P, GROUPS])
        ei = sc.sb("ei", [P, EXPERTS])
        bi = sc.sb("bi", [1, SLOTS_B])
        tok = sc.sb("tok", [P, NT], I32)
        zero = sc.sb("zero", [P, SLOTS_B], I32)
        gmax, gsum, pg, cmin = [sc.sb(n, [P, NT]) for n in ("gmax", "gsum", "pg", "cmin")]
        ge, gc, oh_g = [sc.sb(n, [P, NT, GROUPS]) for n in ("ge", "gc", "oh_g")]
        em = sc.sb("em", [P, NT, EXPERTS])
        cand = sc.sb("cand", [P, NT, EXPERTS])
        oh = sc.sb("oh", [P, TOP_K, NT, EXPERTS])
        both = sc.sb("both", [P, NT, EXPERTS])
        top = sc.sb("top", [P, TOP_K, NT])
        e2, den = sc.sb("e2", [P, NT]), sc.sb("den", [P, NT])
        rank = sc.sb("rank", [P, NT, EXPERTS])
        cnt = sc.sb("cnt", [P, EXPERTS])
        nblk = sc.sb("nblk", [P, EXPERTS])
        pend = sc.sb("pend", [P, 2, EXPERTS])
        dest = sc.sb("dest", [P, TOP_K, NT])
        cmp = sc.sb("cmp", [1, SLOTS_B, EXPERTS])
        be = sc.sb("be", [1, SLOTS_B])
        loaded, iotas, chain, logits, ranks, exp_in, exp_out = [sc.sem(n) for n in
            ("loaded", "iotas", "chain", "logits", "ranks", "exp_in", "exp_out")]
        picked, dest_ready, zeroed, scattered, idx_loaded = [sc.sem(n) for n in ("picked", "dest_ready", "zeroed", "scattered", "idx_loaded")]
        with nc.Block() as block:
            @block.sync
            def _(sp):
                sp.dma_start(wr[:, :, 0:GROUPS], tiled_rows(w_rg)).then_inc(loaded, 16)
                sp.dma_start(wr[:, :, GROUPS:NL], tiled_rows(w_re)).then_inc(loaded, 16)
                sp.dma_start(brow[:, 0:GROUPS], b_rg.partition_broadcast(P)).then_inc(loaded, 16)
                sp.dma_start(brow[:, GROUPS:NL], b_re.partition_broadcast(P)).then_inc(loaded, 16)
                sp.wait_ge(iotas, 5)
                sp.dma_start(slot_tok.rearrange("(p b) a -> p (b a)", p=P), zero[:, :]).then_inc(zeroed, 16)
                sp.wait_ge(scattered, 16 * TOP_K * NT)
                sp.dma_start(R["idx"][:, :], slot_tok.rearrange("(b p) a -> p (b a)", p=P)).then_inc(idx_loaded, 16)
                sp.wait_ge(idx_loaded, 16)

            @block.gpsimd
            def _(pool):
                pool.iota(gi[:, :], pattern=[[1, GROUPS]], base=0, channel_multiplier=0, allow_small_or_imprecise_dtypes=True).then_inc(iotas, 1)
                pool.iota(ei[:, :], pattern=[[1, EXPERTS]], base=0, channel_multiplier=0, allow_small_or_imprecise_dtypes=True).then_inc(iotas, 1)
                pool.iota(bi[:, :], pattern=[[1, SLOTS_B]], base=0, channel_multiplier=0, allow_small_or_imprecise_dtypes=True).then_inc(iotas, 1)
                pool.iota(tok[:, :], pattern=[[P, NT]], base=0, channel_multiplier=1).then_inc(iotas, 1)
                pool.memset(zero[:, :], 0).then_inc(iotas, 1)
                pool.wait_ge(iotas, 5)
                pool.wait_ge(zeroed, 16)
                for i in range(TOP_K):
                    pool.wait_ge(dest_ready, i + 1)
                    for t in range(NT):
                        pool.indirect_dma_start(out=slot_tok, out_offset=bass.IndirectOffsetOnAxis(ap=R["dest"][:, i, t:t + 1], axis=0),
                                                in_=tok[:, t:t + 1], in_offset=None).then_inc(scattered, 16)
                pool.wait_ge(scattered, 16 * TOP_K * NT)

            @block.tensor
            def _(pe):
                pe.wait_ge(loaded, 64)
                for t in range(NT):
                    for k in range(KT):
                        mm = pe.matmul(ps[:, 0, t * NL:(t + 1) * NL], hT[:, k, t * P:(t + 1) * P], wr[:, k, :],
                                       start=(k == 0), stop=(k == KT - 1), skip_group_check=True)
                mm.then_inc(logits, 1)
                pe.wait_ge(picked, 1)
                for t in range(NT):
                    for j in range(t + 1):
                        mm = pe.matmul(ps[:, 1, t * EXPERTS:(t + 1) * EXPERTS], K["ones"][:, :] if j < t else K["earlier"][:, :],
                                       both[:, j, :], start=(j == 0), stop=(j == t), skip_group_check=True)
                for j in range(NT):
                    mm = pe.matmul(ps[:, 2, 0:EXPERTS], K["ones"][:, :], both[:, j, :], start=(j == 0), stop=(j == NT - 1))
                mm.then_inc(ranks, 1)

            @block.scalar
            def _(act):
                act.wait_ge(exp_in, 1)
                act.activation(ge[:, :, :], ge[:, :, :], ACT.Exp).then_inc(exp_out, 1)
                act.wait_ge(exp_in, 2)
                act.activation(e2[:, :], e2[:, :], ACT.Exp).then_inc(exp_out, 1)

            @block.vector
            def _(dve):
                link = Chain(dve, chain)

                def over(ap, n):
                    return ap.rearrange("p (t a) -> p t a", a=1).to_broadcast([P, NT, n])

                def each(ap, n):
                    return ap.rearrange("p (a n) -> p a n", a=1).to_broadcast([P, NT, n])

                def first_max(out, vals, m, idx, c, n):
                    link(dve.tensor_tensor(c, vals, over(m, n), ALU.is_equal))
                    link(dve.scalar_tensor_tensor(out=c, in0=c, scalar=-64.0, in1=each(idx, n), op0=ALU.mult, op1=ALU.add))
                    link(dve.tensor_reduce(cmin[:, :], c, AX.X, ALU.min))
                    link(dve.tensor_tensor(out, c, over(cmin[:, :], n), ALU.is_equal))

                dve.wait_ge(loaded, 64)
                dve.wait_ge(iotas, 5)
                dve.wait_ge(logits, 1)
                link(dve.tensor_tensor(L[:, :, :], ps[:, 0, 0:NT * NL].rearrange("p (t n) -> p t n", n=NL), each(brow[:, :], NL), ALU.add))
                gl, el = L[:, :, 0:GROUPS], L[:, :, GROUPS:NL]
                link(dve.tensor_reduce(gmax[:, :], gl, AX.X, ALU.max))
                dve.tensor_tensor(ge[:, :, :], gl, over(gmax[:, :], GROUPS), ALU.subtract).then_inc(exp_in, 1)
                first_max(oh_g[:, :, :], gl, gmax[:, :], gi[:, :], gc[:, :, :], GROUPS)
                link(dve.tensor_scalar(gc[:, :, :], oh_g[:, :, :], 1.0, -NEG, ALU.subtract, ALU.mult))
                for g in range(GROUPS):
                    i = dve.tensor_tensor(em[:, :, g * PER_GROUP:(g + 1) * PER_GROUP], el[:, :, g * PER_GROUP:(g + 1) * PER_GROUP],
                                          gc[:, :, g:g + 1].to_broadcast([P, NT, PER_GROUP]), ALU.add)
                    link(i)
                link(dve.tensor_reduce(top[:, 0, :], em[:, :, :], AX.X, ALU.max))
                first_max(oh[:, 0, :, :], em[:, :, :], top[:, 0, :], ei[:, :], cand[:, :, :], EXPERTS)
                link(dve.scalar_tensor_tensor(out=em[:, :, :], in0=oh[:, 0, :, :], scalar=2.0 * NEG, in1=em[:, :, :], op0=ALU.mult, op1=ALU.add))
                link(dve.tensor_reduce(top[:, 1, :], em[:, :, :], AX.X, ALU.max))
                dve.tensor_tensor(e2[:, :], top[:, 1, :], top[:, 0, :], ALU.subtract).then_inc(exp_in, 1)
                first_max(oh[:, 1, :, :], em[:, :, :], top[:, 1, :], ei[:, :], cand[:, :, :], EXPERTS)
                dve.tensor_tensor(both[:, :, :], oh[:, 0, :, :], oh[:, 1, :, :], ALU.add).then_inc(picked, 1)
                dve.wait_ge(exp_out, 2)
                link(dve.tensor_reduce(gsum[:, :], ge[:, :, :], AX.X, ALU.add))
                link(dve.reciprocal(pg[:, :], gsum[:, :]))
                link(dve.tensor_scalar(den[:, :], e2[:, :], 1.0, None, ALU.add))
                link(dve.reciprocal(den[:, :], den[:, :]))
                link(dve.tensor_tensor(R["gate"][:, 0, :], pg[:, :], den[:, :], ALU.mult))
                link(dve.tensor_tensor(R["gate"][:, 1, :], R["gate"][:, 0, :], e2[:, :], ALU.mult))
                dve.wait_ge(ranks, 1)
                link(dve.tensor_copy(cnt[:, :], ps[:, 2, 0:EXPERTS]))
                link(dve.tensor_scalar(nblk[:, :], cnt[:, :], 0.0, None, ALU.is_gt))
                for j in range(1, S // P):
                    link(dve.scalar_tensor_tensor(out=nblk[:, :], in0=cnt[:, :], scalar=float(j * P), in1=nblk[:, :], op0=ALU.is_gt, op1=ALU.add))
                link(dve.tensor_copy(pend[:, 0, :], nblk[:, :]))
                cur = 0
                for step in (1, 2, 4, 8, 16):
                    link(dve.tensor_copy(pend[:, 1 - cur, 0:step], pend[:, cur, 0:step]))
                    link(dve.tensor_tensor(pend[:, 1 - cur, step:], pend[:, cur, step:], pend[:, cur, 0:EXPERTS - step], ALU.add))
                    cur = 1 - cur
                link(dve.tensor_tensor(nblk[:, :], pend[:, cur, :], nblk[:, :], ALU.subtract))
                link(dve.tensor_scalar(nblk[:, :], nblk[:, :], float(P), None, ALU.mult))
                link(dve.tensor_tensor(rank[:, :, :], ps[:, 1, 0:NT * EXPERTS].rearrange("p (t e) -> p t e", e=EXPERTS), each(nblk[:, :], EXPERTS), ALU.add))
                for i in range(TOP_K):
                    link(dve.tensor_tensor(cand[:, :, :], rank[:, :, :], oh[:, i, :, :], ALU.mult))
                    link(dve.tensor_reduce(dest[:, i, :], cand[:, :, :], AX.X, ALU.add))
                    dve.tensor_copy(R["dest"][:, i, :], dest[:, i, :]).then_inc(dest_ready, 1)
                ends = pend[0:1, cur, :].rearrange("p (a e) -> p a e", a=1).to_broadcast([1, SLOTS_B, EXPERTS])
                link(dve.tensor_tensor(cmp[:, :, :], ends, bi[:, :].rearrange("p (b a) -> p b a", a=1).to_broadcast([1, SLOTS_B, EXPERTS]), ALU.is_le))
                link(dve.tensor_reduce(be[:, :], cmp[:, :, :], AX.X, ALU.add))
                link(dve.tensor_scalar(be[:, :], be[:, :], float(EXPERTS - 1), None, ALU.min))
                link(dve.tensor_copy(R["block_e"][:, :], be[:, :]))
                link(dve.tensor_copy(R["n_blocks"][:, :], pend[0:1, cur, EXPERTS - 1:EXPERTS]))


def experts(nc, K, R, h_dram, y_dram, w_gate, w_up, w_down):
    ps, ident = K["ps"], K["ident"]
    GC = KT // 2
    CH = 2 * GC + FT
    with ExitStack() as ctx:
        sc = Scope(nc, ctx, "moe")
        wg = sc.sb("wg", [P, KT, D_EXP])
        wu = sc.sb("wu", [P, KT, D_EXP])
        wd = sc.sb("wd", [P, FT, D])
        xg = sc.sb("xg", [P, D])
        xT = sc.sb("xT", [P, KT, P])
        idx = sc.sb("idx", [P, 1], I32)
        sil = sc.sb("sil", [P, HALF])
        hid = sc.sb("hid", [P, FT, P])
        y = sc.sb("y", [P, D])
        loaded = [sc.sem(f"w{c}") for c in range(CH)]
        used, gathered, idx_ready, xt_made, xt_act, xt_dve, sil_ready, hid_ready, y_act, y_dve, y_stored, settled, settled_act = [sc.sem(n) for n in
            ("used", "gathered", "idx_ready", "xt_made", "xt_act", "xt_dve", "sil_ready", "hid_ready", "y_act", "y_dve", "y_stored", "settled", "settled_act")]
        wg_d = w_gate.rearrange("e (c k p) f -> (e c) p k f", p=P, k=2)
        wu_d = w_up.rearrange("e (c k p) f -> (e c) p k f", p=P, k=2)
        wd_d = w_down.rearrange("e (c p) d -> (e c) p d", p=P)
        nb_ap = R["n_blocks"][0:1, 0:1]
        with nc.Block() as block:
            @block.sync
            def _(sp):
                nb = sp.value_load(nb_ap, min_val=1, max_val=BLOCKS)
                with sp.Fori(0, nb) as i:
                    e = sp.value_load(R["block_e"][0:1, bass.ds(i, 1)], min_val=0, max_val=EXPERTS - 1)
                    for c in range(GC):
                        for which, (dst, src) in enumerate(((wg, wg_d), (wu, wu_d))):
                            n = 2 * c + which
                            sp.wait_ge(used, i * CH + n + 1)
                            sp.dma_start(dst[:, 2 * c:2 * c + 2, :], src[bass.ds(e * GC + c, 1), :, :, :].rearrange("a p k f -> p (a k) f")).then_inc(loaded[n], 16)
                    for f in range(FT):
                        n = 2 * GC + f
                        sp.wait_ge(used, i * CH + n + 1)
                        sp.dma_start(wd[:, f, :], wd_d[bass.ds(e * FT + f, 1), :, :].rearrange("a p d -> p (a d)")).then_inc(loaded[n], 16)

            @block.gpsimd
            def _(pool):
                nb = pool.value_load(nb_ap, min_val=1, max_val=BLOCKS)
                with pool.Fori(0, nb + 1) as i:
                    pool.wait_ge(xt_made, i + 1)
                    pool.tensor_copy(idx[:, :], R["idx"][:, bass.ds(i, 1)]).then_inc(idx_ready, 1)
                    pool.wait_ge(idx_ready, i + 1)
                    pool.sem_inc(settled, 1)
                    pool.indirect_dma_start(out=xg[:, :], out_offset=None, in_=h_dram,
                                            in_offset=bass.IndirectOffsetOnAxis(ap=idx[:, 0:1], axis=0)).then_inc(gathered, 16)
                    pool.wait_ge(gathered, i * 16 + 16)

            def turn(pe):
                for k in range(KT):
                    mm = pe.transpose(ps[:, 4 + k // 4, (k % 4) * P:(k % 4 + 1) * P], xg[:, k * P:(k + 1) * P], ident[:, :])
                mm.then_inc(xt_made, 1)

            @block.tensor
            def _(pe):
                pe.sem_inc(used, CH)
                pe.sem_inc(xt_made, 1)
                pe.wait_ge(gathered, 16)
                turn(pe)
                nb = pe.value_load(nb_ap, min_val=1, max_val=BLOCKS)
                with pe.Fori(0, nb) as i:
                    pe.wait_ge(xt_act, i + 1)
                    pe.wait_ge(xt_dve, i + 1)
                    for c in range(GC):
                        for which, w in enumerate((wg, wu)):
                            pe.wait_ge(loaded[2 * c + which], i * 16 + 16)
                            for k in (2 * c, 2 * c + 1):
                                for f in range(FT):
                                    mm = pe.matmul(ps[:, which, f * P:(f + 1) * P], w[:, k, f * P:(f + 1) * P], xT[:, k, :],
                                                   start=(k == 0 and f == 0), stop=(k == KT - 1), skip_group_check=True)
                            mm.then_inc(used, 1)
                    pe.wait_ge(gathered, i * 16 + 32)
                    turn(pe)
                    pe.wait_ge(hid_ready, i + 1)
                    pe.wait_ge(y_act, i + 1)
                    pe.wait_ge(y_dve, i + 1)
                    for f in range(FT):
                        pe.wait_ge(loaded[2 * GC + f], i * 16 + 16)
                        for n in range(2):
                            mm = pe.matmul(ps[:, 2 + n, :], hid[:, f, :], wd[:, f, n * HALF:(n + 1) * HALF], start=(f == 0), stop=(f == FT - 1))
                        mm.then_inc(used, 1)

            @block.scalar
            def _(act):
                act.sem_inc(y_act, 1)
                act.dma_start(y_dram[BLOCKS * P:(BLOCKS + 1) * P, 0:P], ident[:, :]).then_inc(y_stored, 16)
                act.wait_ge(xt_made, 2)
                act.activation(xT[:, 0:4, :], ps[:, 4, :].rearrange("p (k t) -> p k t", t=P), ACT.Copy).then_inc(xt_act, 1)
                nb = act.value_load(nb_ap, min_val=1, max_val=BLOCKS)
                with act.Fori(0, nb) as i:
                    act.wait_ge(used, i * CH + (CH + 2 * GC))
                    act.activation(sil[:, :], ps[:, 0, :], ACT.Silu).then_inc(sil_ready, 1)
                    act.wait_ge(xt_made, i + 3)
                    act.activation(xT[:, 0:4, :], ps[:, 4, :].rearrange("p (k t) -> p k t", t=P), ACT.Copy).then_inc(xt_act, 1)
                    act.wait_ge(used, i * CH + 2 * CH)
                    act.wait_ge(y_stored, i * 16 + 16)
                    act.activation(y[:, 0:HALF], ps[:, 2, :], ACT.Copy).then_inc(y_act, 1)
                    act.wait_ge(y_act, i + 2)
                    act.wait_ge(y_dve, i + 2)
                    act.dma_start(y_dram[bass.ds(i * P, P), :], y[:, :]).then_inc(y_stored, 16)
                act.wait_ge(y_stored, nb * 16 + 16)
                act.sem_inc(settled_act, 1)

            @block.vector
            def _(dve):
                dve.sem_inc(y_dve, 1)
                dve.wait_ge(xt_made, 2)
                dve.tensor_copy(xT[:, 4:8, :], ps[:, 5, :].rearrange("p (k t) -> p k t", t=P)).then_inc(xt_dve, 1)
                nb = dve.value_load(nb_ap, min_val=1, max_val=BLOCKS)
                with dve.Fori(0, nb) as i:
                    dve.wait_ge(sil_ready, i + 1)
                    dve.tensor_tensor(hid[:, :, :], sil[:, :].rearrange("p (f t) -> p f t", t=P), ps[:, 1, :].rearrange("p (f t) -> p f t", t=P), ALU.mult).then_inc(hid_ready, 1)
                    dve.wait_ge(xt_made, i + 3)
                    dve.tensor_copy(xT[:, 4:8, :], ps[:, 5, :].rearrange("p (k t) -> p k t", t=P)).then_inc(xt_dve, 1)
                    dve.wait_ge(used, i * CH + 2 * CH)
                    dve.wait_ge(y_stored, i * 16 + 16)
                    dve.tensor_copy(y[:, HALF:D], ps[:, 3, :]).then_inc(y_dve, 1)


def combine(nc, K, R, y_dram):
    X = K["X"]
    DEPTH = 4
    with ExitStack() as ctx:
        sc = Scope(nc, ctx, "comb")
        yg = sc.sb("yg", [P, DEPTH, D])
        got = [sc.sem(f"got{d}") for d in range(DEPTH)]
        added = sc.sem("added")
        order = [(t, i) for t in range(NT) for i in range(TOP_K)]
        with nc.Block() as block:
            @block.gpsimd
            def _(pool):
                for n, (t, i) in enumerate(order):
                    if n >= DEPTH:
                        pool.wait_ge(added, n - DEPTH + 1)
                    pool.indirect_dma_start(out=yg[:, n % DEPTH, :], out_offset=None, in_=y_dram,
                                            in_offset=bass.IndirectOffsetOnAxis(ap=R["dest"][:, i, t:t + 1], axis=0)).then_inc(got[n % DEPTH], 16)

            @block.vector
            def _(dve):
                for n, (t, i) in enumerate(order):
                    dve.wait_ge(got[n % DEPTH], 16 * (n // DEPTH + 1))
                    if i:
                        dve.wait_ge(added, n)
                    dve.scalar_tensor_tensor(out=X[:, t, :], in0=yg[:, n % DEPTH, :], scalar=R["gate"][:, i, t:t + 1], in1=X[:, t, :],
                                             op0=ALU.mult, op1=ALU.add).then_inc(added, 1)


def bias_tables(nc, K, T, G_dram, rel_bias, onehot, which):
    ps = K["ps"]
    with ExitStack() as ctx:
        sc = Scope(nc, ctx, f"bias{which}")
        rb = sc.sb("rb", [BUCKETS + 1, A_HEADS + B_HEADS])
        oh = sc.sb("oh", [BUCKETS + 1, len(DILATIONS), BAND])
        strip = sc.sb("strip", [A_HEADS + B_HEADS, len(DILATIONS), BAND])
        anti, anti64 = sc.sb("anti", [P, P]), sc.sb("anti64", [64, P])
        rev = sc.sb("rev", [P, 4, HALF])
        rev16 = sc.sb("rev16", [64, B_HEADS, 64])
        loaded, rb_ready, antis, made, strips, written, rev_in, out_sem = [sc.sem(n) for n in
            ("loaded", "rb_ready", "antis", "made", "strips", "written", "rev_in", "out")]
        rev_loaded = [sc.sem(f"rev_loaded{i}") for i in range(4)]
        if which == "A":
            jobs = [(T["A"], 0, h, h) for h in range(0, A_HEADS, 2)]
        else:
            jobs = [(T[f"B{c}"], c, A_HEADS + h, h) for c in range(2) for h in range(0, B_HEADS, 2)]
        NJ = len(jobs)
        with nc.Block() as block:
            @block.sync
            def _(sp):
                sp.dma_start(rb[0:BUCKETS, :], rel_bias).then_inc(loaded, 16)
                sp.dma_start(oh[:, :, :], onehot).then_inc(loaded, 16)
                sp.wait_ge(strips, 3)
                sp.dma_start(G_dram, strip[:, :, :]).then_inc(written, 16)
                sp.wait_ge(written, 16)
                for n, (table, c, h, slot) in enumerate(jobs):
                    if n >= 4:
                        sp.wait_ge(made, n)
                    base = G_dram[h:h + 2, c, 0:1]
                    src = bass.AP(tensor=base.tensor, offset=base.offset, ap=[[1, P], [len(DILATIONS) * BAND, 2], [1, 2 * P]])
                    sp.dma_start(rev[:, n % 4, :].rearrange("p (h j) -> p h j", h=2), src).then_inc(rev_loaded[n % 4], 16)
                if which == "B":
                    base = G_dram[A_HEADS:A_HEADS + 1, 2, 192:193]
                    src = bass.AP(tensor=base.tensor, offset=base.offset, ap=[[1, 64], [len(DILATIONS) * BAND, B_HEADS], [1, 64]])
                    sp.dma_start(rev16[:, :, :], src).then_inc(rev_in, 16)

            @block.gpsimd
            def _(pool):
                pool.memset(rb[BUCKETS:BUCKETS + 1, :], NEG).then_inc(rb_ready, 1)
                pool.wait_ge(rb_ready, 1)
                pool.memset(anti[:, :], 0.0).then_inc(antis, 1)
                pool.memset(anti64[:, :], 0.0).then_inc(antis, 1)
                pool.wait_ge(antis, 2)
                pool.affine_select(out=anti[:, :], in_=anti[:, :], compare_op=ALU.not_equal, fill=1.0, base=1 - P,
                                   pattern=[[1, P]], channel_multiplier=1).then_inc(antis, 1)
                pool.affine_select(out=anti64[:, :].rearrange("p (a n) -> p a n", a=2), in_=anti64[:, :].rearrange("p (a n) -> p a n", a=2),
                                   compare_op=ALU.not_equal, fill=1.0, base=-63, pattern=[[0, 2], [1, 64]], channel_multiplier=1).then_inc(antis, 1)

            @block.tensor
            def _(pe):
                pe.wait_ge(loaded, 32)
                pe.wait_ge(rb_ready, 1)
                for c in range(3):
                    pe.matmul(ps[0:A_HEADS + B_HEADS, c, 0:BAND], rb[:, :], oh[:, c, :], start=True, stop=True).then_inc(made, 1)
                pe.wait_ge(antis, 4)
                for n in range(NJ):
                    pe.wait_ge(rev_loaded[n % 4], 16 * (n // 4 + 1))
                    if n >= 4:
                        pe.wait_ge(out_sem, n - 3)
                    pe.matmul(ps[:, 4 + n % 4, :], anti[:, :], rev[:, n % 4, :], start=True, stop=True).then_inc(made, 1)
                if which == "B":
                    pe.wait_ge(rev_in, 16)
                    pe.wait_ge(out_sem, NJ - 3)
                    pe.matmul(ps[:, 4 + NJ % 4, :], anti64[:, :], rev16[:, :, :], start=True, stop=True).then_inc(made, 1)

            @block.scalar
            def _(act):
                for c in range(3):
                    act.wait_ge(made, c + 1)
                    act.activation(strip[:, c, :], ps[0:A_HEADS + B_HEADS, c, 0:BAND], ACT.Copy, scale=1.0 / SC_AB).then_inc(strips, 1)
                for n, (table, c, h, slot) in enumerate(jobs):
                    act.wait_ge(made, 3 + n + 1)
                    act.activation(table[:, slot:slot + 2, :], ps[:, 4 + n % 4, :].rearrange("p (h j) -> p h j", h=2), ACT.Copy).then_inc(out_sem, 1)
                if which == "B":
                    act.wait_ge(made, 3 + NJ + 1)
                    act.activation(T["B2"][:, :, :], ps[:, 4 + NJ % 4, :].rearrange("p (h j) -> p h j", j=64), ACT.Copy).then_inc(out_sem, 1)


def ab_projections(nc, K, B, w_in, vb_dram):
    hT, ps = K["hT"], K["ps"]
    SLOTS = 6
    with ExitStack() as ctx:
        sc = Scope(nc, ctx, "abp")
        w = sc.sb("w", [P, SLOTS, KT, P])
        vs = sc.sb("vs", [P, 2, HALF])
        loaded = [sc.sem(f"w{i}") for i in range(SLOTS)]
        made, evac, slot_free = sc.sem("made"), sc.sem("evac"), sc.sem("slot_free")
        v_stored = [sc.sem("v_stored0"), sc.sem("v_stored1")]
        tiles = [("qa", i, None) for i in range(4)] + [("ka", 0, COL_KA), ("va", 0, COL_VA)]
        tiles += [("vb", i, COL_VB + i * P) for i in range(4)]
        tiles += [("qb", i, COL_QB + i * P) for i in range(4)] + [("kb", i, COL_KB + i * P) for i in range(4)]
        dma_of = [0] * SLOTS
        need = []
        for n, (kind, i, col) in enumerate(tiles):
            dma_of[n % SLOTS] += 2 if kind == "qa" else 1
            need.append(16 * dma_of[n % SLOTS])
        units = []
        for n, (kind, i, col) in enumerate(tiles):
            if kind in ("qa", "ka", "qb", "kb"):
                dst = {"qa": B["qa"], "ka": B["ka"], "qb": B["qb"], "kb": B["kb"]}[kind]
                units += [(n, dst[:, i, half * HALF:(half + 1) * HALF]) for half in range(NH)]
            elif kind == "va":
                units += [(n, t) for t in range(NT)]
            elif i == 3:
                units += [(n, t) for t in range(NT)]
        with nc.Block() as block:
            @block.sync
            def _(sp):
                for n, (kind, i, col) in enumerate(tiles):
                    if n >= SLOTS:
                        sp.wait_ge(slot_free, n - SLOTS + 1)
                    s = n % SLOTS
                    if kind == "qa":
                        for j in range(2):
                            c0 = COL_QA + (i + 4 * j) * HD
                            sp.dma_start(w[:, s, :, j * HD:(j + 1) * HD], tiled_rows(w_in[:, c0:c0 + HD])).then_inc(loaded[s], 16)
                    else:
                        sp.dma_start(w[:, s, :, :], tiled_rows(w_in[:, col:col + P])).then_inc(loaded[s], 16)

            @block.tensor
            def _(pe):
                u = 0
                for n, (kind, i, col) in enumerate(tiles):
                    s = n % SLOTS
                    pe.wait_ge(loaded[s], need[n])
                    if kind in ("qa", "ka", "qb", "kb"):
                        for half in range(NH):
                            if u >= 8:
                                pe.wait_ge(evac, u - 7)
                            for k in range(KT):
                                mm = pe.matmul(ps[:, u % 8, :], w[:, s, k, :], hT[:, k, half * HALF:(half + 1) * HALF], start=(k == 0), stop=(k == KT - 1))
                            mm.then_inc(made, 1)
                            u += 1
                        pe.wait_ge(made, u)
                        pe.sem_inc(slot_free, 1)
                    elif kind == "va":
                        for t in range(NT):
                            pe.wait_ge(evac, u - 7)
                            for k in range(KT):
                                mm = pe.matmul(ps[:, u % 8, 0:P], hT[:, k, t * P:(t + 1) * P], w[:, s, k, :], start=(k == 0), stop=(k == KT - 1))
                            mm.then_inc(made, 1)
                            u += 1
                        pe.wait_ge(made, u)
                        pe.sem_inc(slot_free, 1)
                    elif i == 3:
                        s0 = (n - 3) % SLOTS
                        for t in range(NT):
                            pe.wait_ge(evac, u - 7)
                            for k in range(KT):
                                mm = pe.matmul(ps[:, u % 8, :], hT[:, k, t * P:(t + 1) * P], w[:, s0:s0 + 4, k, :], start=(k == 0), stop=(k == KT - 1))
                            mm.then_inc(made, 1)
                            u += 1
                        pe.wait_ge(made, u)
                        pe.sem_inc(slot_free, 4)

            @block.scalar
            def _(act):
                for u, (n, dst) in enumerate(units):
                    kind = tiles[n][0]
                    act.wait_ge(made, u + 1)
                    if kind == "va":
                        act.activation(B["va"][:, dst, :], ps[:, u % 8, 0:P], ACT.Copy).then_inc(evac, 1)
                    elif kind == "vb":
                        if dst >= 2:
                            act.wait_ge(v_stored[dst % 2], 16 * (dst // 2))
                        act.activation(vs[:, dst % 2, :], ps[:, u % 8, :], ACT.Copy).then_inc(evac, 1)
                        act.wait_ge(evac, u + 1)
                        act.dma_start(vb_dram[dst * P:(dst + 1) * P, :], vs[:, dst % 2, :]).then_inc(v_stored[dst % 2], 16)
                    else:
                        act.activation(dst, ps[:, u % 8, :], ACT.Copy).then_inc(evac, 1)
                for stored in v_stored:
                    act.wait_ge(stored, 16 * NT // 2)


def banded_attention(nc, K, B, T, oT, which, vb_dram, sinks):
    ps, ident = K["ps"], K["ident"]
    GU = 4
    dil = which == "B"
    with ExitStack() as ctx:
        sc = Scope(nc, ctx, f"att{which}")
        s_sb = sc.sb("s", [P, 2, GU, 2 * P])
        pT = sc.sb("pT", [P, 2, GU, 2 * P])
        mx, nm, rsum, es, den, rden, lse = [sc.sb(n, [P, 2, GU]) for n in ("mx", "nm", "rsum", "es", "den", "rden", "lse")]
        if dil:
            v1 = sc.sb("v1", [P, 2, NT, P])
            v4 = sc.sb("v4", [P, 2, 4, 2, P])
            v16 = sc.sb("v16", [64, 2, 16, P])
            oc = sc.sb("oc", [P, 3, S])
            lb = sc.sb("lb", [P, 3, S])
            v_loaded = [sc.sem("v_loaded0"), sc.sem("v_loaded1")]
        else:
            sk = sc.sb("sk", [P, A_HEADS])
            sk_loaded = sc.sem("sk_loaded")
        s_made, s_taken, m_ready, p_ready, n_ready, turned, pt_act, pt_dve, o_made, o_out, chain, mixed, exp_in, exp_out, l_made = [sc.sem(n) for n in
            ("s_made", "s_taken", "m_ready", "p_ready", "n_ready", "turned", "pt_act", "pt_dve", "o_made", "o_out", "chain", "mixed", "exp_in", "exp_out", "l_made")]
        ln_ready = sc.sem("ln_ready")

        groups = []
        for h in range(B_HEADS if dil else A_HEADS):
            if not dil:
                tile_i, half = h % 4, h // 4
                row = slice(half * HD, (half + 1) * HD)
                q, k = B["qa"][row, tile_i, :], B["ka"][row, 0, :]
                for g in range(2):
                    units = []
                    for i in range(4 * g, 4 * g + 4):
                        k0 = max(i - 1, 0) * P
                        nk = (i + 1) * P - k0
                        vals = [(B["va"][:, k0 // P + b, half * HD:(half + 1) * HD], P, b * P, slice(0, P)) for b in range(nk // P)]
                        units.append(([(0, P, q[:, i * P:(i + 1) * P], k[:, k0:k0 + nk])], nk, T["A"][:, h, 2 * P - nk:], vals))
                    groups.append((h, 0, units, oT[(h % 2) * HD:(h % 2 + 1) * HD, h // 2, g * HALF:(g + 1) * HALF], lambda a: a))
                continue
            row = slice((h % 2) * HD, (h % 2 + 1) * HD)
            q, k = B["qb"][row, h // 2, :], B["kb"][row, h // 2, :]
            vslot, vcol = (h // 2) % 2, slice((h % 2) * HD, (h % 2 + 1) * HD)
            for g in range(2):
                units = []
                for i in range(4 * g, 4 * g + 4):
                    k0 = max(i - 1, 0) * P
                    nk = (i + 1) * P - k0
                    vals = [(v1[:, vslot, k0 // P + b, vcol], P, b * P, slice(0, P)) for b in range(nk // P)]
                    units.append(([(0, P, q[:, i * P:(i + 1) * P], k[:, k0:k0 + nk])], nk, T["B0"][:, h, 2 * P - nk:], vals))
                dst = slice(g * HALF, (g + 1) * HALF)
                groups.append((h, 0, units, (lambda a, dst=dst: a[:, dst]), lambda a: a))
            q4, k4 = q.rearrange("p (m r) -> p r m", r=4), k.rearrange("p (m r) -> p r m", r=4)
            for g in range(2):
                units = []
                for r in (2 * g, 2 * g + 1):
                    for n in range(2):
                        nk = (n + 1) * P
                        vals = [(v4[:, vslot, r, b, vcol], P, b * P, slice(0, P)) for b in range(n + 1)]
                        units.append(([(0, P, q4[:, r, n * P:(n + 1) * P], k4[:, r, 0:nk])], nk, T["B1"][:, h, 2 * P - nk:], vals))
                groups.append((h, 1, units, (lambda a, g=g: a.rearrange("p (m r) -> p r m", r=4)[:, 2 * g:2 * g + 2, :]),
                               lambda a: a.rearrange("p (r m) -> p r m", r=2)))
            q16, k16 = q.rearrange("p (j r) -> p r j", r=16), k.rearrange("p (j r) -> p r j", r=16)
            for g in range(2):
                units = []
                for r in range(8 * g, 8 * g + 8, 2):
                    parts = [(0, 64, q16[:, r, :], k16[:, r, :]), (64, 64, q16[:, r + 1, :], k16[:, r + 1, :])]
                    vals = [(v16[:, vslot, r + j, vcol], 64, 0, slice(64 * j, 64 * j + 64)) for j in range(2)]
                    units.append((parts, 64, T["B2"][:, h, :], vals))
                groups.append((h, 2, units, (lambda a, g=g: a.rearrange("p (j r) -> p r j", r=16)[:, 8 * g:8 * g + 8, :]),
                               lambda a: a.rearrange("p (r j) -> p r j", j=64)))
        NG = len(groups)
        PER_PAIR = 12

        def sbank(g, u):
            return ps[:, 2 * (g % 2) + u // 2, (u % 2) * 2 * P:(u % 2) * 2 * P + 2 * P]

        with nc.Block() as block:
            @block.sync
            def _(sp):
                if dil:
                    rows = vb_dram.rearrange("(i p) n -> p i n", p=P)
                    rows4 = vb_dram.rearrange("(n j r) c -> j r n c", r=4, n=2)
                    rows16 = vb_dram.rearrange("(j r) c -> j r c", r=16)
                    for pair in range(B_HEADS // 2):
                        if pair >= 2:
                            sp.wait_ge(o_made, PER_PAIR * (pair - 1))
                        c = slice(pair * P, (pair + 1) * P)
                        s = pair % 2
                        sp.dma_start(v1[:, s, :, :], rows[:, :, c]).then_inc(v_loaded[s], 16)
                        for n in range(2):
                            sp.dma_start(v4[:, s, :, n, :], rows4[:, :, n, c]).then_inc(v_loaded[s], 16)
                        sp.dma_start(v16[:, s, :, :], rows16[:, :, c]).then_inc(v_loaded[s], 16)
                else:
                    sp.dma_start(sk[:, :], sinks.partition_broadcast(P)).then_inc(sk_loaded, 16)

            @block.tensor
            def _(pe):
                def scores(g):
                    if g >= 2:
                        pe.wait_ge(s_taken, g - 1)
                    for u, (parts, nk, bias, vals) in enumerate(groups[g][2]):
                        for off, nq, q, k in parts:
                            mm = pe.matmul(sbank(g, u)[off:off + nq, 0:nk], q, k, start=True, stop=True, skip_group_check=True)
                    mm.then_inc(s_made, 1)

                def turn(g):
                    pe.wait_ge(n_ready, g + 1)
                    if g >= 1:
                        pe.wait_ge(pt_act, g)
                        pe.wait_ge(pt_dve, g)
                    for u, (parts, nk, bias, vals) in enumerate(groups[g][2]):
                        for b in range((nk + P - 1) // P):
                            w = min(P, nk - b * P)
                            mm = pe.transpose(ps[0:w, 4 + u // 2, (u % 2) * 2 * P + b * P:(u % 2) * 2 * P + (b + 1) * P],
                                              s_sb[:, g % 2, u, b * P:b * P + w], ident[:, :])
                    mm.then_inc(turned, 1)

                def values(g):
                    h = groups[g][0]
                    pe.wait_ge(pt_act, g + 1)
                    pe.wait_ge(pt_dve, g + 1)
                    if dil:
                        pair = h // 2
                        pe.wait_ge(v_loaded[pair % 2], 64 * (pair // 2 + 1))
                    if g >= 1:
                        pe.wait_ge(o_out, g)
                    orow = slice((h % 2) * HD, (h % 2 + 1) * HD)
                    for u, (parts, nk, bias, vals) in enumerate(groups[g][2]):
                        for n, (v, rows, off, cols) in enumerate(vals):
                            one = len(parts) == 2
                            mm = pe.matmul(ps[orow, 6, u * P + cols.start:u * P + cols.stop], v, pT[0:rows, g % 2, u, off + cols.start:off + cols.stop],
                                           start=(one or n == 0), stop=(one or n == len(vals) - 1), skip_group_check=True)
                    if dil:
                        for u in range(GU):
                            mm = pe.matmul(ps[orow, 7, u * P:(u + 1) * P], lse[:, g % 2, u:u + 1].to_broadcast([P, HD]), ident[:, :],
                                           start=True, stop=True, skip_group_check=True)
                    mm.then_inc(o_made, 1)

                scores(0)
                if NG > 1:
                    scores(1)
                for g in range(NG):
                    if g + 2 < NG:
                        scores(g + 2)
                    if g >= 1:
                        values(g - 1)
                    turn(g)
                values(NG - 1)

            @block.scalar
            def _(act):
                def probabilities(g):
                    act.wait_ge(m_ready, g + 1)
                    for u, (parts, nk, bias, vals) in enumerate(groups[g][2]):
                        i = act.activation(s_sb[:, g % 2, u, 0:nk], s_sb[:, g % 2, u, 0:nk], ACT.Exp, bias=nm[:, g % 2, u:u + 1],
                                           accum_out=rsum[:, g % 2, u:u + 1])
                        if u == GU - 1 and dil:
                            i.then_inc(p_ready, 1)
                    if not dil:
                        h = groups[g][0]
                        act.activation(es[:, g % 2, :], nm[:, g % 2, :], ACT.Exp, bias=sk[:, h:h + 1]).then_inc(p_ready, 1)

                def take_turned(g):
                    act.wait_ge(turned, g + 1)
                    if g >= 2:
                        act.wait_ge(o_made, g - 1)
                    act_copy(g)

                def act_copy(g):
                    units = groups[g][2]
                    for u in range(2):
                        nk = units[u][1]
                        rows = min(nk, P)
                        w = max(nk, P)
                        i = act.activation(pT[0:rows, g % 2, u, 0:w], ps[0:rows, 4, u * 2 * P:u * 2 * P + w], ACT.Copy)
                    i.then_inc(pt_act, 1)

                def log_denominators(g):
                    act.wait_ge(n_ready, g + 1)
                    if g >= 2:
                        act.wait_ge(o_made, g - 1)
                    act.activation(lse[:, g % 2, :], den[:, g % 2, :], ACT.Ln).then_inc(ln_ready, 1)

                if not dil:
                    act.wait_ge(sk_loaded, 16)
                probabilities(0)
                for g in range(NG):
                    if g >= 1:
                        take_turned(g - 1)
                    if dil and g % PER_PAIR == 1 and g > PER_PAIR:
                        act.wait_ge(exp_in, g // PER_PAIR)
                        act.activation(lb[:, :, :], lb[:, :, :], ACT.Exp).then_inc(exp_out, 1)
                    if g + 1 < NG:
                        probabilities(g + 1)
                    if dil:
                        log_denominators(g)
                take_turned(NG - 1)
                if dil:
                    act.wait_ge(exp_in, NG // PER_PAIR)
                    act.activation(lb[:, :, :], lb[:, :, :], ACT.Exp).then_inc(exp_out, 1)

            @block.vector
            def _(dve):
                link = Chain(dve, chain)

                def maxima(g):
                    dve.wait_ge(s_made, g + 1)
                    if g >= 2:
                        dve.wait_ge(turned, g - 1)
                    h = groups[g][0]
                    for u, (parts, nk, bias, vals) in enumerate(groups[g][2]):
                        i = dve.tensor_tensor_reduce(s_sb[:, g % 2, u, 0:nk], sbank(g, u)[:, 0:nk], bias, SC_AB, NEG, ALU.add, ALU.max,
                                                     mx[:, g % 2, u:u + 1])
                    i.then_inc(s_taken, 1)
                    dve.wait_ge(s_taken, g + 1)
                    if dil:
                        dve.tensor_scalar(nm[:, g % 2, :], mx[:, g % 2, :], -1.0, None, ALU.mult).then_inc(m_ready, 1)
                    else:
                        dve.tensor_scalar(nm[:, g % 2, :], mx[:, g % 2, :], sk[:, h:h + 1], -1.0, ALU.max, ALU.mult).then_inc(m_ready, 1)

                def normalise(g):
                    dve.wait_ge(p_ready, g + 1)
                    if dil:
                        if g >= 2:
                            dve.wait_ge(ln_ready, g - 1)
                        link(dve.tensor_copy(den[:, g % 2, :], rsum[:, g % 2, :]))
                    else:
                        link(dve.tensor_tensor(den[:, g % 2, :], rsum[:, g % 2, :], es[:, g % 2, :], ALU.add))
                    link(dve.reciprocal(rden[:, g % 2, :], den[:, g % 2, :]))
                    for u, (parts, nk, bias, vals) in enumerate(groups[g][2]):
                        i = dve.tensor_scalar(s_sb[:, g % 2, u, 0:nk], s_sb[:, g % 2, u, 0:nk], rden[:, g % 2, u:u + 1], None, ALU.mult)
                    i.then_inc(n_ready, 1)

                def take_turned(g):
                    dve.wait_ge(turned, g + 1)
                    if g >= 2:
                        dve.wait_ge(o_made, g - 1)
                    if dil:
                        dve.wait_ge(ln_ready, g + 1)
                        link(dve.tensor_tensor(lse[:, g % 2, :], lse[:, g % 2, :], nm[:, g % 2, :], ALU.subtract))
                    units = groups[g][2]
                    for u in range(2, 4):
                        nk = units[u][1]
                        rows = min(nk, P)
                        w = max(nk, P)
                        i = dve.tensor_copy(pT[0:rows, g % 2, u, 0:w], ps[0:rows, 5, (u - 2) * 2 * P:(u - 2) * 2 * P + w])
                    i.then_inc(pt_dve, 1)

                def take_out(g):
                    h, c, units, dst, view = groups[g]
                    dve.wait_ge(o_made, g + 1)
                    orow = slice((h % 2) * HD, (h % 2 + 1) * HD)
                    if not dil:
                        dve.tensor_copy(dst, ps[orow, 6, :]).then_inc(o_out, 1)
                        return
                    link(dve.tensor_copy(dst(oc[orow, c, :]), view(ps[orow, 6, :])))
                    dve.tensor_copy(dst(lb[orow, c, :]), view(ps[orow, 7, :])).then_inc(o_out, 1)
                    if g % PER_PAIR == PER_PAIR - 1:
                        mix(g // PER_PAIR)

                def mix(pair):
                    dve.wait_ge(o_out, PER_PAIR * (pair + 1))
                    o = oT[:, A_WIDTH // P + pair, :]
                    link(dve.tensor_tensor(o, lb[:, 0, :], lb[:, 1, :], ALU.max))
                    link(dve.tensor_tensor(o, o, lb[:, 2, :], ALU.max))
                    dve.tensor_tensor(lb[:, :, :], lb[:, :, :], o.rearrange("p (a n) -> p a n", a=1).to_broadcast([P, 3, S]), ALU.subtract).then_inc(exp_in, 1)

                def mix2(pair):
                    o = oT[:, A_WIDTH // P + pair, :]
                    dve.wait_ge(exp_out, pair + 1)
                    link(dve.tensor_tensor(oc[:, :, :], oc[:, :, :], lb[:, :, :], ALU.mult))
                    link(dve.tensor_tensor(oc[:, 0, :], oc[:, 0, :], oc[:, 1, :], ALU.add))
                    link(dve.tensor_tensor(oc[:, 0, :], oc[:, 0, :], oc[:, 2, :], ALU.add))
                    link(dve.tensor_tensor(lb[:, 0, :], lb[:, 0, :], lb[:, 1, :], ALU.add))
                    link(dve.tensor_tensor(lb[:, 0, :], lb[:, 0, :], lb[:, 2, :], ALU.add))
                    link(dve.reciprocal(lb[:, 0, :], lb[:, 0, :]))
                    link(dve.tensor_tensor(o, oc[:, 0, :], lb[:, 0, :], ALU.mult))

                if not dil:
                    dve.wait_ge(sk_loaded, 16)
                maxima(0)
                for g in range(NG):
                    if g >= 1:
                        take_turned(g - 1)
                    if g + 1 < NG:
                        maxima(g + 1)
                    normalise(g)
                    if dil and g % PER_PAIR == 1 and g > PER_PAIR:
                        mix2(g // PER_PAIR - 1)
                    if g >= 1:
                        take_out(g - 1)
                take_turned(NG - 1)
                take_out(NG - 1)
                if dil:
                    mix2(NG // PER_PAIR - 1)


def gate_output(nc, K, oT, w_in, col, tag, x_dram, fill=False):
    hT, ps = K["hT"], K["ps"]
    with ExitStack() as ctx:
        sc = Scope(nc, ctx, tag)
        w = sc.sb("w", [P, 3, KT, P])
        sg = sc.sb("sg", [P, 2, HALF])
        loaded = [sc.sem(f"w{i}") for i in range(3)]
        x_loaded, done, sig, out_sem = sc.sem("x_loaded"), sc.sem("done"), sc.sem("sig"), sc.sem("out")
        with nc.Block() as block:
            @block.sync
            def _(sp):
                for j in range(KT):
                    if j >= 3:
                        sp.wait_ge(done, 2 * (j - 2))
                    sp.dma_start(w[:, j % 3, :, :], tiled_rows(w_in[:, col + j * P:col + (j + 1) * P])).then_inc(loaded[j % 3], 16)
                for t in range(NT):
                    rows, tile = x_dram[t * P:(t + 1) * P, :], K["X"][:, t, :]
                    sp.dma_start(rows if fill else tile, tile if fill else rows).then_inc(x_loaded, 16)
                sp.wait_ge(x_loaded, 16 * NT)

            @block.tensor
            def _(pe):
                for j in range(KT):
                    pe.wait_ge(loaded[j % 3], 16 * (j // 3 + 1))
                    for half in range(NH):
                        u = 2 * j + half
                        if u >= 8:
                            pe.wait_ge(sig, u - 7)
                        for k in range(KT):
                            mm = pe.matmul(ps[:, u % 8, :], w[:, j % 3, k, :], hT[:, k, half * HALF:(half + 1) * HALF], start=(k == 0), stop=(k == KT - 1))
                        mm.then_inc(done, 1)

            @block.scalar
            def _(act):
                for u in range(2 * KT):
                    act.wait_ge(done, u + 1)
                    if fill:
                        act.activation(oT[:, u // 2, (u % 2) * HALF:(u % 2 + 1) * HALF], ps[:, u % 8, :], ACT.Silu).then_inc(sig, 1)
                        continue
                    if u >= 2:
                        act.wait_ge(out_sem, u - 1)
                    act.activation(sg[:, u % 2, :], ps[:, u % 8, :], ACT.Silu).then_inc(sig, 1)

            @block.vector
            def _(dve):
                for u in range(0 if fill else 2 * KT):
                    j, half = u // 2, u % 2
                    dve.wait_ge(sig, u + 1)
                    dst = oT[:, j, half * HALF:(half + 1) * HALF]
                    dve.tensor_tensor(dst, dst, sg[:, u % 2, :], ALU.mult).then_inc(out_sem, 1)


def latents(nc, K, C, w_in, q_norm, kv_norm, positions, inv_freq):
    hT, ps, ident = K["hT"], K["ps"], K["ident"]
    with ExitStack() as ctx:
        sc = Scope(nc, ctx, "lat")
        w = sc.sb("w", [P, KT, C_LAT])
        ck = sc.sb("ck", [P, NT, C_LAT])
        sq = sc.sb("sq", [P, C_QR])
        kp = sc.sb("kp", [P, NT, C_QK])
        gq, gkv = sc.sb("gq", [P, QR_T]), sc.sb("gkv", [P, 1])
        ss, var, std, rs = [sc.sb(n, [P, 2, NT]) for n in ("ss", "var", "std", "rs")]
        pos_i, pos = sc.sb("pos_i", [P, NT], I32), sc.sb("pos", [P, NT])
        fr = sc.sb("fr", [P, ROPE_HALF])
        ang, turns, red, mag = [sc.sb(n, [P, NT, ROPE_HALF]) for n in ("ang", "turns", "red", "mag")]
        ra, rb = [sc.sb(n, [P, NT, ROPE_HALF]) for n in ("ra", "rb")]
        loaded, made, copied, summed, var_ready, std_ready, ang_ready, tables, scaled, roped, turned, chain, out_act, out_dve = [sc.sem(n) for n in
            ("loaded", "made", "copied", "summed", "var_ready", "std_ready", "ang_ready", "tables", "scaled", "roped", "turned", "chain", "out_act", "out_dve")]
        cs, sn = C["cos"], C["sin"]
        n_loads = 5 + KT
        with nc.Block() as block:
            @block.sync
            def _(sp):
                sp.dma_start(pos_i[:, :], positions.rearrange("(t p) -> p t", p=P)).then_inc(loaded, 16)
                sp.dma_start(fr[:, :], inv_freq.partition_broadcast(P)).then_inc(loaded, 16)
                sp.dma_start(gq[:, :], q_norm.rearrange("(k p) -> p k", p=P)).then_inc(loaded, 16)
                sp.dma_start(gkv[:, :], kv_norm.rearrange("(k p) -> p k", p=P)).then_inc(loaded, 16)
                sp.dma_start(C["wkv"][:, :], C["w_kvb"]).then_inc(loaded, 16)
                for k in range(KT):
                    sp.dma_start(w[:, k, :], w_in[k * P:(k + 1) * P, 0:C_LAT]).then_inc(loaded, 16)

            @block.tensor
            def _(pe):
                pe.wait_ge(loaded, 16 * n_loads)
                for t in range(NT):
                    for k in range(KT):
                        mm = pe.matmul(ps[:, t, 0:C_LAT], hT[:, k, t * P:(t + 1) * P], w[:, k, :], start=(k == 0), stop=(k == KT - 1))
                    mm.then_inc(made, 1)
                pe.wait_ge(copied, NT)
                pe.wait_ge(roped, 1)
                for t in range(NT):
                    pe.wait_ge(scaled, 2 * t + 2)
                    for j in range(3):
                        pe.transpose(ps[:, t, j * P:(j + 1) * P], ck[:, t, j * P:(j + 1) * P], ident[:, :])
                    pe.transpose(ps[0:C_QK, t, 3 * P:4 * P], kp[:, t, :], ident[:, :]).then_inc(turned, 1)

            @block.scalar
            def _(act):
                act.wait_ge(ang_ready, 1)
                act.activation(sn[:, :, :], red[:, :, :], ACT.Sin).then_inc(tables, 1)
                act.activation(cs[:, :, :], mag[:, :, :], ACT.Sin).then_inc(tables, 1)
                for t in range(NT):
                    act.wait_ge(made, t + 1)
                    act.activation(ck[:, t, :], ps[:, t, 0:C_LAT], ACT.Copy).then_inc(copied, 1)
                    act.wait_ge(copied, t + 1)
                    if t:
                        act.wait_ge(summed, 2 * t)
                    act.activation(sq[:, :], ck[:, t, 0:C_QR], ACT.Square, accum_out=ss[:, 0, t:t + 1]).then_inc(summed, 1)
                    act.wait_ge(summed, 2 * t + 1)
                    act.activation(sq[:, 0:C_KVR], ck[:, t, C_QR:C_QR + C_KVR], ACT.Square, accum_out=ss[:, 1, t:t + 1]).then_inc(summed, 1)
                act.wait_ge(var_ready, 1)
                act.activation(std[:, :, :], var[:, :, :], ACT.Sqrt).then_inc(std_ready, 1)
                for t in range(NT):
                    act.wait_ge(turned, t + 1)
                    for j in range(2):
                        act.activation(C["cqT"][:, j, t * P:(t + 1) * P], ps[:, t, j * P:(j + 1) * P], ACT.Copy, scale=gq[:, j:j + 1]).then_inc(out_act, 1)

            @block.vector
            def _(dve):
                link = Chain(dve, chain)
                dve.memset(kp[:, :, 0:C_NOPE], 0.0).then_inc(chain, 1)
                link.n = 1
                dve.wait_ge(loaded, 16 * n_loads)
                link(dve.tensor_copy(pos[:, :], pos_i[:, :]))
                link(dve.tensor_tensor(ang[:, :, :], pos[:, :].rearrange("p (t a) -> p t a", a=1).to_broadcast([P, NT, ROPE_HALF]),
                                       fr[:, :].rearrange("p (a f) -> p a f", a=1).to_broadcast([P, NT, ROPE_HALF]), ALU.mult))
                link(dve.tensor_scalar(turns[:, :, :], ang[:, :, :], 1.0 / TWO_PI, None, ALU.mult))
                link(dve.tensor_scalar(turns[:, :, :], turns[:, :, :], ROUND, None, ALU.add))
                link(dve.tensor_scalar(turns[:, :, :], turns[:, :, :], ROUND, None, ALU.subtract))
                link(dve.scalar_tensor_tensor(out=red[:, :, :], in0=turns[:, :, :], scalar=-TWO_PI_1, in1=ang[:, :, :], op0=ALU.mult, op1=ALU.add))
                link(dve.scalar_tensor_tensor(out=red[:, :, :], in0=turns[:, :, :], scalar=-TWO_PI_2, in1=red[:, :, :], op0=ALU.mult, op1=ALU.add))
                link(dve.scalar_tensor_tensor(out=red[:, :, :], in0=turns[:, :, :], scalar=-TWO_PI_3, in1=red[:, :, :], op0=ALU.mult, op1=ALU.add))
                link(dve.tensor_scalar(red[:, :, :], red[:, :, :], PI_BELOW, -PI_BELOW, ALU.min, ALU.max))
                link(dve.scalar_tensor_tensor(out=mag[:, :, :], in0=red[:, :, :], scalar=-1.0, in1=red[:, :, :], op0=ALU.mult, op1=ALU.max))
                dve.tensor_scalar(mag[:, :, :], mag[:, :, :], -1.0, math.pi / 2, ALU.mult, ALU.add).then_inc(ang_ready, 1)
                dve.wait_ge(copied, NT)
                dve.wait_ge(tables, 2)
                t1, t2 = ck[:, :, C_QR + C_KVR:C_QR + C_KVR + ROPE_HALF], ck[:, :, C_QR + C_KVR + ROPE_HALF:C_LAT]
                link(dve.tensor_tensor(ra[:, :, :], t1, cs[:, :, :], ALU.mult))
                link(dve.tensor_tensor(rb[:, :, :], t2, sn[:, :, :], ALU.mult))
                link(dve.tensor_tensor(kp[:, :, C_NOPE:C_NOPE + ROPE_HALF], ra[:, :, :], rb[:, :, :], ALU.subtract))
                link(dve.tensor_tensor(ra[:, :, :], t1, sn[:, :, :], ALU.mult))
                link(dve.tensor_tensor(rb[:, :, :], t2, cs[:, :, :], ALU.mult))
                dve.tensor_tensor(kp[:, :, C_NOPE + ROPE_HALF:C_QK], ra[:, :, :], rb[:, :, :], ALU.add).then_inc(roped, 1)
                dve.wait_ge(summed, 2 * NT)
                link(dve.tensor_scalar(var[:, 0, :], ss[:, 0, :], 1.0 / C_QR, EPS, ALU.mult, ALU.add))
                dve.tensor_scalar(var[:, 1, :], ss[:, 1, :], 1.0 / C_KVR, EPS, ALU.mult, ALU.add).then_inc(var_ready, 1)
                dve.wait_ge(std_ready, 1)
                link(dve.reciprocal(rs[:, :, :], std[:, :, :]))
                for t in range(NT):
                    dve.tensor_scalar(ck[:, t, 0:C_QR], ck[:, t, 0:C_QR], rs[:, 0, t:t + 1], None, ALU.mult).then_inc(scaled, 1)
                    dve.tensor_scalar(ck[:, t, C_QR:C_QR + C_KVR], ck[:, t, C_QR:C_QR + C_KVR], rs[:, 1, t:t + 1], None, ALU.mult).then_inc(scaled, 1)
                for t in range(NT):
                    dve.wait_ge(turned, t + 1)
                    dve.wait_ge(out_act, 2 * (t + 1))
                    cols = slice(t * P, (t + 1) * P)
                    dve.tensor_scalar(C["ckvT"][:, cols], ps[:, t, 2 * P:3 * P], gkv[:, 0:1], None, ALU.mult).then_inc(out_dve, 1)
                    for slot in range(2):
                        dve.tensor_copy(C["kT"][C_NOPE:C_QK, slot, cols], ps[C_NOPE:C_QK, t, 3 * P:4 * P]).then_inc(out_dve, 1)


def latent_queries(nc, K, C, w_qb):
    ps, ident = K["ps"], K["ident"]
    W = C_HEADS * C_QK
    with ExitStack() as ctx:
        sc = Scope(nc, ctx, "lq")
        wq = sc.sb("wq", [P, QR_T, W])
        qt = sc.sb("qt", [P, 2, C_HEADS, C_QK])
        ra, rb, rc = [sc.sb(n, [P, C_HEADS, ROPE_HALF]) for n in ("ra", "rb", "rc")]
        loaded, q_made, q_out, v_made, v_out, roped, turned, out_act, out_dve, chain = [sc.sem(n) for n in
            ("loaded", "q_made", "q_out", "v_made", "v_out", "roped", "turned", "out_act", "out_dve", "chain")]
        with nc.Block() as block:
            @block.sync
            def _(sp):
                sp.dma_start(wq[:, :, :], tiled_rows(w_qb)).then_inc(loaded, 16)

            @block.tensor
            def _(pe):
                def turn(t):
                    pe.wait_ge(roped, t + 1)
                    for b in range(2):
                        for n in range(2):
                            u = 2 * t + b
                            if n == 0 and u:
                                pe.wait_ge(out_act, u)
                                pe.wait_ge(out_dve, u)
                            for j in range(4):
                                mm = pe.transpose(ps[0:C_QK, 6 + n, j * P:(j + 1) * P], qt[:, t % 2, 8 * b + 4 * n + j, :], ident[:, :])
                        mm.then_inc(turned, 1)

                pe.wait_ge(loaded, 16)
                wv = C["wkv"][:, :].rearrange("p (h x) -> p h x", x=C_NOPE + C_V)
                for t in range(NT):
                    cols = slice(t * P, (t + 1) * P)
                    if t:
                        pe.wait_ge(q_out, t)
                    for n in range(3):
                        for k in range(QR_T):
                            mm = pe.matmul(ps[:, n, :], C["cqT"][:, k, cols], wq[:, k, n * HALF:(n + 1) * HALF], start=(k == 0), stop=(k == QR_T - 1))
                    mm.then_inc(q_made, 1)
                    if t:
                        pe.wait_ge(v_out, t)
                    for n in range(2):
                        mm = pe.matmul(ps[:, 4 + n, :], C["ckvT"][:, cols], wv[:, 8 * n:8 * n + 8, C_NOPE:], start=True, stop=True)
                    mm.then_inc(v_made, 1)
                    if t:
                        turn(t - 1)
                turn(NT - 1)

            def out(act, t):
                for b in range(2):
                    act.wait_ge(turned, 2 * t + b + 1)
                    dst = C["qT"](8 * b)
                    act.activation(dst[0:C_QK, 0:4, t * P:(t + 1) * P], ps[0:C_QK, 6, :].rearrange("p (h t) -> p h t", t=P), ACT.Copy).then_inc(out_act, 1)

            @block.scalar
            def _(act):
                for t in range(NT):
                    act.wait_ge(q_made, t + 1)
                    if t >= 2:
                        act.wait_ge(turned, 2 * (t - 1))
                    flat = qt[:, t % 2, :, :].rearrange("p h x -> p (h x)")
                    for n in range(3):
                        i = act.activation(flat[:, n * HALF:(n + 1) * HALF], ps[:, n, :], ACT.Copy)
                    i.then_inc(q_out, 1)
                    act.wait_ge(v_made, t + 1)
                    for n in range(2):
                        i = act.activation(C["v"][:, t, n * HALF:(n + 1) * HALF], ps[:, 4 + n, :], ACT.Copy)
                    i.then_inc(v_out, 1)
                    if t:
                        out(act, t - 1)
                out(act, NT - 1)

            @block.vector
            def _(dve):
                link = Chain(dve, chain)

                def outd(t):
                    for b in range(2):
                        dve.wait_ge(turned, 2 * t + b + 1)
                        dst = C["qT"](8 * b)
                        dve.tensor_copy(dst[0:C_QK, 4:8, t * P:(t + 1) * P], ps[0:C_QK, 7, :].rearrange("p (h t) -> p h t", t=P)).then_inc(out_dve, 1)

                for t in range(NT):
                    dve.wait_ge(q_out, t + 1)
                    t1, t2 = qt[:, t % 2, :, C_NOPE:C_NOPE + ROPE_HALF], qt[:, t % 2, :, C_NOPE + ROPE_HALF:]
                    cs = C["cos"][:, t:t + 1, :].to_broadcast([P, C_HEADS, ROPE_HALF])
                    sn = C["sin"][:, t:t + 1, :].to_broadcast([P, C_HEADS, ROPE_HALF])
                    link(dve.tensor_tensor(ra[:, :, :], t2, sn, ALU.mult))
                    link(dve.tensor_tensor(rb[:, :, :], t1, sn, ALU.mult))
                    link(dve.tensor_tensor(rc[:, :, :], t2, cs, ALU.mult))
                    link(dve.tensor_tensor(t1, t1, cs, ALU.mult))
                    link(dve.tensor_tensor(t1, t1, ra[:, :, :], ALU.subtract))
                    dve.tensor_tensor(t2, rb[:, :, :], rc[:, :, :], ALU.add).then_inc(roped, 1)
                    if t:
                        outd(t - 1)
                outd(NT - 1)


def latent_attention(nc, K, C, oT):
    ps, ident = K["ps"], K["ident"]
    NU = C_HEADS * NT
    with ExitStack() as ctx:
        sc = Scope(nc, ctx, "lattn")
        s_sb = sc.sb("s", [P, 2, S])
        pT = [sc.sb("pT0", [P, 4, HALF]), sc.sb("pT1", [P, 8, HALF])]
        mx, nm, den, rden = [sc.sb(n, [P, 2]) for n in ("mx", "nm", "den", "rden")]
        s_made, s_masked, m_ready, p_ready, n_ready, turned, pt_out, o_made, o_out, k_made, k_out, chain = [sc.sem(n) for n in
            ("s_made", "s_masked", "m_ready", "p_ready", "n_ready", "turned", "pt_out", "o_made", "o_out", "k_made", "k_out", "chain")]

        with nc.Block() as block:
            @block.tensor
            def _(pe):
                def keys(h):
                    for half in range(NH):
                        if 2 * h + half:
                            pe.wait_ge(k_out, 2 * h + half)
                        pe.matmul(ps[0:C_NOPE, 7, :], C["wkv"][:, h * (C_NOPE + C_V):h * (C_NOPE + C_V) + C_NOPE],
                                  C["ckvT"][:, half * HALF:(half + 1) * HALF], start=True, stop=True).then_inc(k_made, 1)

                def scores(u):
                    h, i = u // NT, u % NT
                    if i == 0:
                        pe.wait_ge(k_out, 2 * h + 2)
                    if u >= 2:
                        pe.wait_ge(p_ready, u - 1)
                    q = C["qT"](h)[0:C_QK, 0, i * P:(i + 1) * P]
                    w = (i + 1) * P
                    for n in range((w + HALF - 1) // HALF):
                        c1 = min(w, (n + 1) * HALF)
                        mm = pe.matmul(ps[:, 2 * (u % 2) + n, 0:c1 - n * HALF], q, C["kT"][0:C_QK, h % 2, n * HALF:c1], start=True, stop=True)
                    mm.then_inc(s_made, 1)

                def turn(u):
                    i = u % NT
                    pe.wait_ge(n_ready, u + 1)
                    if u:
                        pe.wait_ge(pt_out, u)
                    for b in range(i + 1):
                        mm = pe.transpose(ps[:, 4 + b // 4, (b % 4) * P:(b % 4 + 1) * P], s_sb[:, u % 2, b * P:(b + 1) * P], ident[:, :])
                    mm.then_inc(turned, 1)

                def values(g):
                    h, half = g // 2, g % 2
                    pe.wait_ge(pt_out, 4 * (g + 1))
                    if g:
                        pe.wait_ge(o_out, g)
                    orow = slice((h % 2) * C_V, (h % 2 + 1) * C_V)
                    nb = 4 * (half + 1)
                    for b in range(nb):
                        q0 = max(0, b * P - half * HALF)
                        mm = pe.matmul(ps[orow, 6, q0:HALF], C["v"][:, b, h * C_V:(h + 1) * C_V], pT[half][:, b, q0:HALF],
                                       start=(b == 0), stop=(b == nb - 1), skip_group_check=True)
                    mm.then_inc(o_made, 1)

                keys(0)
                scores(0)
                scores(1)
                for u in range(NU):
                    h, i = u // NT, u % NT
                    if i == 3 and h + 1 < C_HEADS:
                        keys(h + 1)
                    if u + 2 < NU:
                        scores(u + 2)
                    turn(u)
                    if u % 4 == 0 and u:
                        values(u // 4 - 1)
                values(NU // 4 - 1)

            @block.scalar
            def _(act):
                def keys_out(h):
                    for half in range(NH):
                        act.wait_ge(k_made, 2 * h + half + 1)
                        act.activation(C["kT"][0:C_NOPE, h % 2, half * HALF:(half + 1) * HALF], ps[0:C_NOPE, 7, :], ACT.Copy).then_inc(k_out, 1)

                def probabilities(u):
                    w = (u % NT + 1) * P
                    act.wait_ge(m_ready, u + 1)
                    src = ps[:, 2 * (u % 2):2 * (u % 2) + 2, :].rearrange("p a n -> p (a n)")
                    act.activation(s_sb[:, u % 2, 0:w], src[:, 0:w], ACT.Exp, scale=C_SCALE, bias=nm[:, u % 2:u % 2 + 1],
                                   accum_out=den[:, u % 2:u % 2 + 1]).then_inc(p_ready, 1)

                keys_out(0)
                probabilities(0)
                for u in range(NU):
                    h, i = u // NT, u % NT
                    if i == 3 and h + 1 < C_HEADS:
                        keys_out(h + 1)
                    if u + 1 < NU:
                        if u >= 1:
                            act.wait_ge(turned, u)
                        probabilities(u + 1)
                    act.wait_ge(turned, u + 1)
                    half = i // 4
                    if i % 4 == 0:
                        g = u // 4
                        if g >= 2:
                            act.wait_ge(o_made, g - 1)
                    n = i + 1
                    src = ps[:, 4:6, :].rearrange("p a (b t) -> p (a b) t", t=P)
                    act.activation(pT[half][:, 0:n, (i % 4) * P:(i % 4 + 1) * P], src[:, 0:n, :], ACT.Copy).then_inc(pt_out, 1)

            @block.vector
            def _(dve):
                link = Chain(dve, chain)

                def maxima(u):
                    i = u % NT
                    w = (i + 1) * P
                    dve.wait_ge(s_made, u + 1)
                    src = ps[:, 2 * (u % 2):2 * (u % 2) + 2, :].rearrange("p a n -> p (a n)")
                    diag = src[:, i * P:w]
                    link(dve.tensor_tensor(diag, diag, K["neg_after"][:, :], ALU.add))
                    link(dve.tensor_reduce(mx[:, u % 2:u % 2 + 1], src[:, 0:w], AX.X, ALU.max))
                    dve.tensor_scalar(nm[:, u % 2:u % 2 + 1], mx[:, u % 2:u % 2 + 1], -C_SCALE, None, ALU.mult).then_inc(m_ready, 1)

                def normalise(u):
                    w = (u % NT + 1) * P
                    dve.wait_ge(p_ready, u + 1)
                    link(dve.reciprocal(rden[:, u % 2:u % 2 + 1], den[:, u % 2:u % 2 + 1]))
                    dve.tensor_scalar(s_sb[:, u % 2, 0:w], s_sb[:, u % 2, 0:w], rden[:, u % 2:u % 2 + 1], None, ALU.mult).then_inc(n_ready, 1)

                def take_out(g):
                    h, half = g // 2, g % 2
                    dve.wait_ge(o_made, g + 1)
                    orow = slice((h % 2) * C_V, (h % 2 + 1) * C_V)
                    dst = oT[orow, h // 2, half * HALF:(half + 1) * HALF]
                    dve.tensor_tensor(dst, dst, ps[orow, 6, :], ALU.mult).then_inc(o_out, 1)

                maxima(0)
                for u in range(NU):
                    if u + 1 < NU:
                        maxima(u + 1)
                    normalise(u)
                    if u % 4 == 1 and u > 4:
                        take_out(u // 4 - 1)
                take_out(NU // 4 - 1)


def build(nc, A, out, invcnt, onehot, inv_freq, dump=None, stop=None):
    with ExitStack() as ctx:
        def sb(name, shape, dt=F32):
            return ctx.enter_context(nc.sbuf_tensor(name, shape, dt))

        ctx.enter_context(nc.allow_non_contiguous_dma(reason="gains and taps of one element a partition"))
        K = {
            "X": sb("X", [P, NT, D]), "hT": sb("hT", [P, KT, S]), "ident": sb("ident", [P, P]), "ones": sb("ones", [P, P]),
            "neg_after": sb("neg_after", [P, P]), "neg_before": sb("neg_before", [P, P]), "earlier": sb("earlier", [P, P]),
            "sel_neg": sb("sel_neg", [HEADS, HEADS, P]), "sel_one": sb("sel_one", [HEADS, HEADS, P]),
            "ps": ctx.enter_context(nc.psum_tensor("ps", [P, 8, HALF], F32)),
        }
        dmp = dump or (lambda name, ap: None)
        y_dram = nc.dram_tensor("y_rows", [SLOTS_B * P, D], F32).ap()
        make_constants(nc, K, None)
        load_x(nc, K, A["x"][0])
        norm_transpose(nc, K, A["g_mix"][0], "n1")
        w_in = A["w_in"][0]
        with ExitStack() as mctx:
            def msb(name, shape, dt=F32):
                return mctx.enter_context(nc.sbuf_tensor("mix_" + name, shape, dt))
            M = {"yT": msb("yT", [P, 4, S]), "hmT": msb("hmT", [P, HEADS, S]), "ghead": msb("ghead", [P, HEADS]),
                 "g_head_dram": A["g_head"][0]}
            with ExitStack() as ictx:
                def isb(name, shape, dt=F32):
                    return ictx.enter_context(nc.sbuf_tensor("mixin_" + name, shape, dt))
                M.update({"qT": isb("qT", [P, HEADS, S]), "kT": isb("kT", [P, HEADS, S]), "og": isb("og", [P, HEADS, S]),
                          "v": isb("v", [P, NT, HEADS, DH + 1]), "U": isb("U", [HEADS, NC, P]),
                          "G": isb("G", [HEADS, NC, P]), "SP": isb("SP", [P, HEADS, NC])})
                M["R"] = K["X"][:, NT - 2, :]
                M["RT"] = K["X"][:, NT - 1, :].rearrange("p (c r) -> p c r", r=P)
                M["dT"] = M["hmT"]
                mixer_projections(nc, K, M, w_in, A["b_if"][0], A["conv_q"][0], A["conv_k"][0], A["w_pool"][0], A["pool_scale"][0], invcnt)
                dmp("qT", M["qT"][:, :, :]); dmp("kT", M["kT"][:, :, :]); dmp("v", M["v"][:, :, :, :]); dmp("yT", M["yT"][:, :, :]); dmp("og", M["og"][:, :, :]); dmp("RT", M["RT"][:, :, :]); dmp("SP", M["SP"][:, :, :]); dmp("G", M["G"][:, :, :])
                mlstm(nc, K, M)
                dmp("hmT", M["hmT"][:, :, :])
            with ExitStack() as octx:
                m = octx.enter_context(nc.sbuf_tensor("merged", [P, 2, KT, S], F32R))
                mixer_merge(nc, K, M, w_in, A["w_br_a"][0], A["w_br_b"][0], m, y_dram)
                project_add(nc, K, None, A["w_out"][0], "wout", x_dram=A["x"][0], halves=m)
        dmp("x1", K["X"][:, :, :])
        if stop == "x1":
            return
        with ExitStack() as ectx:
            def esb(name, shape, dt=F32):
                return ectx.enter_context(nc.sbuf_tensor("routed_" + name, shape, dt))
            h_dram = nc.dram_tensor("h_rows", [S, D], F32).ap()
            slot_tok = nc.dram_tensor("slot_tok", [SLOTS_B * P, 1], I32).ap()
            R = {"idx": esb("idx", [P, SLOTS_B], I32), "dest": esb("dest", [P, TOP_K, NT], I32), "gate": esb("gate", [P, TOP_K, NT]),
                 "block_e": esb("block_e", [1, SLOTS_B], I32), "n_blocks": esb("n_blocks", [1, 1], I32)}
            norm_transpose(nc, K, A["g_ffn"][0], "n2", h_dram)
            route(nc, K, R, A["w_rg"][0], A["b_rg"][0], A["w_re"][0], A["b_re"][0], slot_tok)
            for n in ("dest", "gate", "block_e", "n_blocks"):
                dmp(n, R[n][:, :, :] if n in ("dest", "gate") else R[n][:, :])
            experts(nc, K, R, h_dram, y_dram, A["w_e_gate"][0], A["w_e_up"][0], A["w_e_down"][0])
            combine(nc, K, R, y_dram)
        dmp("x2", K["X"][:, :, :])
        x3_dram = nc.dram_tensor("x3_rows", [S, D], F32).ap()
        norm_rows(nc, K, A["g_final"], "nf", x3_dram)
        dmp("x3", K["X"][:, :, :])
        norm_transpose(nc, K, A["norm_w_2"][0], "n3")
        with ExitStack() as actx:
            vb_dram = nc.dram_tensor("vb_rows", [S, B_WIDTH], F32).ap()
            G_dram = nc.dram_tensor("bias_strips", [A_HEADS + B_HEADS, len(DILATIONS), BAND], F32).ap()
            oT = actx.enter_context(nc.sbuf_tensor("ab_oT", [P, KT, S], F32))
            B = {"qb": K["X"][:, 0:4, :], "kb": K["X"][:, 4:8, :]}
            w_ab = A["ab_w_in_2"][0]
            with ExitStack() as a1:
                B["qa"] = a1.enter_context(nc.sbuf_tensor("ab_qa", [P, 4, S], F32))
                B["ka"] = a1.enter_context(nc.sbuf_tensor("ab_ka", [P, 1, S], F32))
                B["va"] = a1.enter_context(nc.sbuf_tensor("ab_va", [P, NT, P], F32))
                ab_projections(nc, K, B, w_ab, vb_dram)
                T = {"A": a1.enter_context(nc.sbuf_tensor("ab_biasA", [P, A_HEADS, 2 * P], F32))}
                bias_tables(nc, K, T, G_dram, A["rel_bias_2"], onehot, "A")
                dmp("biasA", T["A"][:, :, :])
                banded_attention(nc, K, B, T, oT, "A", None, A["ab_sinks_2"][0])
            with ExitStack() as a2:
                T = {"B0": a2.enter_context(nc.sbuf_tensor("ab_biasB0", [P, B_HEADS, 2 * P], F32)),
                     "B1": a2.enter_context(nc.sbuf_tensor("ab_biasB1", [P, B_HEADS, 2 * P], F32)),
                     "B2": a2.enter_context(nc.sbuf_tensor("ab_biasB2", [P, B_HEADS, 64], F32))}
                bias_tables(nc, K, T, G_dram, A["rel_bias_2"], onehot, "B")
                banded_attention(nc, K, B, T, oT, "B", vb_dram, None)
            dmp("oT", oT[:, :, :])
            gate_output(nc, K, oT, w_ab, COL_Z, "abz", x3_dram)
            project_add(nc, K, oT, A["ab_w_out_2"][0], "abo")
        dmp("x4", K["X"][:, :, :])
        norm_transpose(nc, K, A["norm_w_2"][1], "n4")
        with ExitStack() as cctx:
            def csb(name, shape, dt=F32):
                return cctx.enter_context(nc.sbuf_tensor("c_" + name, shape, dt))
            x4_dram = nc.dram_tensor("x4_rows", [S, D], F32).ap()
            w_c = A["c_w_in_2"][0]
            oT = csb("oT", [P, KT, S])
            gate_output(nc, K, oT, w_c, C_LAT, "cz", x4_dram, fill=True)
            with ExitStack() as qctx:
                def qsb(name, shape):
                    return qctx.enter_context(nc.sbuf_tensor("c_" + name, shape, F32))
                C = {"ckvT": qsb("ckvT", [P, S]), "kT": qsb("kT", [C_QK, 2, S]), "wkv": qsb("wkv", [P, C_HEADS * (C_NOPE + C_V)]),
                     "w_kvb": A["c_w_kvb_2"][0], "cos": qsb("cos", [P, NT, ROPE_HALF]), "sin": qsb("sin", [P, NT, ROPE_HALF]),
                     "v": K["X"]}
                more = qsb("q8", [P, 8, S])
                C["qT"] = lambda h: (K["hT"] if h < 8 else more)[:, h % 8:, :]
                with ExitStack() as lctx:
                    C["cqT"] = lctx.enter_context(nc.sbuf_tensor("c_cqT", [P, QR_T, S], F32))
                    latents(nc, K, C, w_c, A["c_q_norm_2"][0], A["c_kv_norm_2"][0], A["positions_2"][0], inv_freq)
                    latent_queries(nc, K, C, A["c_w_qb_2"][0])
                latent_attention(nc, K, C, oT)
            project_add(nc, K, oT, A["c_w_out_2"][0], "co", x4_dram)
        dmp("x5", K["X"][:, :, :])
        norm_rows(nc, K, A["final_norm_2"], "nout", out)


_INS = ["x", "g_mix", "w_in", "b_if", "conv_q", "conv_k", "g_head", "w_pool", "pool_scale", "w_br_a", "w_br_b", "w_out",
        "g_ffn", "w_rg", "b_rg", "w_re", "b_re", "w_e_gate", "w_e_up", "w_e_down", "g_final", "positions_2", "norm_w_2",
        "rel_bias_2", "ab_w_in_2", "ab_sinks_2", "ab_w_out_2", "c_w_in_2", "c_q_norm_2", "c_w_qb_2", "c_kv_norm_2",
        "c_w_kvb_2", "c_w_out_2", "final_norm_2"]


def kernel(**inputs):
    import numpy as _np
    import concourse.bacc as _bacc
    from concourse import mybir as _mybir
    from concourse.bass_utils import run_bass_kernel_spmd as _run

    nc = _bacc.Bacc("TRN2", target_bir_lowering=False, num_devices=1)
    arrays, aps = {}, {}

    def give(name, a):
        arrays[f"in_{name}_dram"] = a
        return nc.dram_tensor(f"in_{name}_dram", a.shape, _mybir.dt.from_np(a.dtype), kind="ExternalInput").ap()

    for name in _INS:
        aps[name] = give(name, _np.ascontiguousarray(inputs[name]))
    invcnt, onehot, inv_freq = [give(n, f()) for n, f in
                                (("window_reciprocals", window_reciprocals), ("bucket_onehot", bucket_onehot),
                                 ("inverse_frequencies", inverse_frequencies))]
    out = nc.dram_tensor("out_0_dram", (S, D), _mybir.dt.float32, kind="ExternalOutput").ap()
    build(nc, aps, out, invcnt, onehot, inv_freq)
    r = _run(nc, [arrays], core_ids=[0])
    return r.results[0]["out_0_dram"].reshape(1, S, D)
```

```python
import math
from contextlib import ExitStack

import numpy as np

import concourse.bass as bass
from concourse import mybir

ALU = mybir.AluOpType
ACT = mybir.ActivationFunctionType
AX = mybir.AxisListType
F32 = mybir.dt.float32
F32R = mybir.dt.float32r
I32 = mybir.dt.int32

P = 128
S = 1024
D = 1024
NT = S // P
KT = D // P
HALF = 512
NH = S // HALF
EPS = 1e-6

D_POOL = D // 2
D_ML = D // 2
HEADS = 4
DH = D_ML // HEADS
POOL_WINDOWS = (2, 4, 8, 16)
PAD = max(POOL_WINDOWS)
CONV_K = 4
COL_POOL = 0
COL_Q = D_POOL
COL_K = COL_Q + D_ML
COL_V = COL_K + D_ML
COL_O = COL_V + D_ML
COL_I = COL_O + D_ML
COL_GA = COL_I + 2 * HEADS
COL_GB = COL_GA + D
NC = S // P
NEG = -1.0e30

GROUPS = 4
PER_GROUP = 8
EXPERTS = GROUPS * PER_GROUP
TOP_K = 2
D_EXP = D // 2
FT = D_EXP // P
BLOCKS = S * TOP_K // P + EXPERTS
SLOTS_B = BLOCKS + 1

HD = 64
A_HEADS, A_KV, B_HEADS = 8, 2, 8
A_WIDTH, A_KVW, B_WIDTH = A_HEADS * HD, A_KV * HD, B_HEADS * HD
COL_QA, COL_KA = 0, A_WIDTH
COL_VA = COL_KA + A_KVW
COL_QB = COL_VA + A_KVW
COL_KB, COL_VB = COL_QB + B_WIDTH, COL_QB + 2 * B_WIDTH
COL_Z = COL_QB + 3 * B_WIDTH
DILATIONS = (1, 4, 16)
BUCKETS, MAX_DISTANCE = 32, 2048
BAND = 384
SC_AB = HD ** -0.5

C_HEADS, C_QR, C_KVR, C_NOPE, C_ROPE, C_V = 16, 256, 128, 64, 32, 64
C_LAT = C_QR + C_KVR + C_ROPE
C_QK = C_NOPE + C_ROPE
C_SCALE = C_QK ** -0.5
QR_T = C_QR // P
ROPE_HALF = C_ROPE // 2
ROPE_THETA = 10000.0
TWO_PI = 2.0 * math.pi
TWO_PI_1 = 6.28125
TWO_PI_2 = float(np.float32(round((TWO_PI - TWO_PI_1) * 2 ** 21)) / np.float32(2 ** 21))
TWO_PI_3 = TWO_PI - TWO_PI_1 - TWO_PI_2
ROUND = 1.5 * 2 ** 23
PI_BELOW = 3.1415925


def inverse_frequencies():
    return np.power(np.float32(ROPE_THETA), -np.arange(0, C_ROPE, 2, dtype=np.float32) / np.float32(C_ROPE))


def window_reciprocals():
    t = np.arange(PAD)
    return np.stack([1.0 / np.minimum(t + 1, w) for w in POOL_WINDOWS]).astype(np.float32)


def bucket_onehot():
    dist = 255 - np.arange(BAND)
    inside = (dist >= 0) & (dist <= P)
    out = np.zeros((BUCKETS + 1, len(DILATIONS), BAND), np.float32)
    exact = BUCKETS // 2
    for c, dilation in enumerate(DILATIONS):
        d = np.maximum(dist, 0) * dilation
        far = np.maximum(d, 1).astype(np.float32) / np.float32(exact)
        large = exact + (np.log(far) / np.float32(math.log(MAX_DISTANCE / exact)) * np.float32(BUCKETS - exact)).astype(np.int32)
        bucket = np.where(d < exact, d, np.minimum(large, BUCKETS - 1))
        for x in range(BAND):
            out[bucket[x] if inside[x] else BUCKETS, c, x] = 1.0
    return out


class Scope:

    def __init__(self, nc, ctx, tag):
        self.nc, self.ctx, self.tag, self.sems = nc, ctx, tag, []
        ctx.callback(self.clear)

    def clear(self):
        self.nc.clear_and_free_semaphores(self.sems)
        self.nc.all_engine_barrier()

    def sb(self, name, shape, dt=F32):
        return self.ctx.enter_context(self.nc.sbuf_tensor(f"{self.tag}_{name}", shape, dt))

    def sem(self, name):
        self.sems.append(self.nc.alloc_semaphore(f"{self.tag}_{name}"))
        return self.sems[-1]


class Chain:

    def __init__(self, engine, sem):
        self.engine, self.sem, self.n = engine, sem, 0

    def __call__(self, instruction):
        self.n += 1
        instruction.then_inc(self.sem, 1)
        self.engine.wait_ge(self.sem, self.n)


def multiply_split(pe, out, a, b, start, stop):
    pe.matmul(out, a[0], b[0], start=start, stop=False)
    pe.matmul(out, a[0], b[1], start=False, stop=False)
    return pe.matmul(out, a[1], b[0], start=False, stop=stop)


def low_part(dve, low, x, high):
    return dve.tensor_tensor(low, x, high.bitcast(F32), ALU.subtract)


def tiled_rows(ap):
    return ap.rearrange("(k p) n -> p k n", p=P)


def make_constants(nc, K):
    with ExitStack() as ctx:
        sc = Scope(nc, ctx, "const")
        filled, made = sc.sem("filled"), sc.sem("made")
        with nc.Block() as block:
            @block.gpsimd
            def _(pool):
                pool.memset(K["ident"][:, :], 0.0).then_inc(filled, 1)
                pool.memset(K["ones"][:, :], 1.0).then_inc(filled, 1)
                pool.memset(K["neg_after"][:, :], 0.0).then_inc(filled, 1)
                pool.memset(K["neg_before"][:, :], 0.0).then_inc(filled, 1)
                pool.memset(K["sel_neg"][:, :, :], 0.0).then_inc(filled, 1)
                pool.memset(K["sel_one"][:, :, :], 0.0).then_inc(filled, 1)
                pool.memset(K["earlier"][:, :], 1.0).then_inc(filled, 1)
                pool.wait_ge(filled, 7)
                pool.affine_select(out=K["ident"][:, :], in_=K["ident"][:, :], compare_op=ALU.not_equal, fill=1.0,
                                   base=0, pattern=[[-1, P]], channel_multiplier=1).then_inc(made, 1)
                pool.affine_select(out=K["neg_after"][:, :], in_=K["neg_after"][:, :], compare_op=ALU.is_ge, fill=NEG,
                                   base=0, pattern=[[-1, P]], channel_multiplier=1).then_inc(made, 1)
                pool.affine_select(out=K["neg_before"][:, :], in_=K["neg_before"][:, :], compare_op=ALU.is_ge,
                                   fill=NEG, base=0, pattern=[[1, P]], channel_multiplier=-1).then_inc(made, 1)
                pool.affine_select(out=K["earlier"][:, :], in_=K["earlier"][:, :], compare_op=ALU.is_gt, fill=0.0,
                                   base=0, pattern=[[1, P]], channel_multiplier=-1).then_inc(made, 1)
                pool.affine_select(out=K["sel_neg"][:, :, :], in_=K["sel_neg"][:, :, :], compare_op=ALU.not_equal,
                                   fill=-1.0, base=0, pattern=[[-1, HEADS], [0, P]], channel_multiplier=1).then_inc(made, 1)
                pool.affine_select(out=K["sel_one"][:, :, :], in_=K["sel_one"][:, :, :], compare_op=ALU.not_equal,
                                   fill=1.0, base=0, pattern=[[-1, HEADS], [0, P]], channel_multiplier=1).then_inc(made, 1)
                pool.wait_ge(made, 6)


def square_sum(act, K, t, scratch, summed):
    act.activation(scratch, K["X"][:, t, :], ACT.Square, accum_out=K["ss"][:, t:t + 1]).then_inc(summed, 1)


def load_x(nc, K, x):
    with ExitStack() as ctx:
        sc = Scope(nc, ctx, "load")
        squares = sc.sb("squares", [P, 2, D])
        loaded = [sc.sem(f"loaded{t}") for t in range(NT)]
        summed = sc.sem("summed")
        with nc.Block() as block:
            @block.sync
            def _(sp):
                for t in range(0, NT, 2):
                    sp.dma_start(K["X"][:, t, :], x[t * P:(t + 1) * P, :]).then_inc(loaded[t], 16)

            @block.scalar
            def _(act):
                for t in range(1, NT, 2):
                    act.dma_start(K["X"][:, t, :], x[t * P:(t + 1) * P, :]).then_inc(loaded[t], 16)
                for t in range(NT):
                    act.wait_ge(loaded[t], 16)
                    if t >= 2:
                        act.wait_ge(summed, t - 1)
                    square_sum(act, K, t, squares[:, t % 2, :], summed)


def norm_transpose(nc, K, g, tag, h_dram=None, halves=None, in_place=False):
    by_row = h_dram is not None
    assert not (by_row and halves is not None)
    X, hT, ps, ident = K["X"], K["hT"], K["ps"], K["ident"]
    with ExitStack() as ctx:
        sc = Scope(nc, ctx, tag)
        gcol = sc.sb("gcol", [P, KT])
        var = sc.sb("var", [P, NT])
        std = sc.sb("std", [P, NT])
        rs = sc.sb("rs", [P, NT])
        h = sc.sb("h", [P, NT, D])
        grow = sc.sb("grow", [P, D]) if by_row else None
        stored = sc.sem("stored")
        g_loaded, var_ready, std_ready = sc.sem("g_loaded"), sc.sem("var_ready"), sc.sem("std_ready")
        rs_ready, h_act = sc.sem("rs_ready"), sc.sem("h_act")
        h_ready, turned, out_act, out_dve = sc.sem("h_ready"), sc.sem("turned"), sc.sem("out_act"), sc.sem("out_dve")
        units = [(half, k) for half in range(NH) for k in range(KT)]
        with nc.Block() as block:
            @block.sync
            def _(sp):
                if by_row:
                    sp.dma_start(grow[:, :], g.partition_broadcast(P)).then_inc(g_loaded, 16)
                    for t in range(NT):
                        sp.wait_ge(h_ready, t + 1)
                        sp.dma_start(h_dram[t * P:(t + 1) * P, :], h[:, t, :]).then_inc(stored, 16)
                    sp.wait_ge(stored, 16 * NT)
                else:
                    sp.dma_start(gcol[:, :], g.rearrange("(k p) -> p k", p=P)).then_inc(g_loaded, 16)

            @block.scalar
            def _(act):
                act.wait_ge(var_ready, 1)
                act.activation(std[:, :], var[:, :], ACT.Sqrt).then_inc(std_ready, 1)
                if not by_row:
                    act.wait_ge(rs_ready, 1)
                    for t in range(1, NT, 2):
                        act.activation(h[:, t, :], X[:, t, :], ACT.Copy, scale=rs[:, t:t + 1]).then_inc(h_act, 1)
                act.wait_ge(g_loaded, 16)
                for u, (half, k) in enumerate(units):
                    if halves is not None:
                        act.wait_ge(turned, u + 1)
                        act.activation(halves[:, 0, k, half * HALF:(half + 1) * HALF], ps[:, u % 8, :], ACT.Copy,
                                       scale=gcol[:, k:k + 1]).then_inc(out_act, 1)
                    elif u % 2 == 0:
                        act.wait_ge(turned, u + 1)
                        act.activation(hT[:, k, half * HALF:(half + 1) * HALF], ps[:, u % 8, :], ACT.Copy,
                                       scale=1.0 if by_row else gcol[:, k:k + 1]).then_inc(out_act, 1)

            @block.vector
            def _(dve):
                dve.tensor_scalar(var[:, :], K["ss"][:, :], 1.0 / D, EPS, ALU.mult, ALU.add).then_inc(var_ready, 1)
                dve.wait_ge(std_ready, 1)
                dve.reciprocal(rs[:, :], std[:, :]).then_inc(rs_ready, 1)
                dve.wait_ge(rs_ready, 1)
                dve.wait_ge(g_loaded, 16)
                for t in range(0, NT, 1 if by_row else 2):
                    if by_row:
                        dve.scalar_tensor_tensor(out=h[:, t, :], in0=X[:, t, :], scalar=rs[:, t:t + 1], in1=grow[:, :],
                                                 op0=ALU.mult, op1=ALU.mult).then_inc(h_ready, 1)
                    else:
                        dve.tensor_scalar(h[:, t, :], X[:, t, :], rs[:, t:t + 1], None, ALU.mult).then_inc(h_ready, 1)
                for u, (half, k) in enumerate(units):
                    if halves is not None:
                        dve.wait_ge(out_act, u + 1)
                        cols = slice(half * HALF, (half + 1) * HALF)
                        dve.scalar_tensor_tensor(out=halves[:, 1, k, cols], in0=ps[:, u % 8, :], scalar=gcol[:, k:k + 1],
                                                 in1=halves[:, 0, k, cols].bitcast(F32), op0=ALU.mult, op1=ALU.subtract).then_inc(out_dve, 1)
                    elif u % 2 == 1:
                        dve.wait_ge(turned, u + 1)
                        dve.tensor_scalar(hT[:, k, half * HALF:(half + 1) * HALF], ps[:, u % 8, :],
                                          1.0 if by_row else gcol[:, k:k + 1], None, ALU.mult).then_inc(out_dve, 1)

            @block.tensor
            def _(pe):
                for u, (half, k) in enumerate(units):
                    if by_row:
                        pe.wait_ge(h_ready, (half + 1) * NT // NH)
                    else:
                        tiles = NT if in_place else (half + 1) * NT // NH
                        pe.wait_ge(h_ready, tiles // 2)
                        pe.wait_ge(h_act, tiles // 2)
                    if u >= 8 and halves is not None:
                        pe.wait_ge(out_dve, u - 7)
                    elif u >= 8:
                        pe.wait_ge(out_act if u % 2 == 0 else out_dve, (u - 8) // 2 + 1)
                    for j in range(4):
                        mm = pe.transpose(ps[:, u % 8, j * P:(j + 1) * P], h[:, half * 4 + j, k * P:(k + 1) * P], ident[:, :])
                    mm.then_inc(turned, 1)


def mixer_projections(nc, K, M, w_in, b_if, conv_q, conv_k, w_pool, pool_scale, invcnt):
    hT, ps = K["hT"], K["ps"]
    SLOTS = 6
    with ExitStack() as ctx:
        sc = Scope(nc, ctx, "proj")
        w = sc.sb("w", [P, SLOTS, KT, P])
        wif = sc.sb("wif", [P, KT, 2 * HEADS])
        raw = sc.sb("raw", [P, 2, PAD + S])
        acc = sc.sb("acc", [P, 2, PAD + S])
        cw = sc.sb("cw", [P, 2, HEADS, CONV_K])
        wp = sc.sb("wp", [P, 4, P])
        pscale = sc.sb("pscale", [P, 4])
        icnt = sc.sb("icnt", [P, 4, PAD])
        bi = sc.sb("bi", [HEADS, 2])
        ig, fg, e1, e2 = [M["yT"][0:HEADS, i, :].rearrange("p (c t) -> p c t", t=P) for i in range(4)]
        bb = M["og"][0:HEADS, 0:2, :].rearrange("p a (c t) -> p a c t", t=P)
        cm = M["og"][0:HEADS, 2:4, :].rearrange("p a (c t) -> p a c t", t=P)
        small = sc.sb("small", [HEADS, 4, NC])
        loaded = [sc.sem(f"w{i}") for i in range(SLOTS)]
        consts, evac, made, slot_free = sc.sem("consts"), sc.sem("evac"), sc.sem("made"), sc.sem("slot_free")
        conv_done, silu_done, pool_done, chain = sc.sem("conv_done"), sc.sem("silu_done"), sc.sem("pool_done"), sc.sem("chain")
        gate_dve, gate_act, rows = sc.sem("gate_dve"), sc.sem("gate_act"), sc.sem("rows")
        achain = sc.sem("achain")
        tiles = []
        for h in range(HEADS):
            tiles += [("q", h, COL_Q + h * P), ("k", h, COL_K + h * P)]
        tiles += [("v", j, COL_V + j * P) for j in range(4)]
        tiles += [("p", g, COL_POOL + g * P) for g in range(4)]
        tiles += [("o", h, COL_O + h * P) for h in range(HEADS)]
        V0 = 8
        UQ = 4
        UV = UQ + 2 * V0
        UP = UV + NT
        UO = UP + 8
        UY = UO + 8
        wif_loaded = sc.sem("wif_loaded")
        consts_n = 16 * 14

        with nc.Block() as block:
            @block.sync
            def _(sp):
                sp.dma_start(wif[:, :, :], tiled_rows(w_in[:, COL_I:COL_I + 2 * HEADS])).then_inc(wif_loaded, 16)
                for n, (kind, j, col) in enumerate(tiles):
                    if n >= SLOTS:
                        sp.wait_ge(slot_free, n - SLOTS + 1)
                    sp.dma_start(w[:, n % SLOTS, :, :], tiled_rows(w_in[:, col:col + P])).then_inc(loaded[n % SLOTS], 16)

            @block.tensor
            def _(pe):
                pe.wait_ge(wif_loaded, 16)
                u = 0
                for part in range(2):
                    for half in range(NH):
                        for k in range(KT):
                            mm = pe.matmul(ps[0:HEADS, u % 8, :], wif[:, k, part * HEADS:(part + 1) * HEADS],
                                           hT[:, k, half * HALF:(half + 1) * HALF], start=(k == 0), stop=(k == KT - 1))
                        mm.then_inc(made, 1)
                        u += 1
                for n, (kind, j, col) in enumerate(tiles):
                    if kind == "v":
                        if j < 3:
                            continue
                        for i in range(4):
                            pe.wait_ge(loaded[(V0 + i) % SLOTS], 16 * ((V0 + i) // SLOTS + 1))
                        s0 = V0 % SLOTS
                        for t in range(NT):
                            pe.wait_ge(evac, u - 7)
                            for k in range(KT):
                                mm = pe.matmul(ps[:, u % 8, :], hT[:, k, t * P:(t + 1) * P], w[:, s0:s0 + 4, k, :],
                                               start=(k == 0), stop=(k == KT - 1))
                            mm.then_inc(made, 1)
                            u += 1
                        pe.wait_ge(made, u)
                        pe.sem_inc(slot_free, 4)
                        continue
                    pe.wait_ge(loaded[n % SLOTS], 16 * (n // SLOTS + 1))
                    for half in range(NH):
                        if u >= 8:
                            pe.wait_ge(evac, u - 7)
                        for k in range(KT):
                            mm = pe.matmul(ps[:, u % 8, :], w[:, n % SLOTS, k, :], hT[:, k, half * HALF:(half + 1) * HALF],
                                           start=(k == 0), stop=(k == KT - 1))
                        mm.then_inc(made, 1)
                        u += 1
                    pe.wait_ge(made, u)
                    pe.sem_inc(slot_free, 1)
                assert u == UY
                pe.wait_ge(consts, consts_n)
                for g in range(4):
                    pe.wait_ge(pool_done, g + 1)
                    for half in range(NH):
                        pe.wait_ge(evac, u - 7)
                        pe.matmul(ps[:, u % 8, :], wp[:, g, :], M["dT"][:, g, half * HALF:(half + 1) * HALF],
                                  start=True, stop=True).then_inc(made, 1)
                        u += 1
                pe.wait_ge(rows, 1)
                pe.wait_ge(evac, u)
                for c in range(NC):
                    mm = pe.transpose(ps[:, c // 4, (c % 4) * P:(c % 4 + 1) * P], M["R"][:, c * P:(c + 1) * P], K["ident"][:, :])
                for h in range(HEADS):
                    mm = pe.matmul(ps[:, 2, h * NC:(h + 1) * NC], K["sel_one"][:, h, :], small[:, 3, :], start=True, stop=True,
                                   skip_group_check=True)
                mm.then_inc(made, 1)

            @block.scalar
            def _(act):
                for which, taps in enumerate((conv_q, conv_k)):
                    for h in range(HEADS):
                        act.dma_start(cw[:, which, h, :], taps[:, h * DH:(h + 1) * DH].rearrange("j p -> p j")).then_inc(consts, 16)
                act.dma_start(wp[:, :, :], w_pool.rearrange("g c d -> c g d")).then_inc(consts, 16)
                act.dma_start(pscale[:, :], pool_scale.rearrange("(g p) -> p g", p=P)).then_inc(consts, 16)
                act.dma_start(icnt[:, :, :], invcnt.partition_broadcast(P)).then_inc(consts, 16)
                act.dma_start(bi[:, 0:1], b_if[0:HEADS].rearrange("(h a) -> h a", a=1)).then_inc(consts, 16)
                act.dma_start(bi[:, 1:2], b_if[HEADS:2 * HEADS].rearrange("(h a) -> h a", a=1)).then_inc(consts, 16)
                act.dma_start(M["ghead"][:, :], M["g_head_dram"].rearrange("(h p) -> p h", p=P)).then_inc(consts, 16)
                act.wait_ge(consts, consts_n)
                for u in range(4):
                    half = u % 2
                    dst = (ig, fg)[u // 2]
                    act.wait_ge(made, u + 1)
                    act.activation(dst[:, half * 4:half * 4 + 4, :], ps[0:HEADS, u % 8, :].rearrange("p (c t) -> p c t", t=P),
                                   ACT.Identity, bias=bi[:, u // 2:u // 2 + 1]).then_inc(evac, 1)
                link = Chain(act, achain)
                act.wait_ge(gate_dve, 1)
                link(act.activation(e1[:, :, :], e1[:, :, :], ACT.Exp, scale=-1.0))
                act.activation(e1[:, :, :], e1[:, :, :], ACT.Ln, bias=1.0).then_inc(gate_act, 1)
                for n in range(V0):
                    for half in range(NH):
                        u = UQ + 2 * n + half
                        act.wait_ge(made, u + 1)
                        if n >= 2:
                            act.wait_ge(conv_done, n - 1)
                        act.activation(raw[:, n % 2, PAD + half * HALF:PAD + (half + 1) * HALF], ps[:, u % 8, :],
                                       ACT.Copy).then_inc(evac, 1)
                    if n == 0:
                        act.wait_ge(gate_dve, 2)
                        act.activation(M["R"][32:32 + HEADS, :], e1[:, :, :].rearrange("p c t -> p (c t)"), ACT.Exp, scale=-1.0).then_inc(gate_act, 1)
                        act.activation(M["R"][64:64 + HEADS, :], e2[:, :, :].rearrange("p c t -> p (c t)"), ACT.Exp).then_inc(gate_act, 1)
                        act.activation(M["R"][96:96 + HEADS, :], fg[:, :, :].rearrange("p c t -> p (c t)"), ACT.Exp).then_inc(gate_act, 1)
                        act.activation(small[:, 3, :], small[:, 2, :], ACT.Exp).then_inc(gate_act, 1)
                        act.wait_ge(gate_act, 5)
                        act.sem_inc(rows, 1)
                    if n >= 1:
                        act.wait_ge(conv_done, n)
                        m = n - 1
                        dst = M["qT"] if m % 2 == 0 else M["kT"]
                        act.activation(dst[:, m // 2, :], acc[:, m % 2, 0:S], ACT.Silu).then_inc(silu_done, 1)
                act.wait_ge(conv_done, V0)
                act.activation(M["kT"][:, HEADS - 1, :], acc[:, 1, 0:S], ACT.Silu).then_inc(silu_done, 1)
                for t in range(NT):
                    u = UV + t
                    act.wait_ge(made, u + 1)
                    act.activation(M["v"][:, t, :, 0:DH], ps[:, u % 8, :].rearrange("p (h e) -> p h e", e=DH), ACT.Copy).then_inc(evac, 1)
                for g in range(4):
                    for half in range(NH):
                        u = UP + 2 * g + half
                        act.wait_ge(made, u + 1)
                        if g >= 2:
                            act.wait_ge(pool_done, g - 1)
                        act.activation(raw[:, g % 2, PAD + half * HALF:PAD + (half + 1) * HALF], ps[:, u % 8, :],
                                       ACT.Copy).then_inc(evac, 1)
                for h in range(HEADS):
                    for half in range(NH):
                        u = UO + 2 * h + half
                        act.wait_ge(made, u + 1)
                        act.activation(M["og"][:, h, half * HALF:(half + 1) * HALF], ps[:, u % 8, :], ACT.Sigmoid).then_inc(evac, 1)
                for g in range(4):
                    for half in range(NH):
                        u = UY + 2 * g + half
                        act.wait_ge(made, u + 1)
                        act.activation(M["yT"][:, g, half * HALF:(half + 1) * HALF], ps[:, u % 8, :], ACT.Copy,
                                       scale=pscale[:, g:g + 1]).then_inc(evac, 1)
                act.wait_ge(made, UY + 9)
                for j in range(2):
                    act.activation(M["RT"][:, 4 * j:4 * j + 4, :], ps[:, j, :].rearrange("p (c r) -> p c r", r=P), ACT.Copy).then_inc(achain, 1)
                act.activation(M["SP"][:, :, :], ps[:, 2, 0:HEADS * NC].rearrange("p (h c) -> p h c", c=NC), ACT.Copy).then_inc(achain, 1)

            @block.vector
            def _(dve):
                link = Chain(dve, chain)
                dve.memset(raw[:, 0, 0:PAD], 0.0).then_inc(chain, 1)
                dve.memset(raw[:, 1, 0:PAD], 0.0).then_inc(chain, 1)
                dve.memset(acc[:, 0, 0:PAD], 0.0).then_inc(chain, 1)
                dve.memset(acc[:, 1, 0:PAD], 0.0).then_inc(chain, 1)
                dve.memset(M["v"][:, :, :, DH:DH + 1], 1.0).then_inc(chain, 1)
                link.n = 5
                link(dve.memset(M["R"][:, :], 0.0))
                dve.wait_ge(evac, 4)
                link(dve.scalar_tensor_tensor(out=e1[:, :, :], in0=fg[:, :, :], scalar=-1.0, in1=fg[:, :, :], op0=ALU.mult, op1=ALU.max))
                dve.tensor_scalar(e2[:, :, :], fg[:, :, :], 0.0, None, ALU.min).then_inc(gate_dve, 1)
                dve.wait_ge(gate_act, 1)
                dve.wait_ge(gate_dve, 1)
                link(dve.tensor_tensor(bb[:, 0, :, :], e2[:, :, :], e1[:, :, :], ALU.subtract))
                cur = 0
                for step in (1, 2, 4, 8, 16, 32, 64):
                    link(dve.tensor_copy(bb[:, 1 - cur, :, 0:step], bb[:, cur, :, 0:step]))
                    link(dve.tensor_tensor(bb[:, 1 - cur, :, step:], bb[:, cur, :, step:], bb[:, cur, :, 0:P - step], ALU.add))
                    cur = 1 - cur
                b = bb[:, cur, :, :]
                U = M["U"]
                link(dve.tensor_tensor(U[:, :, :], ig[:, :, :], b, ALU.subtract))
                link(dve.tensor_copy(cm[:, 0, :, :], U[:, :, :]))
                cur = 0
                for step in (1, 2, 4, 8, 16, 32, 64):
                    link(dve.tensor_copy(cm[:, 1 - cur, :, 0:step], cm[:, cur, :, 0:step]))
                    link(dve.tensor_tensor(cm[:, 1 - cur, :, step:], cm[:, cur, :, step:], cm[:, cur, :, 0:P - step], ALU.max))
                    cur = 1 - cur
                cmx = cm[:, cur, :, :]
                prev = small[:, 0, :]
                link(dve.memset(small[:, :, :], 0.0))
                for c in range(NC - 1):
                    link(dve.scalar_tensor_tensor(out=small[:, 0, c + 1:c + 2], in0=small[:, 0, c:c + 1], scalar=cmx[:, c, P - 1:P],
                                                  in1=b[:, c, P - 1:P], op0=ALU.max, op1=ALU.add))
                G = M["G"]
                prev_all = small[:, 0, :].rearrange("p (c a) -> p c a", a=1).to_broadcast([HEADS, NC, P])
                link(dve.tensor_tensor(G[:, :, :], cmx, prev_all, ALU.max))
                link(dve.tensor_copy(small[:, 1, :], G[:, :, P - 1:P].rearrange("p c a -> p (c a)")))
                last_all = small[:, 1, :].rearrange("p (c a) -> p c a", a=1).to_broadcast([HEADS, NC, P])
                link(dve.tensor_copy(M["R"][0:HEADS, :], U[:, :, :].rearrange("p c t -> p (c t)")))
                link(dve.tensor_tensor(e1[:, :, :], b, G[:, :, :], ALU.add))
                link(dve.tensor_tensor(e2[:, :, :], prev_all, G[:, :, :], ALU.subtract))
                link(dve.tensor_tensor(fg[:, :, :], U[:, :, :], last_all, ALU.subtract))
                dve.tensor_tensor(small[:, 2, :], small[:, 0, :], small[:, 1, :], ALU.subtract).then_inc(gate_dve, 1)
                dve.wait_ge(consts, consts_n)
                for n in range(V0):
                    kind = n % 2
                    h = n // 2
                    dve.wait_ge(evac, UQ + 2 * n + 2)
                    if n >= 2:
                        dve.wait_ge(silu_done, n - 1)
                    for j in range(CONV_K):
                        src = raw[:, n % 2, PAD - CONV_K + 1 + j:PAD - CONV_K + 1 + j + S]
                        dst = acc[:, n % 2, 0:S]
                        tap = cw[:, kind, h, j:j + 1]
                        if j == 0:
                            link(dve.tensor_scalar(dst, src, tap, None, ALU.mult))
                        elif j < CONV_K - 1:
                            link(dve.scalar_tensor_tensor(out=dst, in0=src, scalar=tap, in1=dst, op0=ALU.mult, op1=ALU.add))
                        else:
                            dve.scalar_tensor_tensor(out=dst, in0=src, scalar=tap, in1=dst, op0=ALU.mult, op1=ALU.add).then_inc(conv_done, 1)
                dve.wait_ge(silu_done, V0)
                link(dve.memset(acc[:, :, 0:PAD], 0.0))
                for g, win in enumerate(POOL_WINDOWS):
                    dve.wait_ge(evac, UP + 2 * g + 2)
                    u_in = raw[:, g % 2, :]
                    cur, width, flip = u_in, 1, 0
                    while width < win:
                        nxt = acc[:, flip, :]
                        link(dve.tensor_tensor(nxt[:, PAD:], cur[:, PAD:], cur[:, PAD - width:PAD + S - width], ALU.add))
                        cur, width, flip = nxt, 2 * width, 1 - flip
                    dT = M["dT"]
                    link(dve.scalar_tensor_tensor(out=dT[:, g, :], in0=cur[:, PAD:], scalar=1.0 / win, in1=u_in[:, PAD:], op0=ALU.mult, op1=ALU.subtract))
                    link(dve.tensor_tensor(icnt[:, g, :], icnt[:, g, :], cur[:, PAD:2 * PAD], ALU.mult))
                    dve.tensor_tensor(dT[:, g, 0:PAD], icnt[:, g, :], u_in[:, PAD:2 * PAD], ALU.subtract).then_inc(pool_done, 1)


def mlstm(nc, K, M):
    ps, ident = K["ps"], K["ident"]
    qT, kT, v, U, G, RT, SP = M["qT"], M["kT"], M["v"], M["U"], M["G"], M["RT"], M["SP"]
    SCALE = DH ** -0.5
    E = DH + 1
    with ExitStack() as ctx:
        sc = Scope(nc, ctx, "ml")
        C = sc.sb("C", [P, HEADS, E])
        ex = sc.sb("ex", [P, HEADS, P])
        pt = sc.sb("pt", [P, HEADS, P])
        kw = sc.sb("kw", [P, HEADS, P])
        inter = sc.sb("inter", [P, HEADS, E])
        num = sc.sb("num", [P, HEADS, E])
        den = sc.sb("den", [P, 2, HEADS])
        stats = sc.sb("stats", [P, HEADS, 6])
        mv = sc.sb("mv", [P, NC, HEADS, 2])
        std, rstd = sc.sb("std", [P, NC, HEADS]), sc.sb("rstd", [P, NC, HEADS])
        hm = sc.sb("hm", [P, NC, HEADS, DH])
        scores, gb, kt_done, e_ready, e_done, p_done, kw_done = [sc.sem(x) for x in
            ("scores", "gb", "kt_done", "e_ready", "e_done", "p_done", "kw_done")]
        inter_done, inter_out, intra_done, state_done, c_new, num_done, chain, achain = [sc.sem(x) for x in
            ("inter_done", "inter_out", "intra_done", "state_done", "c_new", "num_done", "chain", "achain")]
        var_ready, std_ready, hn_ready, turned, out_sem = [sc.sem(x) for x in ("var_ready", "std_ready", "hn_ready", "turned", "out")]

        def pair(bank, j):
            return ps[:, bank, j * E:(j + 1) * E]

        with nc.Block() as block:
            @block.tensor
            def _(pe):
                pe.wait_ge(c_new, 1)
                for c in range(NC):
                    cols = slice(c * P, (c + 1) * P)
                    if c:
                        pe.wait_ge(e_ready, c)
                    for h in range(HEADS):
                        mm = pe.matmul(ps[:, 1, h * P:(h + 1) * P], K["sel_neg"][:, h, :], G[:, c, :], start=True, stop=True, skip_group_check=True)
                    mm.then_inc(gb, 1)
                    if c:
                        pe.wait_ge(p_done, c)
                    for h in range(HEADS):
                        mm = pe.matmul(ps[:, 0, h * P:(h + 1) * P], kT[:, h, cols], qT[:, h, cols], start=True, stop=True, skip_group_check=True)
                    mm.then_inc(scores, 1)
                    if c:
                        pe.wait_ge(c_new, c + 1)
                    for h in range(HEADS):
                        mm = pe.transpose(ps[:, 2, h * P:(h + 1) * P], kT[:, h, cols], ident[:, :])
                    mm.then_inc(kt_done, 1)
                    if c:
                        pe.wait_ge(inter_out, c)
                    for h in range(HEADS):
                        mm = pe.matmul(pair(3 + h // 2, h % 2), qT[:, h, cols], C[:, h, :], start=True, stop=True, skip_group_check=True)
                    mm.then_inc(inter_done, 1)
                    pe.wait_ge(p_done, c + 1)
                    if c:
                        pe.wait_ge(num_done, c)
                    for h in range(HEADS):
                        mm = pe.matmul(pair(5 + h // 2, h % 2), pt[:, h, :], v[:, c, h, :], start=True, stop=True, skip_group_check=True)
                    mm.then_inc(intra_done, 1)
                    pe.wait_ge(kw_done, c + 1)
                    for h in range(HEADS):
                        mm = pe.matmul(pair((7, 2)[h // 2], h % 2), kw[:, h, :], v[:, c, h, :], start=True, stop=True, skip_group_check=True)
                    mm.then_inc(state_done, 1)
                for u in range(8):
                    half, h = u // HEADS, u % HEADS
                    pe.wait_ge(hn_ready, half + 1)
                    for j in range(4):
                        mm = pe.transpose(ps[:, u, j * P:(j + 1) * P], hm[:, half * 4 + j, h, :], ident[:, :])
                    mm.then_inc(turned, 1)

            @block.scalar
            def _(act):
                act.wait_ge(c_new, 1)
                for c in range(NC):
                    act.wait_ge(e_ready, c + 1)
                    for h in range(HEADS):
                        i = act.activation(ex[:, h, :], ex[:, h, :], ACT.Exp, bias=RT[:, c, h:h + 1])
                    i.then_inc(e_done, 1)
                    act.wait_ge(kt_done, c + 1)
                    if c:
                        act.wait_ge(state_done, c)
                    for h in range(HEADS):
                        i = act.activation(kw[:, h, :], ps[:, 2, h * P:(h + 1) * P], ACT.Copy, scale=RT[:, c, 96 + h:97 + h])
                    i.then_inc(kw_done, 1)
                    act.wait_ge(inter_done, c + 1)
                    if c:
                        act.wait_ge(num_done, c)
                    for h in range(HEADS):
                        i = act.activation(inter[:, h, :], pair(3 + h // 2, h % 2), ACT.Copy, scale=RT[:, c, 64 + h:65 + h])
                    i.then_inc(inter_out, 1)
                act.wait_ge(var_ready, 1)
                act.activation(std[:, :, :], std[:, :, :], ACT.Sqrt).then_inc(std_ready, 1)
                for u in range(8):
                    half, h = u // HEADS, u % HEADS
                    act.wait_ge(turned, u + 1)
                    act.activation(M["hmT"][:, h, half * HALF:(half + 1) * HALF], ps[:, u, :], ACT.Copy, scale=M["ghead"][:, h:h + 1]).then_inc(out_sem, 1)

            @block.vector
            def _(dve):
                link = Chain(dve, chain)
                link(dve.tensor_scalar(RT[:, :, 96:96 + HEADS], RT[:, :, 96:96 + HEADS], SCALE, None, ALU.mult))
                dve.memset(C[:, :, :], 0.0).then_inc(c_new, 1)
                dve.wait_ge(c_new, 1)
                mask = K["neg_before"][:, :].rearrange("p (a t) -> p a t", a=1).to_broadcast([P, HEADS, P])

                def all_done(instructions):
                    for i in instructions:
                        i.then_inc(chain, 1)
                        link.n += 1
                    dve.wait_ge(chain, link.n)

                def exponents(c):
                    dve.wait_ge(gb, c + 1)
                    if c:
                        dve.wait_ge(p_done, c)
                    dve.tensor_tensor(ex[:, :, :], ps[:, 1, :].rearrange("p (h t) -> p h t", t=P), mask, ALU.add).then_inc(e_ready, 1)

                def weights(c):
                    dve.wait_ge(e_done, c + 1)
                    dve.wait_ge(scores, c + 1)
                    if c:
                        dve.wait_ge(intra_done, c)
                    dve.scalar_tensor_tensor(out=pt[:, :, :], in0=ps[:, 0, :].rearrange("p (h t) -> p h t", t=P), scalar=SCALE, in1=ex[:, :, :],
                                             op0=ALU.mult, op1=ALU.mult).then_inc(p_done, 1)

                def outputs(c):
                    nq = num[:, :, DH:E].rearrange("p h a -> p (h a)")
                    link(dve.scalar_tensor_tensor(out=den[:, 0, :], in0=nq, scalar=-1.0, in1=nq, op0=ALU.mult, op1=ALU.max))
                    link(dve.tensor_tensor(den[:, 0, :], den[:, 0, :], RT[:, c, 32:32 + HEADS], ALU.max))
                    link(dve.reciprocal(den[:, 1, :], den[:, 0, :]))
                    all_done([dve.tensor_scalar(hm[:, c, h, :], num[:, h, 0:DH], den[:, 1, h:h + 1], None, ALU.mult) for h in range(HEADS)])

                def moments(c):
                    all_done([dve.bn_stats(stats[:, h, :], hm[:, c, h, :]) for h in range(HEADS)])
                    all_done([dve.bn_aggr(mv[:, c, h, :], stats[:, h, :]) for h in range(HEADS)])

                exponents(0)
                weights(0)
                for c in range(NC):
                    dve.wait_ge(inter_out, c + 1)
                    dve.wait_ge(intra_done, c + 1)
                    for j in range(2):
                        i = dve.tensor_tensor(num[:, 2 * j:2 * j + 2, :], ps[:, 5 + j, 0:2 * E].rearrange("p (h e) -> p h e", e=E),
                                              inter[:, 2 * j:2 * j + 2, :], ALU.add)
                        if j == 0:
                            link(i)
                    i.then_inc(num_done, 1)
                    dve.wait_ge(num_done, c + 1)
                    dve.wait_ge(state_done, c + 1)
                    for h in range(HEADS):
                        i = dve.scalar_tensor_tensor(out=C[:, h, :], in0=C[:, h, :], scalar=SP[:, h, c:c + 1],
                                                     in1=pair((7, 2)[h // 2], h % 2), op0=ALU.mult, op1=ALU.add)
                        if h < HEADS - 1:
                            i.then_inc(chain, 1)
                            link.n += 1
                    i.then_inc(c_new, 1)
                    if c + 1 < NC:
                        exponents(c + 1)
                    outputs(c)
                    if c + 1 < NC:
                        weights(c + 1)
                    moments(c)
                dve.tensor_scalar(std[:, :, :], mv[:, :, :, 1:2].rearrange("p c h a -> p c (h a)"), EPS, None, ALU.add).then_inc(var_ready, 1)
                dve.wait_ge(std_ready, 1)
                link(dve.reciprocal(rstd[:, :, :], std[:, :, :]))
                for half in range(NH):
                    all_done([dve.tensor_scalar(hm[:, c, h, :], hm[:, c, h, :], mv[:, c, h, 0:1], rstd[:, c, h:h + 1], ALU.subtract, ALU.mult)
                              for c in range(half * 4, half * 4 + 4) for h in range(HEADS)])
                    dve.sem_inc(hn_ready, 1)
                for u in range(8):
                    half, h = u // HEADS, u % HEADS
                    dve.wait_ge(out_sem, u + 1)
                    dst = M["hmT"][:, h, half * HALF:(half + 1) * HALF]
                    dve.tensor_tensor(dst, dst, M["og"][:, h, half * HALF:(half + 1) * HALF], ALU.mult).then_inc(chain, 1)


def mixer_merge(nc, K, M, hT, w_in, w_br_a, w_br_b, mT, y_dram):
    ps = K["ps"]
    with ExitStack() as ctx:
        sc = Scope(nc, ctx, "merge")
        h = sc.sb("h", [P, 2, KT, S], F32R)
        W = split_weights(sc, 3, P, [16 * (n // 3 + 1) for n in range(2 * KT)])
        w, raw = W["w"], W["raw"]
        wb = sc.sb("wb", [P, 2, 2, 4, P])
        sg = sc.sb("sg", [P, 4, HALF])
        part = sc.sb("part", [P, 2, HALF])
        loaded = [sc.sem(f"wb{i}") for i in range(2)]
        h_high, h_split = sc.sem("h_high"), sc.sem("h_split")
        done, sig, out_sem, chain = sc.sem("done"), sc.sem("sig"), sc.sem("out"), sc.sem("chain")
        zeroed = sc.sem("zeroed")
        chain_pool = sc.sem("chain_pool")
        zero = sc.sb("zero", [P, D])
        with nc.Block() as block:
            @block.sync
            def _(sp):
                for n in range(2 * KT):
                    j, which = n // 2, n % 2
                    if n >= 3:
                        sp.wait_ge(W["split"], n - 2)
                    col = (COL_GA, COL_GB)[which] + j * P
                    sp.dma_start(raw[:, n % 3, :, :], tiled_rows(w_in[:, col:col + P])).then_inc(W["loaded"][n % 3], 16)
                    if which == 0:
                        if j >= 2:
                            sp.wait_ge(done, 8 * (j - 1))
                        for b, src in enumerate((w_br_a, w_br_b)):
                            sp.dma_start(wb[:, j % 2, b, :, :], tiled_rows(src[:, j * P:(j + 1) * P])).then_inc(loaded[j % 2], 16)

            @block.gpsimd
            def _(pool):
                pool.memset(zero[:, :], 0.0).then_inc(chain_pool, 1)
                pool.wait_ge(chain_pool, 1)
                for b in range(SLOTS_B):
                    pool.dma_start(y_dram[b * P:(b + 1) * P, :], zero[:, :]).then_inc(zeroed, 16)
                pool.wait_ge(zeroed, 16 * SLOTS_B)

            @block.tensor
            def _(pe):
                for j in range(KT):
                    for which in range(2):
                        n = 2 * j + which
                        pe.wait_ge(W["split"], n + 1)
                        if which == 0:
                            pe.wait_ge(loaded[j % 2], 32 * (j // 2 + 1))
                        s = n % 3
                        src = (M["yT"], M["hmT"])[which]
                        for half in range(NH):
                            base = 4 * half
                            cols = slice(half * HALF, (half + 1) * HALF)
                            if which == 0 and j:
                                pe.wait_ge(out_sem, 2 * (j - 1) + half + 1)
                            for k in range(KT):
                                if n == 0 and half == 0:
                                    pe.wait_ge(h_split, k + 1)
                                mm = multiply_split(pe, ps[:, base + which, :], (w[:, s, 0, k, :], w[:, s, 1, k, :]), (h[:, 0, k, cols], h[:, 1, k, cols]),
                                                    k == 0, k == KT - 1)
                            mm.then_inc(done, 1)
                            for k in range(4):
                                mm = pe.matmul(ps[:, base + 2 + which, :], wb[:, j % 2, which, k, :], src[:, k, cols], start=(k == 0), stop=(k == 3))
                            mm.then_inc(done, 1)
                        pe.wait_ge(done, 4 * (n + 1))
                        pe.sem_inc(W["free"], 1)

            @block.scalar
            def _(act):
                high_weights(act, W, 0)
                for k in range(KT):
                    act.activation(h[:, 0, k, :], hT[:, k, :], ACT.Copy).then_inc(h_high, 1)
                high_weights(act, W, 1)
                high_weights(act, W, 2)
                for j in range(KT):
                    for which in range(2):
                        n = 2 * j + which
                        for half in range(NH):
                            act.wait_ge(done, 4 * n + 2 * half + 1)
                            if j:
                                act.wait_ge(out_sem, 2 * (j - 1) + half + 1)
                            act.activation(sg[:, 2 * half + which, :], ps[:, 4 * half + which, :], ACT.Sigmoid).then_inc(sig, 1)
                        if n + 3 < 2 * KT:
                            high_weights(act, W, n + 3)

            @block.vector
            def _(dve):
                link = Chain(dve, chain)
                low_weights(dve, W, 0)
                for k in range(KT):
                    dve.wait_ge(h_high, k + 1)
                    low_part(dve, h[:, 1, k, :], hT[:, k, :], h[:, 0, k, :]).then_inc(h_split, 1)
                low_weights(dve, W, 1)
                low_weights(dve, W, 2)
                for j in range(KT):
                    for half in range(NH):
                        r = 2 * j + half
                        for which in range(2):
                            n = 2 * j + which
                            dve.wait_ge(sig, 2 * n + half + 1)
                            dve.wait_ge(done, 4 * n + 2 * half + 2)
                            link(dve.tensor_tensor(part[:, which, :], ps[:, 4 * half + 2 + which, :], sg[:, 2 * half + which, :], ALU.mult))
                            if half == 0 and n + 3 < 2 * KT and which == 0:
                                low_weights(dve, W, n + 3)
                        dve.tensor_tensor(mT[:, j, half * HALF:(half + 1) * HALF], part[:, 0, :], part[:, 1, :], ALU.add).then_inc(out_sem, 1)
                        dve.wait_ge(out_sem, r + 1)
                    if 2 * j + 4 < 2 * KT:
                        low_weights(dve, W, 2 * j + 4)


def project_add(nc, K, mT, w_out, tag, x_dram=None, over_x=False):
    X, ps = K["X"], K["ps"]
    N = HALF // 2
    KH = KT // 2
    with ExitStack() as ctx:
        sc = Scope(nc, ctx, tag)
        m = sc.sb("m", [P, 2, KT, S], F32R)
        raw = sc.sb("raw", [P, 2, KH, N])
        w = sc.sb("w", [P, 2, 2, KT, N], F32R)
        loaded = [sc.sem(f"w{i}") for i in range(2)]
        done, out_sem, x_loaded = sc.sem("done"), sc.sem("out"), sc.sem("x_loaded")
        w_high, w_split, m_high, m_split = sc.sem("w_high"), sc.sem("w_split"), sc.sem("m_high"), sc.sem("m_split")
        CHUNKS = D // N
        summed = sc.sem("summed")
        with nc.Block() as block:
            @block.sync
            def _(sp):
                for p in range(2 * CHUNKS):
                    if p >= 2:
                        sp.wait_ge(w_split, p - 1)
                    n, kh = p // 2, p % 2
                    sp.dma_start(raw[:, p % 2, :, :], tiled_rows(w_out[kh * KH * P:(kh + 1) * KH * P, n * N:(n + 1) * N])).then_inc(loaded[p % 2], 16)
                if x_dram is not None:
                    sp.wait_ge(x_loaded, 16 * NT)

            @block.scalar
            def _(act):
                def fetch_x():
                    for t in range(NT):
                        act.dma_start(X[:, t, :], x_dram[t * P:(t + 1) * P, :]).then_inc(x_loaded, 16)

                if x_dram is not None and not over_x:
                    fetch_x()
                for n in range(CHUNKS):
                    if n >= 2:
                        act.wait_ge(done, NT * (n - 1))
                    for kh in range(2):
                        p = 2 * n + kh
                        act.wait_ge(loaded[p % 2], 16 * (p // 2 + 1))
                        act.activation(w[:, n % 2, 0, kh * KH:(kh + 1) * KH, :], raw[:, p % 2, :, :], ACT.Copy).then_inc(w_high, 1)
                    if n == 0:
                        for t in range(NT):
                            act.activation(m[:, 0, :, t * P:(t + 1) * P], mT[:, :, t * P:(t + 1) * P], ACT.Copy).then_inc(m_high, 1)
                    if n == 1 and over_x:
                        act.wait_ge(m_split, NT)
                        fetch_x()
                act.wait_ge(w_split, 2 * CHUNKS)
                for t in range(NT):
                    act.wait_ge(out_sem, (CHUNKS - 1) * NT + t + 1)
                    if t >= 2:
                        act.wait_ge(summed, t - 1)
                    square_sum(act, K, t, raw[:, t % 2, :, :].rearrange("p k n -> p (k n)"), summed)

            @block.vector
            def _(dve):
                def split(n):
                    for kh in range(2):
                        p = 2 * n + kh
                        dve.wait_ge(w_high, p + 1)
                        low_part(dve, w[:, n % 2, 1, kh * KH:(kh + 1) * KH, :], raw[:, p % 2, :, :],
                                 w[:, n % 2, 0, kh * KH:(kh + 1) * KH, :]).then_inc(w_split, 1)

                split(0)
                for t in range(NT):
                    cols = slice(t * P, (t + 1) * P)
                    dve.wait_ge(m_high, t + 1)
                    low_part(dve, m[:, 1, :, cols], mT[:, :, cols], m[:, 0, :, cols]).then_inc(m_split, 1)
                for n in range(CHUNKS):
                    if n + 1 < CHUNKS:
                        split(n + 1)
                    if n == 0 and x_dram is not None:
                        dve.wait_ge(x_loaded, 16 * NT)
                    for t in range(NT):
                        u = n * NT + t
                        dve.wait_ge(done, u + 1)
                        dve.tensor_tensor(X[:, t, n * N:(n + 1) * N], X[:, t, n * N:(n + 1) * N], ps[:, u % 8, 0:N], ALU.add).then_inc(out_sem, 1)

            @block.tensor
            def _(pe):
                for n in range(CHUNKS):
                    pe.wait_ge(w_split, 2 * n + 2)
                    for t in range(NT):
                        u = n * NT + t
                        if n == 0:
                            pe.wait_ge(m_split, t + 1)
                        if u >= 8:
                            pe.wait_ge(out_sem, u - 7)
                        for k in range(KT):
                            mm = multiply_split(pe, ps[:, u % 8, 0:N], (m[:, 0, k, t * P:(t + 1) * P], m[:, 1, k, t * P:(t + 1) * P]),
                                                (w[:, n % 2, 0, k, :], w[:, n % 2, 1, k, :]), k == 0, k == KT - 1)
                        mm.then_inc(done, 1)


def norm_rows(nc, K, g, tag, out, last=False):
    X = K["X"]
    with ExitStack() as ctx:
        sc = Scope(nc, ctx, tag)
        grow = sc.sb("grow", [P, D])
        squares = sc.sb("squares", [P, 2, D])
        var, std, rs = [sc.sb(n, [P, NT]) for n in ("var", "std", "rs")]
        g_loaded, summed, var_ready, std_ready, done, chain, stored = [sc.sem(n) for n in
            ("g_loaded", "summed", "var_ready", "std_ready", "done", "chain", "stored")]
        with nc.Block() as block:
            @block.sync
            def _(sp):
                sp.dma_start(grow[:, :], g.partition_broadcast(P)).then_inc(g_loaded, 16)
                for t in range(NT):
                    sp.wait_ge(done, t + 1)
                    sp.dma_start(out[t * P:(t + 1) * P, :], X[:, t, :]).then_inc(stored, 16)
                sp.wait_ge(stored, 16 * NT)

            @block.scalar
            def _(act):
                act.wait_ge(var_ready, 1)
                act.activation(std[:, :], var[:, :], ACT.Sqrt).then_inc(std_ready, 1)
                for t in range(0 if last else NT):
                    act.wait_ge(done, t + 1)
                    if t >= 2:
                        act.wait_ge(summed, t - 1)
                    square_sum(act, K, t, squares[:, t % 2, :], summed)

            @block.vector
            def _(dve):
                link = Chain(dve, chain)
                dve.tensor_scalar(var[:, :], K["ss"][:, :], 1.0 / D, EPS, ALU.mult, ALU.add).then_inc(var_ready, 1)
                dve.wait_ge(std_ready, 1)
                link(dve.reciprocal(rs[:, :], std[:, :]))
                dve.wait_ge(g_loaded, 16)
                for t in range(NT):
                    dve.scalar_tensor_tensor(out=X[:, t, :], in0=X[:, t, :], scalar=rs[:, t:t + 1], in1=grow[:, :],
                                             op0=ALU.mult, op1=ALU.mult).then_inc(done, 1)


def route(nc, K, R, w_rg, b_rg, w_re, b_re, slot_tok):
    hT, ps = K["hT"], K["ps"]
    NL = GROUPS + EXPERTS
    with ExitStack() as ctx:
        sc = Scope(nc, ctx, "route")
        wr = sc.sb("wr", [P, KT, NL])
        brow = sc.sb("brow", [P, NL])
        L = sc.sb("L", [P, NT, NL])
        gi = sc.sb("gi", [P, GROUPS])
        ei = sc.sb("ei", [P, EXPERTS])
        bi = sc.sb("bi", [1, SLOTS_B])
        tok = sc.sb("tok", [P, NT], I32)
        zero = sc.sb("zero", [P, SLOTS_B], I32)
        gmax, gsum, pg, cmin = [sc.sb(n, [P, NT]) for n in ("gmax", "gsum", "pg", "cmin")]
        ge, gc, oh_g = [sc.sb(n, [P, NT, GROUPS]) for n in ("ge", "gc", "oh_g")]
        em = sc.sb("em", [P, NT, EXPERTS])
        cand = sc.sb("cand", [P, NT, EXPERTS])
        oh = sc.sb("oh", [P, TOP_K, NT, EXPERTS])
        both = sc.sb("both", [P, NT, EXPERTS])
        top = sc.sb("top", [P, TOP_K, NT])
        e2, den = sc.sb("e2", [P, NT]), sc.sb("den", [P, NT])
        rank = sc.sb("rank", [P, NT, EXPERTS])
        cnt = sc.sb("cnt", [P, EXPERTS])
        nblk = sc.sb("nblk", [P, EXPERTS])
        pend = sc.sb("pend", [P, 2, EXPERTS])
        dest = sc.sb("dest", [P, TOP_K, NT])
        cmp = sc.sb("cmp", [1, SLOTS_B, EXPERTS])
        be = sc.sb("be", [1, SLOTS_B])
        loaded, iotas, chain, logits, ranks, exp_in, exp_out = [sc.sem(n) for n in
            ("loaded", "iotas", "chain", "logits", "ranks", "exp_in", "exp_out")]
        picked, dest_ready, zeroed, scattered, idx_loaded = [sc.sem(n) for n in ("picked", "dest_ready", "zeroed", "scattered", "idx_loaded")]
        with nc.Block() as block:
            @block.sync
            def _(sp):
                sp.dma_start(wr[:, :, 0:GROUPS], tiled_rows(w_rg)).then_inc(loaded, 16)
                sp.dma_start(wr[:, :, GROUPS:NL], tiled_rows(w_re)).then_inc(loaded, 16)
                sp.dma_start(brow[:, 0:GROUPS], b_rg.partition_broadcast(P)).then_inc(loaded, 16)
                sp.dma_start(brow[:, GROUPS:NL], b_re.partition_broadcast(P)).then_inc(loaded, 16)
                sp.wait_ge(iotas, 5)
                sp.dma_start(slot_tok.rearrange("(p b) a -> p (b a)", p=P), zero[:, :]).then_inc(zeroed, 16)
                sp.wait_ge(scattered, 16 * TOP_K * NT)
                sp.dma_start(R["idx"][:, :], slot_tok.rearrange("(b p) a -> p (b a)", p=P)).then_inc(idx_loaded, 16)
                sp.wait_ge(idx_loaded, 16)

            @block.gpsimd
            def _(pool):
                pool.iota(gi[:, :], pattern=[[1, GROUPS]], base=0, channel_multiplier=0, allow_small_or_imprecise_dtypes=True).then_inc(iotas, 1)
                pool.iota(ei[:, :], pattern=[[1, EXPERTS]], base=0, channel_multiplier=0, allow_small_or_imprecise_dtypes=True).then_inc(iotas, 1)
                pool.iota(bi[:, :], pattern=[[1, SLOTS_B]], base=0, channel_multiplier=0, allow_small_or_imprecise_dtypes=True).then_inc(iotas, 1)
                pool.iota(tok[:, :], pattern=[[P, NT]], base=0, channel_multiplier=1).then_inc(iotas, 1)
                pool.memset(zero[:, :], 0).then_inc(iotas, 1)
                pool.wait_ge(iotas, 5)
                pool.wait_ge(zeroed, 16)
                for i in range(TOP_K):
                    pool.wait_ge(dest_ready, i + 1)
                    for t in range(NT):
                        pool.indirect_dma_start(out=slot_tok, out_offset=bass.IndirectOffsetOnAxis(ap=R["dest"][:, i, t:t + 1], axis=0),
                                                in_=tok[:, t:t + 1], in_offset=None).then_inc(scattered, 16)
                pool.wait_ge(scattered, 16 * TOP_K * NT)

            @block.tensor
            def _(pe):
                pe.wait_ge(loaded, 64)
                for t in range(NT):
                    for k in range(KT):
                        mm = pe.matmul(ps[:, 0, t * NL:(t + 1) * NL], hT[:, k, t * P:(t + 1) * P], wr[:, k, :],
                                       start=(k == 0), stop=(k == KT - 1), skip_group_check=True)
                mm.then_inc(logits, 1)
                pe.wait_ge(picked, 1)
                for t in range(NT):
                    for j in range(t + 1):
                        mm = pe.matmul(ps[:, 1, t * EXPERTS:(t + 1) * EXPERTS], K["ones"][:, :] if j < t else K["earlier"][:, :],
                                       both[:, j, :], start=(j == 0), stop=(j == t), skip_group_check=True)
                for j in range(NT):
                    mm = pe.matmul(ps[:, 2, 0:EXPERTS], K["ones"][:, :], both[:, j, :], start=(j == 0), stop=(j == NT - 1))
                mm.then_inc(ranks, 1)

            @block.scalar
            def _(act):
                act.wait_ge(exp_in, 1)
                act.activation(ge[:, :, :], ge[:, :, :], ACT.Exp).then_inc(exp_out, 1)
                act.wait_ge(exp_in, 2)
                act.activation(e2[:, :], e2[:, :], ACT.Exp).then_inc(exp_out, 1)

            @block.vector
            def _(dve):
                link = Chain(dve, chain)

                def over(ap, n):
                    return ap.rearrange("p (t a) -> p t a", a=1).to_broadcast([P, NT, n])

                def each(ap, n):
                    return ap.rearrange("p (a n) -> p a n", a=1).to_broadcast([P, NT, n])

                def first_max(out, vals, m, idx, c, n):
                    link(dve.tensor_tensor(c, vals, over(m, n), ALU.is_equal))
                    link(dve.scalar_tensor_tensor(out=c, in0=c, scalar=-64.0, in1=each(idx, n), op0=ALU.mult, op1=ALU.add))
                    link(dve.tensor_reduce(cmin[:, :], c, AX.X, ALU.min))
                    link(dve.tensor_tensor(out, c, over(cmin[:, :], n), ALU.is_equal))

                dve.wait_ge(loaded, 64)
                dve.wait_ge(iotas, 5)
                dve.wait_ge(logits, 1)
                link(dve.tensor_tensor(L[:, :, :], ps[:, 0, 0:NT * NL].rearrange("p (t n) -> p t n", n=NL), each(brow[:, :], NL), ALU.add))
                gl, el = L[:, :, 0:GROUPS], L[:, :, GROUPS:NL]
                link(dve.tensor_reduce(gmax[:, :], gl, AX.X, ALU.max))
                dve.tensor_tensor(ge[:, :, :], gl, over(gmax[:, :], GROUPS), ALU.subtract).then_inc(exp_in, 1)
                first_max(oh_g[:, :, :], gl, gmax[:, :], gi[:, :], gc[:, :, :], GROUPS)
                link(dve.tensor_scalar(gc[:, :, :], oh_g[:, :, :], 1.0, -NEG, ALU.subtract, ALU.mult))
                for g in range(GROUPS):
                    i = dve.tensor_tensor(em[:, :, g * PER_GROUP:(g + 1) * PER_GROUP], el[:, :, g * PER_GROUP:(g + 1) * PER_GROUP],
                                          gc[:, :, g:g + 1].to_broadcast([P, NT, PER_GROUP]), ALU.add)
                    link(i)
                link(dve.tensor_reduce(top[:, 0, :], em[:, :, :], AX.X, ALU.max))
                first_max(oh[:, 0, :, :], em[:, :, :], top[:, 0, :], ei[:, :], cand[:, :, :], EXPERTS)
                link(dve.scalar_tensor_tensor(out=em[:, :, :], in0=oh[:, 0, :, :], scalar=2.0 * NEG, in1=em[:, :, :], op0=ALU.mult, op1=ALU.add))
                link(dve.tensor_reduce(top[:, 1, :], em[:, :, :], AX.X, ALU.max))
                dve.tensor_tensor(e2[:, :], top[:, 1, :], top[:, 0, :], ALU.subtract).then_inc(exp_in, 1)
                first_max(oh[:, 1, :, :], em[:, :, :], top[:, 1, :], ei[:, :], cand[:, :, :], EXPERTS)
                dve.tensor_tensor(both[:, :, :], oh[:, 0, :, :], oh[:, 1, :, :], ALU.add).then_inc(picked, 1)
                dve.wait_ge(exp_out, 2)
                link(dve.tensor_reduce(gsum[:, :], ge[:, :, :], AX.X, ALU.add))
                link(dve.reciprocal(pg[:, :], gsum[:, :]))
                link(dve.tensor_scalar(den[:, :], e2[:, :], 1.0, None, ALU.add))
                link(dve.reciprocal(den[:, :], den[:, :]))
                link(dve.tensor_tensor(R["gate"][:, 0, :], pg[:, :], den[:, :], ALU.mult))
                link(dve.tensor_tensor(R["gate"][:, 1, :], R["gate"][:, 0, :], e2[:, :], ALU.mult))
                dve.wait_ge(ranks, 1)
                link(dve.tensor_copy(cnt[:, :], ps[:, 2, 0:EXPERTS]))
                link(dve.tensor_scalar(nblk[:, :], cnt[:, :], 0.0, None, ALU.is_gt))
                for j in range(1, S // P):
                    link(dve.scalar_tensor_tensor(out=nblk[:, :], in0=cnt[:, :], scalar=float(j * P), in1=nblk[:, :], op0=ALU.is_gt, op1=ALU.add))
                link(dve.tensor_copy(pend[:, 0, :], nblk[:, :]))
                cur = 0
                for step in (1, 2, 4, 8, 16):
                    link(dve.tensor_copy(pend[:, 1 - cur, 0:step], pend[:, cur, 0:step]))
                    link(dve.tensor_tensor(pend[:, 1 - cur, step:], pend[:, cur, step:], pend[:, cur, 0:EXPERTS - step], ALU.add))
                    cur = 1 - cur
                link(dve.tensor_tensor(nblk[:, :], pend[:, cur, :], nblk[:, :], ALU.subtract))
                link(dve.tensor_scalar(nblk[:, :], nblk[:, :], float(P), None, ALU.mult))
                link(dve.tensor_tensor(rank[:, :, :], ps[:, 1, 0:NT * EXPERTS].rearrange("p (t e) -> p t e", e=EXPERTS), each(nblk[:, :], EXPERTS), ALU.add))
                for i in range(TOP_K):
                    link(dve.tensor_tensor(cand[:, :, :], rank[:, :, :], oh[:, i, :, :], ALU.mult))
                    link(dve.tensor_reduce(dest[:, i, :], cand[:, :, :], AX.X, ALU.add))
                    dve.tensor_copy(R["dest"][:, i, :], dest[:, i, :]).then_inc(dest_ready, 1)
                ends = pend[0:1, cur, :].rearrange("p (a e) -> p a e", a=1).to_broadcast([1, SLOTS_B, EXPERTS])
                link(dve.tensor_tensor(cmp[:, :, :], ends, bi[:, :].rearrange("p (b a) -> p b a", a=1).to_broadcast([1, SLOTS_B, EXPERTS]), ALU.is_le))
                link(dve.tensor_reduce(be[:, :], cmp[:, :, :], AX.X, ALU.add))
                link(dve.tensor_scalar(be[:, :], be[:, :], float(EXPERTS - 1), None, ALU.min))
                link(dve.tensor_copy(R["block_e"][:, :], be[:, :]))
                link(dve.tensor_copy(R["n_blocks"][:, :], pend[0:1, cur, EXPERTS - 1:EXPERTS]))


def experts(nc, K, R, h_dram, y_dram, w_gate, w_up, w_down):
    ps, ident = K["ps"], K["ident"]
    GC = KT // 2
    CH = 2 * GC + FT
    with ExitStack() as ctx:
        sc = Scope(nc, ctx, "moe")
        wg = sc.sb("wg", [P, KT, D_EXP])
        wu = sc.sb("wu", [P, KT, D_EXP])
        wd = sc.sb("wd", [P, FT, D])
        xg = sc.sb("xg", [P, D])
        xT = sc.sb("xT", [P, KT, P])
        idx = sc.sb("idx", [P, 1], I32)
        sil = sc.sb("sil", [P, HALF])
        hid = sc.sb("hid", [P, FT, P])
        hid_parts = sc.sb("hid_parts", [P, 2, FT, P], F32R)
        wd_parts = sc.sb("wd_parts", [P, 2, FT, D], F32R)
        wd_high, wd_split, hid_made = sc.sem("wd_high"), sc.sem("wd_split"), sc.sem("hid_made")
        y = sc.sb("y", [P, D])
        loaded = [sc.sem(f"w{c}") for c in range(CH)]
        used, gathered, idx_ready, xt_made, xt_act, xt_dve, sil_ready, hid_ready, y_act, y_dve, y_stored, settled, settled_act = [sc.sem(n) for n in
            ("used", "gathered", "idx_ready", "xt_made", "xt_act", "xt_dve", "sil_ready", "hid_ready", "y_act", "y_dve", "y_stored", "settled", "settled_act")]
        wg_d = w_gate.rearrange("e (c k p) f -> (e c) p k f", p=P, k=2)
        wu_d = w_up.rearrange("e (c k p) f -> (e c) p k f", p=P, k=2)
        wd_d = w_down.rearrange("e (c p) d -> (e c) p d", p=P)
        nb_ap = R["n_blocks"][0:1, 0:1]
        with nc.Block() as block:
            @block.sync
            def _(sp):
                nb = sp.value_load(nb_ap, min_val=1, max_val=BLOCKS)
                with sp.Fori(0, nb) as i:
                    e = sp.value_load(R["block_e"][0:1, bass.ds(i, 1)], min_val=0, max_val=EXPERTS - 1)
                    for c in range(GC):
                        for which, (dst, src) in enumerate(((wg, wg_d), (wu, wu_d))):
                            n = 2 * c + which
                            sp.wait_ge(used, i * CH + n + 1)
                            sp.dma_start(dst[:, 2 * c:2 * c + 2, :], src[bass.ds(e * GC + c, 1), :, :, :].rearrange("a p k f -> p (a k) f")).then_inc(loaded[n], 16)
                    for f in range(FT):
                        n = 2 * GC + f
                        sp.wait_ge(wd_split, i * FT + f + 1)
                        sp.dma_start(wd[:, f, :], wd_d[bass.ds(e * FT + f, 1), :, :].rearrange("a p d -> p (a d)")).then_inc(loaded[n], 16)

            @block.gpsimd
            def _(pool):
                nb = pool.value_load(nb_ap, min_val=1, max_val=BLOCKS)
                with pool.Fori(0, nb + 1) as i:
                    pool.wait_ge(xt_made, i + 1)
                    pool.tensor_copy(idx[:, :], R["idx"][:, bass.ds(i, 1)]).then_inc(idx_ready, 1)
                    pool.wait_ge(idx_ready, i + 1)
                    pool.sem_inc(settled, 1)
                    pool.indirect_dma_start(out=xg[:, :], out_offset=None, in_=h_dram,
                                            in_offset=bass.IndirectOffsetOnAxis(ap=idx[:, 0:1], axis=0)).then_inc(gathered, 16)
                    pool.wait_ge(gathered, i * 16 + 16)

            def turn(pe):
                for k in range(KT):
                    mm = pe.transpose(ps[:, 4 + k // 4, (k % 4) * P:(k % 4 + 1) * P], xg[:, k * P:(k + 1) * P], ident[:, :])
                mm.then_inc(xt_made, 1)

            @block.tensor
            def _(pe):
                pe.sem_inc(used, CH)
                pe.sem_inc(xt_made, 1)
                pe.wait_ge(gathered, 16)
                turn(pe)
                nb = pe.value_load(nb_ap, min_val=1, max_val=BLOCKS)
                with pe.Fori(0, nb) as i:
                    pe.wait_ge(xt_act, i + 1)
                    pe.wait_ge(xt_dve, i + 1)
                    for c in range(GC):
                        for which, w in enumerate((wg, wu)):
                            pe.wait_ge(loaded[2 * c + which], i * 16 + 16)
                            for k in (2 * c, 2 * c + 1):
                                for f in range(FT):
                                    mm = pe.matmul(ps[:, which, f * P:(f + 1) * P], w[:, k, f * P:(f + 1) * P], xT[:, k, :],
                                                   start=(k == 0 and f == 0), stop=(k == KT - 1), skip_group_check=True)
                            mm.then_inc(used, 1)
                    pe.wait_ge(gathered, i * 16 + 32)
                    turn(pe)
                    pe.wait_ge(y_act, i + 1)
                    pe.wait_ge(y_dve, i + 1)
                    for f in range(FT):
                        pe.wait_ge(wd_split, i * FT + (FT + f + 1))
                        if f % 2 == 0:
                            pe.wait_ge(hid_ready, i * 2 + (f // 2 + 1))
                        for n in range(2):
                            cols = slice(n * HALF, (n + 1) * HALF)
                            mm = multiply_split(pe, ps[:, 2 + n, :], (hid_parts[:, 0, f, :], hid_parts[:, 1, f, :]),
                                                (wd_parts[:, 0, f, cols], wd_parts[:, 1, f, cols]), f == 0, f == FT - 1)
                        mm.then_inc(used, 1)

            @block.scalar
            def _(act):
                act.sem_inc(y_act, 1)
                act.dma_start(y_dram[BLOCKS * P:(BLOCKS + 1) * P, 0:P], ident[:, :]).then_inc(y_stored, 16)
                act.wait_ge(xt_made, 2)
                act.activation(xT[:, 0:4, :], ps[:, 4, :].rearrange("p (k t) -> p k t", t=P), ACT.Copy).then_inc(xt_act, 1)
                nb = act.value_load(nb_ap, min_val=1, max_val=BLOCKS)
                with act.Fori(0, nb) as i:
                    act.wait_ge(used, i * CH + CH)
                    for f in range(FT):
                        act.wait_ge(loaded[2 * GC + f], i * 16 + 16)
                        act.activation(wd_parts[:, 0, f, :], wd[:, f, :], ACT.Copy).then_inc(wd_high, 1)
                    act.wait_ge(used, i * CH + (CH + 2 * GC - 1))
                    act.activation(sil[:, :], ps[:, 0, :], ACT.Silu).then_inc(sil_ready, 1)
                    act.wait_ge(xt_made, i + 3)
                    act.activation(xT[:, 0:4, :], ps[:, 4, :].rearrange("p (k t) -> p k t", t=P), ACT.Copy).then_inc(xt_act, 1)
                    act.wait_ge(used, i * CH + 2 * CH)
                    act.wait_ge(y_stored, i * 16 + 16)
                    act.activation(y[:, 0:HALF], ps[:, 2, :], ACT.Copy).then_inc(y_act, 1)
                    act.wait_ge(y_act, i + 2)
                    act.wait_ge(y_dve, i + 2)
                    act.dma_start(y_dram[bass.ds(i * P, P), :], y[:, :]).then_inc(y_stored, 16)
                act.wait_ge(y_stored, nb * 16 + 16)
                act.sem_inc(settled_act, 1)

            @block.vector
            def _(dve):
                dve.sem_inc(y_dve, 1)
                dve.sem_inc(wd_split, FT)
                dve.wait_ge(xt_made, 2)
                dve.tensor_copy(xT[:, 4:8, :], ps[:, 5, :].rearrange("p (k t) -> p k t", t=P)).then_inc(xt_dve, 1)
                nb = dve.value_load(nb_ap, min_val=1, max_val=BLOCKS)
                with dve.Fori(0, nb) as i:
                    for f in range(FT):
                        dve.wait_ge(wd_high, i * FT + (f + 1))
                        low_part(dve, wd_parts[:, 1, f, :], wd[:, f, :], wd_parts[:, 0, f, :]).then_inc(wd_split, 1)
                    dve.wait_ge(sil_ready, i + 1)
                    dve.wait_ge(used, i * CH + (CH + 2 * GC))
                    for q in range(2):
                        fs, cols = slice(q * FT // 2, (q + 1) * FT // 2), slice(q * HALF // 2, (q + 1) * HALF // 2)
                        dve.tensor_tensor(hid[:, fs, :], sil[:, cols].rearrange("p (f t) -> p f t", t=P),
                                          ps[:, 1, cols].rearrange("p (f t) -> p f t", t=P), ALU.mult).then_inc(hid_made, 1)
                        dve.wait_ge(hid_made, i * 4 + (2 * q + 1))
                        dve.tensor_copy(hid_parts[:, 0, fs, :], hid[:, fs, :]).then_inc(hid_made, 1)
                        dve.wait_ge(hid_made, i * 4 + (2 * q + 2))
                        low_part(dve, hid_parts[:, 1, fs, :], hid[:, fs, :], hid_parts[:, 0, fs, :]).then_inc(hid_ready, 1)
                    dve.wait_ge(xt_made, i + 3)
                    dve.tensor_copy(xT[:, 4:8, :], ps[:, 5, :].rearrange("p (k t) -> p k t", t=P)).then_inc(xt_dve, 1)
                    dve.wait_ge(used, i * CH + 2 * CH)
                    dve.wait_ge(y_stored, i * 16 + 16)
                    dve.tensor_copy(y[:, HALF:D], ps[:, 3, :]).then_inc(y_dve, 1)


def combine(nc, K, R, y_dram):
    X = K["X"]
    DEPTH = 4
    with ExitStack() as ctx:
        sc = Scope(nc, ctx, "comb")
        yg = sc.sb("yg", [P, DEPTH, D])
        squares = sc.sb("squares", [P, 2, D])
        summed = sc.sem("summed")
        got = [sc.sem(f"got{d}") for d in range(DEPTH)]
        added = sc.sem("added")
        order = [(t, i) for t in range(NT) for i in range(TOP_K)]
        with nc.Block() as block:
            @block.gpsimd
            def _(pool):
                for n, (t, i) in enumerate(order):
                    if n >= DEPTH:
                        pool.wait_ge(added, n - DEPTH + 1)
                    pool.indirect_dma_start(out=yg[:, n % DEPTH, :], out_offset=None, in_=y_dram,
                                            in_offset=bass.IndirectOffsetOnAxis(ap=R["dest"][:, i, t:t + 1], axis=0)).then_inc(got[n % DEPTH], 16)

            @block.scalar
            def _(act):
                for t in range(NT):
                    act.wait_ge(added, TOP_K * (t + 1))
                    if t >= 2:
                        act.wait_ge(summed, t - 1)
                    square_sum(act, K, t, squares[:, t % 2, :], summed)

            @block.vector
            def _(dve):
                for n, (t, i) in enumerate(order):
                    dve.wait_ge(got[n % DEPTH], 16 * (n // DEPTH + 1))
                    if i:
                        dve.wait_ge(added, n)
                    dve.scalar_tensor_tensor(out=X[:, t, :], in0=yg[:, n % DEPTH, :], scalar=R["gate"][:, i, t:t + 1], in1=X[:, t, :],
                                             op0=ALU.mult, op1=ALU.add).then_inc(added, 1)


def bias_tables(nc, K, T, G_dram, rel_bias, onehot, which):
    ps = K["ps"]
    with ExitStack() as ctx:
        sc = Scope(nc, ctx, f"bias{which}")
        rb = sc.sb("rb", [BUCKETS + 1, A_HEADS + B_HEADS])
        oh = sc.sb("oh", [BUCKETS + 1, len(DILATIONS), BAND])
        strip = sc.sb("strip", [A_HEADS + B_HEADS, len(DILATIONS), BAND])
        anti, anti64 = sc.sb("anti", [P, P]), sc.sb("anti64", [64, P])
        rev = sc.sb("rev", [P, 4, HALF])
        rev16 = sc.sb("rev16", [64, B_HEADS, 64])
        loaded, rb_ready, antis, made, strips, written, rev_in, out_sem = [sc.sem(n) for n in
            ("loaded", "rb_ready", "antis", "made", "strips", "written", "rev_in", "out")]
        rev_loaded = [sc.sem(f"rev_loaded{i}") for i in range(4)]
        if which == "A":
            jobs = [(T["A"], 0, h, h) for h in range(0, A_HEADS, 2)]
        else:
            jobs = [(T[f"B{c}"], c, A_HEADS + h, h) for c in range(2) for h in range(0, B_HEADS, 2)]
        NJ = len(jobs)
        NS = 3 if which == "A" else 0
        with nc.Block() as block:
            @block.sync
            def _(sp):
                if NS:
                    sp.dma_start(rb[0:BUCKETS, :], rel_bias).then_inc(loaded, 16)
                    sp.dma_start(oh[:, :, :], onehot).then_inc(loaded, 16)
                    sp.wait_ge(strips, 3)
                    sp.dma_start(G_dram, strip[:, :, :]).then_inc(written, 16)
                    sp.wait_ge(written, 16)
                for n, (table, c, h, slot) in enumerate(jobs):
                    if n >= 4:
                        sp.wait_ge(made, NS + n - 3)
                    base = G_dram[h:h + 2, c, 0:1]
                    src = bass.AP(tensor=base.tensor, offset=base.offset, ap=[[1, P], [len(DILATIONS) * BAND, 2], [1, 2 * P]])
                    sp.dma_start(rev[:, n % 4, :].rearrange("p (h j) -> p h j", h=2), src).then_inc(rev_loaded[n % 4], 16)
                if which == "B":
                    base = G_dram[A_HEADS:A_HEADS + 1, 2, 192:193]
                    src = bass.AP(tensor=base.tensor, offset=base.offset, ap=[[1, 64], [len(DILATIONS) * BAND, B_HEADS], [1, 64]])
                    sp.dma_start(rev16[:, :, :], src).then_inc(rev_in, 16)

            @block.gpsimd
            def _(pool):
                if NS:
                    pool.memset(rb[BUCKETS:BUCKETS + 1, :], NEG).then_inc(rb_ready, 1)
                    pool.wait_ge(rb_ready, 1)
                pool.memset(anti[:, :], 0.0).then_inc(antis, 1)
                pool.memset(anti64[:, :], 0.0).then_inc(antis, 1)
                pool.wait_ge(antis, 2)
                pool.affine_select(out=anti[:, :], in_=anti[:, :], compare_op=ALU.not_equal, fill=1.0, base=1 - P,
                                   pattern=[[1, P]], channel_multiplier=1).then_inc(antis, 1)
                pool.affine_select(out=anti64[:, :].rearrange("p (a n) -> p a n", a=2), in_=anti64[:, :].rearrange("p (a n) -> p a n", a=2),
                                   compare_op=ALU.not_equal, fill=1.0, base=-63, pattern=[[0, 2], [1, 64]], channel_multiplier=1).then_inc(antis, 1)

            @block.tensor
            def _(pe):
                if NS:
                    pe.wait_ge(loaded, 32)
                    pe.wait_ge(rb_ready, 1)
                for c in range(NS):
                    pe.matmul(ps[0:A_HEADS + B_HEADS, c, 0:BAND], rb[:, :], oh[:, c, :], start=True, stop=True).then_inc(made, 1)
                pe.wait_ge(antis, 4)
                for n in range(NJ):
                    pe.wait_ge(rev_loaded[n % 4], 16 * (n // 4 + 1))
                    if n >= 4:
                        pe.wait_ge(out_sem, n - 3)
                    pe.matmul(ps[:, 4 + n % 4, :], anti[:, :], rev[:, n % 4, :], start=True, stop=True).then_inc(made, 1)
                if which == "B":
                    pe.wait_ge(rev_in, 16)
                    pe.wait_ge(out_sem, NJ - 3)
                    pe.matmul(ps[:, 4 + NJ % 4, :], anti64[:, :], rev16[:, :, :], start=True, stop=True).then_inc(made, 1)

            @block.scalar
            def _(act):
                for c in range(NS):
                    act.wait_ge(made, c + 1)
                    act.activation(strip[:, c, :], ps[0:A_HEADS + B_HEADS, c, 0:BAND], ACT.Copy, scale=1.0 / SC_AB).then_inc(strips, 1)
                for n, (table, c, h, slot) in enumerate(jobs):
                    act.wait_ge(made, NS + n + 1)
                    act.activation(table[:, slot:slot + 2, :], ps[:, 4 + n % 4, :].rearrange("p (h j) -> p h j", h=2), ACT.Copy).then_inc(out_sem, 1)
                if which == "B":
                    act.wait_ge(made, NS + NJ + 1)
                    act.activation(T["B2"][:, :, :], ps[:, 4 + NJ % 4, :].rearrange("p (h j) -> p h j", j=64), ACT.Copy).then_inc(out_sem, 1)


def split_weights(sc, slots, width, steps):
    return {"raw": sc.sb("raw", [P, 3, KT, width]), "w": sc.sb("w", [P, slots, 2, KT, width], F32R), "slots": slots,
            "loaded": [sc.sem(f"w{i}") for i in range(3)], "high": sc.sem("w_high"), "split": sc.sem("w_split"),
            "free": sc.sem("slot_free"), "steps": steps}


def high_weights(act, W, n):
    act.wait_ge(W["loaded"][n % 3], W["steps"][n])
    if n >= W["slots"]:
        act.wait_ge(W["free"], n - W["slots"] + 1)
    act.activation(W["w"][:, n % W["slots"], 0, :, :], W["raw"][:, n % 3, :, :], ACT.Copy).then_inc(W["high"], 1)


def low_weights(dve, W, n):
    dve.wait_ge(W["high"], n + 1)
    s = n % W["slots"]
    low_part(dve, W["w"][:, s, 1, :, :], W["raw"][:, n % 3, :, :], W["w"][:, s, 0, :, :]).then_inc(W["split"], 1)


def ab_projections(nc, K, B, h, oT, w_in, vb_dram):
    ps = K["ps"]
    SLOTS = 4
    AHEAD = 3
    with ExitStack() as ctx:
        sc = Scope(nc, ctx, "abp")
        vs = sc.sb("vs", [P, 2, HALF])
        made, evac = sc.sem("made"), sc.sem("evac")
        v_stored = [sc.sem("v_stored0"), sc.sem("v_stored1")]
        tiles = [("qa", i, None) for i in range(4)]
        tiles += [("vb", i, COL_VB + i * P) for i in range(4)] + [("ka", 0, COL_KA), ("va", 0, COL_VA)]
        tiles += [("qb", i, COL_QB + i * P) for i in range(4)] + [("kb", i, COL_KB + i * P) for i in range(4)]
        tiles += [("z", i, COL_Z + i * P) for i in range(KT)]
        dma_of = [0] * 3
        steps = []
        for n, (kind, i, col) in enumerate(tiles):
            dma_of[n % 3] += 2 if kind == "qa" else 1
            steps.append(16 * dma_of[n % 3])
        W = split_weights(sc, SLOTS, P, steps)
        w, raw = W["w"], W["raw"]
        units = []
        for n, (kind, i, col) in enumerate(tiles):
            if kind in ("qa", "ka", "qb", "kb", "z"):
                dst = {"qa": B["qa"], "ka": B["ka"], "qb": B["qb"], "kb": B["kb"], "z": oT}[kind]
                units += [(n, dst[:, i, half * HALF:(half + 1) * HALF]) for half in range(NH)]
            elif kind == "va":
                units += [(n, t) for t in range(NT)]
            elif i == 3:
                units += [(n, t) for t in range(NT)]
        tile_end = [0] * len(tiles)
        for n, (kind, i, col) in enumerate(tiles):
            last = n - i + 3 if kind == "vb" else n
            tile_end[n] = max(u for u, (m, dst) in enumerate(units) if m == last) + 1

        with nc.Block() as block:
            @block.sync
            def _(sp):
                for n, (kind, i, col) in enumerate(tiles):
                    if n >= 3:
                        sp.wait_ge(W["split"], n - 2)
                    s = n % 3
                    if kind == "qa":
                        for j in range(2):
                            c0 = COL_QA + (i + 4 * j) * HD
                            sp.dma_start(raw[:, s, :, j * HD:(j + 1) * HD], tiled_rows(w_in[:, c0:c0 + HD])).then_inc(W["loaded"][s], 16)
                    else:
                        sp.dma_start(raw[:, s, :, :], tiled_rows(w_in[:, col:col + P])).then_inc(W["loaded"][s], 16)

            @block.tensor
            def _(pe):
                u = 0
                for n, (kind, i, col) in enumerate(tiles):
                    s = n % SLOTS
                    pe.wait_ge(W["split"], n + 1)
                    if kind in ("qa", "ka", "qb", "kb", "z"):
                        for half in range(NH):
                            if u >= 8:
                                pe.wait_ge(evac, u - 7)
                            cols = slice(half * HALF, (half + 1) * HALF)
                            for k in range(KT):
                                mm = multiply_split(pe, ps[:, u % 8, :], (w[:, s, 0, k, :], w[:, s, 1, k, :]), (h[:, 0, k, cols], h[:, 1, k, cols]),
                                                    k == 0, k == KT - 1)
                            mm.then_inc(made, 1)
                            u += 1
                        pe.wait_ge(made, u)
                        pe.sem_inc(W["free"], 1)
                    elif kind == "va" or i == 3:
                        for t in range(NT):
                            pe.wait_ge(evac, u - 7)
                            cols = slice(t * P, (t + 1) * P)
                            for k in range(KT):
                                right = (w[:, s, 0, k, :], w[:, s, 1, k, :]) if kind == "va" else (w[:, :, 0, k, :], w[:, :, 1, k, :])
                                mm = multiply_split(pe, ps[:, u % 8, 0:P if kind == "va" else HALF], (h[:, 0, k, cols], h[:, 1, k, cols]), right,
                                                    k == 0, k == KT - 1)
                            mm.then_inc(made, 1)
                            u += 1
                        pe.wait_ge(made, u)
                        pe.sem_inc(W["free"], 1 if kind == "va" else 4)

            @block.scalar
            def _(act):
                split = 0
                for u, (n, dst) in enumerate(units):
                    kind = tiles[n][0]
                    while split < min(len(tiles), n + 1 + AHEAD) and (split < SLOTS or tile_end[split - SLOTS] <= u):
                        high_weights(act, W, split)
                        split += 1
                    act.wait_ge(made, u + 1)
                    if kind == "va":
                        act.activation(B["va"][:, dst, :], ps[:, u % 8, 0:P], ACT.Copy).then_inc(evac, 1)
                    elif kind == "vb":
                        if dst >= 2:
                            act.wait_ge(v_stored[dst % 2], 16 * (dst // 2))
                        act.activation(vs[:, dst % 2, :], ps[:, u % 8, :], ACT.Copy).then_inc(evac, 1)
                        act.wait_ge(evac, u + 1)
                        act.dma_start(vb_dram[dst * P:(dst + 1) * P, :], vs[:, dst % 2, :]).then_inc(v_stored[dst % 2], 16)
                    else:
                        act.activation(dst, ps[:, u % 8, :], ACT.Silu if kind == "z" else ACT.Copy).then_inc(evac, 1)
                for stored in v_stored:
                    act.wait_ge(stored, 16 * NT // 2)

            @block.vector
            def _(dve):
                for n in range(len(tiles)):
                    low_weights(dve, W, n)


def banded_attention(nc, K, B, T, oT, which, vb_dram, sinks):
    ps, ident = K["ps"], K["ident"]
    GU = 4
    dil = which == "B"
    with ExitStack() as ctx:
        sc = Scope(nc, ctx, f"att{which}")
        s_sb = sc.sb("s", [P, 2, GU, 2 * P])
        pT = sc.sb("pT", [P, 2, GU, 2 * P])
        mx, rsum, es, rden = [sc.sb(n, [P, 2, GU]) for n in ("mx", "rsum", "es", "rden")]
        LB = 4
        nm, den, lse = [sc.sb(n, [P, 2, LB, GU]) for n in ("nm", "den", "lse")]

        def kept(a, g):
            return a[:, g // LB % 2, g % LB, :]

        if dil:
            v1 = sc.sb("v1", [P, 2, NT, P])
            v4 = sc.sb("v4", [P, 2, 4, 2, P])
            v16 = sc.sb("v16", [64, 2, 16, P])
            oc = sc.sb("oc", [P, 2, 3, S])
            lb = sc.sb("lb", [P, 2, 3, S])
            top = sc.sb("top", [P, S])
            v_loaded = [sc.sem("v_loaded0"), sc.sem("v_loaded1")]
        else:
            sk = sc.sb("sk", [P, A_HEADS])
            sk_loaded = sc.sem("sk_loaded")
        s_made, s_taken, m_ready, p_ready, n_ready, turned, pt_act, pt_dve, o_made, o_out, chain, mixed, exp_in, exp_out, l_made = [sc.sem(n) for n in
            ("s_made", "s_taken", "m_ready", "p_ready", "n_ready", "turned", "pt_act", "pt_dve", "o_made", "o_out", "chain", "mixed", "exp_in", "exp_out", "l_made")]
        sum_ready, logged, inverse_ready = sc.sem("sum_ready"), sc.sem("logged"), sc.sem("inverse_ready")
        lse_ready, l_copied = sc.sem("lse_ready"), sc.sem("l_copied")
        ln_ready, o_copied, topped, pool_chain = sc.sem("ln_ready"), sc.sem("o_copied"), sc.sem("topped"), sc.sem("pool_chain")

        groups = []
        for h in range(B_HEADS if dil else A_HEADS):
            if not dil:
                tile_i, half = h % 4, h // 4
                row = slice(half * HD, (half + 1) * HD)
                q, k = B["qa"][row, tile_i, :], B["ka"][row, 0, :]
                for g in range(2):
                    units = []
                    for i in range(4 * g, 4 * g + 4):
                        k0 = max(i - 1, 0) * P
                        nk = (i + 1) * P - k0
                        vals = [(B["va"][:, k0 // P + b, half * HD:(half + 1) * HD], P, b * P, slice(0, P)) for b in range(nk // P)]
                        units.append(([(0, P, q[:, i * P:(i + 1) * P], k[:, k0:k0 + nk])], nk, T["A"][:, h, 2 * P - nk:], vals))
                    groups.append((h, 0, units, oT[(h % 2) * HD:(h % 2 + 1) * HD, h // 2, g * HALF:(g + 1) * HALF], lambda a: a))
                continue
            row = slice((h % 2) * HD, (h % 2 + 1) * HD)
            q, k = B["qb"][row, h // 2, :], B["kb"][row, h // 2, :]
            vslot, vcol = (h // 2) % 2, slice((h % 2) * HD, (h % 2 + 1) * HD)
            for g in range(2):
                units = []
                for i in range(4 * g, 4 * g + 4):
                    k0 = max(i - 1, 0) * P
                    nk = (i + 1) * P - k0
                    vals = [(v1[:, vslot, k0 // P + b, vcol], P, b * P, slice(0, P)) for b in range(nk // P)]
                    units.append(([(0, P, q[:, i * P:(i + 1) * P], k[:, k0:k0 + nk])], nk, T["B0"][:, h, 2 * P - nk:], vals))
                dst = slice(g * HALF, (g + 1) * HALF)
                groups.append((h, 0, units, (lambda a, dst=dst: a[:, dst]), lambda a: a))
            q4, k4 = q.rearrange("p (m r) -> p r m", r=4), k.rearrange("p (m r) -> p r m", r=4)
            for g in range(2):
                units = []
                for r in (2 * g, 2 * g + 1):
                    for n in range(2):
                        nk = (n + 1) * P
                        vals = [(v4[:, vslot, r, b, vcol], P, b * P, slice(0, P)) for b in range(n + 1)]
                        units.append(([(0, P, q4[:, r, n * P:(n + 1) * P], k4[:, r, 0:nk])], nk, T["B1"][:, h, 2 * P - nk:], vals))
                groups.append((h, 1, units, (lambda a, g=g: a.rearrange("p (m r) -> p r m", r=4)[:, 2 * g:2 * g + 2, :]),
                               lambda a: a.rearrange("p (r m) -> p r m", r=2)))
            q16, k16 = q.rearrange("p (j r) -> p r j", r=16), k.rearrange("p (j r) -> p r j", r=16)
            for g in range(2):
                units = []
                for r in range(8 * g, 8 * g + 8, 2):
                    parts = [(0, 64, q16[:, r, :], k16[:, r, :]), (64, 64, q16[:, r + 1, :], k16[:, r + 1, :])]
                    vals = [(v16[:, vslot, r + j, vcol], 64, 0, slice(64 * j, 64 * j + 64)) for j in range(2)]
                    units.append((parts, 64, T["B2"][:, h, :], vals))
                groups.append((h, 2, units, (lambda a, g=g: a.rearrange("p (j r) -> p r j", r=16)[:, 8 * g:8 * g + 8, :]),
                               lambda a: a.rearrange("p (r j) -> p r j", j=64)))
        NG = len(groups)
        PER_PAIR = 12
        INVERSE_AT = 11
        EXP_AT = 8

        def sbank(g, u):
            return ps[:, 2 * (g % 2) + u // 2, (u % 2) * 2 * P:(u % 2) * 2 * P + 2 * P]

        def mix(engine, link, pair):
            o, l = oc[:, pair % 2, :, :], lb[:, pair % 2, :, :]
            dst = oT[:, A_WIDTH // P + pair, :]
            engine.wait_ge(topped, pair + 1)
            engine.tensor_tensor(l, l, top[:, :].rearrange("p (a n) -> p a n", a=1).to_broadcast([P, 3, S]), ALU.subtract).then_inc(exp_in, 1)
            engine.wait_ge(exp_out, pair + 1)
            link(engine.tensor_tensor(o, o, l, ALU.mult))
            link(engine.tensor_tensor(l[:, 0, :], l[:, 0, :], l[:, 1, :], ALU.add))
            engine.tensor_tensor(l[:, 0, :], l[:, 0, :], l[:, 2, :], ALU.add).then_inc(sum_ready, 1)
            link(engine.tensor_tensor(o[:, 0, :], o[:, 0, :], o[:, 1, :], ALU.add))
            link(engine.tensor_tensor(o[:, 0, :], o[:, 0, :], o[:, 2, :], ALU.add))
            link(engine.tensor_tensor(o[:, 0, :], o[:, 0, :], dst, ALU.mult))
            engine.wait_ge(inverse_ready, pair + 1)
            engine.tensor_tensor(dst, o[:, 0, :], l[:, 0, :], ALU.mult).then_inc(mixed, 1)

        with nc.Block() as block:
            @block.sync
            def _(sp):
                if dil:
                    rows = vb_dram.rearrange("(i p) n -> p i n", p=P)
                    rows4 = vb_dram.rearrange("(n j r) c -> j r n c", r=4, n=2)
                    rows16 = vb_dram.rearrange("(j r) c -> j r c", r=16)
                    for pair in range(B_HEADS // 2):
                        if pair >= 2:
                            sp.wait_ge(o_made, PER_PAIR * (pair - 1))
                        c = slice(pair * P, (pair + 1) * P)
                        s = pair % 2
                        sp.dma_start(v1[:, s, :, :], rows[:, :, c]).then_inc(v_loaded[s], 16)
                        for n in range(2):
                            sp.dma_start(v4[:, s, :, n, :], rows4[:, :, n, c]).then_inc(v_loaded[s], 16)
                        sp.dma_start(v16[:, s, :, :], rows16[:, :, c]).then_inc(v_loaded[s], 16)
                else:
                    sp.dma_start(sk[:, :], sinks.partition_broadcast(P)).then_inc(sk_loaded, 16)

            @block.tensor
            def _(pe):
                def scores(g):
                    if g >= 2:
                        pe.wait_ge(s_taken, g - 1)
                    for u, (parts, nk, bias, vals) in enumerate(groups[g][2]):
                        for off, nq, q, k in parts:
                            mm = pe.matmul(sbank(g, u)[off:off + nq, 0:nk], q, k, start=True, stop=True, skip_group_check=True)
                    mm.then_inc(s_made, 1)

                def turn(g):
                    pe.wait_ge(n_ready, g + 1)
                    if g >= 1:
                        pe.wait_ge(pt_act, g)
                        pe.wait_ge(pt_dve, g)
                    for u, (parts, nk, bias, vals) in enumerate(groups[g][2]):
                        for b in range((nk + P - 1) // P):
                            w = min(P, nk - b * P)
                            mm = pe.transpose(ps[0:w, 4 + u // 2, (u % 2) * 2 * P + b * P:(u % 2) * 2 * P + (b + 1) * P],
                                              s_sb[:, g % 2, u, b * P:b * P + w], ident[:, :])
                    mm.then_inc(turned, 1)

                def values(g):
                    h = groups[g][0]
                    pe.wait_ge(pt_act, g + 1)
                    pe.wait_ge(pt_dve, g + 1)
                    if dil:
                        pair = h // 2
                        pe.wait_ge(v_loaded[pair % 2], 64 * (pair // 2 + 1))
                    if g >= 1:
                        pe.wait_ge(o_out, g)
                    orow = slice((h % 2) * HD, (h % 2 + 1) * HD)
                    for u, (parts, nk, bias, vals) in enumerate(groups[g][2]):
                        for n, (v, rows, off, cols) in enumerate(vals):
                            one = len(parts) == 2
                            mm = pe.matmul(ps[orow, 6, u * P + cols.start:u * P + cols.stop], v, pT[0:rows, g % 2, u, off + cols.start:off + cols.stop],
                                           start=(one or n == 0), stop=(one or n == len(vals) - 1), skip_group_check=True)
                    if dil and g >= LB:
                        mm = spread(g - LB)
                    mm.then_inc(o_made, 1)

                def spread(g):
                    h = groups[g][0]
                    pe.wait_ge(lse_ready, g // LB + 1)
                    for u in range(GU):
                        mm = pe.matmul(ps[(h % 2) * HD:(h % 2 + 1) * HD, 7, u * P:(u + 1) * P], kept(lse, g)[:, u:u + 1].to_broadcast([P, HD]), ident[:, :],
                                       start=True, stop=True, skip_group_check=True)
                    return mm

                scores(0)
                if NG > 1:
                    scores(1)
                for g in range(NG):
                    if g + 2 < NG:
                        scores(g + 2)
                    if g >= 1:
                        values(g - 1)
                    turn(g)
                values(NG - 1)
                for g in range(NG - LB if dil else NG, NG):
                    pe.wait_ge(o_out, g + LB)
                    spread(g).then_inc(o_made, 1)

            @block.scalar
            def _(act):
                def probabilities(g):
                    act.wait_ge(m_ready, g + 1)
                    for u, (parts, nk, bias, vals) in enumerate(groups[g][2]):
                        i = act.activation(s_sb[:, g % 2, u, 0:nk], s_sb[:, g % 2, u, 0:nk], ACT.Exp, bias=kept(nm, g)[:, u:u + 1],
                                           accum_out=rsum[:, g % 2, u:u + 1])
                        if u == GU - 1 and dil:
                            i.then_inc(p_ready, 1)
                    if not dil:
                        h = groups[g][0]
                        act.activation(es[:, g % 2, :], kept(nm, g), ACT.Exp, bias=sk[:, h:h + 1]).then_inc(p_ready, 1)

                def take_turned(g):
                    act.wait_ge(turned, g + 1)
                    if g >= 2:
                        act.wait_ge(o_made, g - 1)
                    act_copy(g)

                def act_copy(g):
                    units = groups[g][2]
                    for u in range(2):
                        nk = units[u][1]
                        rows = min(nk, P)
                        w = max(nk, P)
                        i = act.activation(pT[0:rows, g % 2, u, 0:w], ps[0:rows, 4, u * 2 * P:u * 2 * P + w], ACT.Copy)
                    i.then_inc(pt_act, 1)

                def weights_of_pair(pair):
                    act.wait_ge(exp_in, pair + 1)
                    act.activation(lb[:, pair % 2, :, :], lb[:, pair % 2, :, :], ACT.Exp).then_inc(exp_out, 1)

                def inverse_of_pair(pair):
                    act.wait_ge(sum_ready, pair + 1)
                    total = lb[:, pair % 2, 0, :]
                    act.activation(total, total, ACT.Ln).then_inc(logged, 1)
                    act.wait_ge(logged, pair + 1)
                    act.activation(total, total, ACT.Exp, scale=-1.0).then_inc(inverse_ready, 1)

                def log_denominators(batch):
                    act.wait_ge(n_ready, LB * (batch + 1))
                    if batch >= 2:
                        act.wait_ge(o_made, LB * batch)
                    act.activation(lse[:, batch % 2, :, :], den[:, batch % 2, :, :], ACT.Ln).then_inc(ln_ready, 1)

                if not dil:
                    act.wait_ge(sk_loaded, 16)
                probabilities(0)
                for g in range(NG):
                    if g >= 1:
                        take_turned(g - 1)
                    if dil and g % PER_PAIR == EXP_AT and g > PER_PAIR:
                        weights_of_pair(g // PER_PAIR - 1)
                    if dil and g % PER_PAIR == INVERSE_AT and g > PER_PAIR:
                        inverse_of_pair(g // PER_PAIR - 1)
                    if g + 1 < NG:
                        probabilities(g + 1)
                    if dil and g % LB == LB - 1:
                        log_denominators(g // LB)
                take_turned(NG - 1)
                if dil:
                    weights_of_pair(NG // PER_PAIR - 1)
                    inverse_of_pair(NG // PER_PAIR - 1)

            @block.vector
            def _(dve):
                link = Chain(dve, chain)

                def maxima(g):
                    dve.wait_ge(s_made, g + 1)
                    if g >= 2:
                        dve.wait_ge(turned, g - 1)
                    h = groups[g][0]
                    for u, (parts, nk, bias, vals) in enumerate(groups[g][2]):
                        i = dve.tensor_tensor_reduce(s_sb[:, g % 2, u, 0:nk], sbank(g, u)[:, 0:nk], bias, SC_AB, NEG, ALU.add, ALU.max,
                                                     mx[:, g % 2, u:u + 1])
                    i.then_inc(s_taken, 1)
                    dve.wait_ge(s_taken, g + 1)
                    if dil:
                        dve.tensor_scalar(kept(nm, g), mx[:, g % 2, :], -1.0, None, ALU.mult).then_inc(m_ready, 1)
                    else:
                        dve.tensor_scalar(kept(nm, g), mx[:, g % 2, :], sk[:, h:h + 1], -1.0, ALU.max, ALU.mult).then_inc(m_ready, 1)

                def normalise(g):
                    dve.wait_ge(p_ready, g + 1)
                    if dil:
                        if g >= 2 * LB:
                            dve.wait_ge(ln_ready, g // LB - 1)
                        link(dve.tensor_copy(kept(den, g), rsum[:, g % 2, :]))
                    else:
                        link(dve.tensor_tensor(kept(den, g), rsum[:, g % 2, :], es[:, g % 2, :], ALU.add))
                    link(dve.reciprocal(rden[:, g % 2, :], kept(den, g)))
                    for u, (parts, nk, bias, vals) in enumerate(groups[g][2]):
                        i = dve.tensor_scalar(s_sb[:, g % 2, u, 0:nk], s_sb[:, g % 2, u, 0:nk], rden[:, g % 2, u:u + 1], None, ALU.mult)
                    i.then_inc(n_ready, 1)

                def take_turned(g):
                    dve.wait_ge(turned, g + 1)
                    if g >= 2:
                        dve.wait_ge(o_made, g - 1)
                    units = groups[g][2]
                    for u in range(2, 4):
                        nk = units[u][1]
                        rows = min(nk, P)
                        w = max(nk, P)
                        i = dve.tensor_copy(pT[0:rows, g % 2, u, 0:w], ps[0:rows, 5, (u - 2) * 2 * P:(u - 2) * 2 * P + w])
                    i.then_inc(pt_dve, 1)

                def log_denominators(batch):
                    dve.wait_ge(ln_ready, batch + 1)
                    slot = lse[:, batch % 2, :, :]
                    dve.tensor_tensor(slot, slot, nm[:, batch % 2, :, :], ALU.subtract).then_inc(lse_ready, 1)

                def take_spread(g):
                    h, c, units, dst, view = groups[g]
                    orow = slice((h % 2) * HD, (h % 2 + 1) * HD)
                    pair = g // PER_PAIR
                    l = lb[:, pair % 2, :, :]
                    dve.tensor_copy(dst(l[orow, c, :]), view(ps[orow, 7, :])).then_inc(l_copied, 1)
                    dve.wait_ge(l_copied, g + 1)
                    if g % PER_PAIR == PER_PAIR - 1:
                        if pair:
                            dve.wait_ge(exp_in, pair)
                        link(dve.tensor_tensor(top[:, :], l[:, 0, :], l[:, 1, :], ALU.max))
                        dve.tensor_tensor(top[:, :], top[:, :], l[:, 2, :], ALU.max).then_inc(topped, 1)

                def take_out(g):
                    h, c, units, dst, view = groups[g]
                    dve.wait_ge(o_made, g + 1)
                    orow = slice((h % 2) * HD, (h % 2 + 1) * HD)
                    if not dil:
                        dve.tensor_tensor(dst, ps[orow, 6, :], dst, ALU.mult).then_inc(o_out, 1)
                        return
                    slot = g // PER_PAIR % 2
                    if g % PER_PAIR == 0 and g >= 2 * PER_PAIR:
                        dve.wait_ge(mixed, g // PER_PAIR - 1)
                    dve.tensor_copy(dst(oc[orow, slot, c, :]), view(ps[orow, 6, :])).then_inc(o_copied, 1)
                    if g >= LB:
                        take_spread(g - LB)
                    dve.wait_ge(o_copied, g + 1)
                    dve.sem_inc(o_out, 1)

                if not dil:
                    dve.wait_ge(sk_loaded, 16)
                maxima(0)
                for g in range(NG):
                    if dil and g % LB == 1 and g > LB:
                        log_denominators(g // LB - 1)
                    if g >= 1:
                        take_turned(g - 1)
                    if g + 1 < NG:
                        maxima(g + 1)
                    normalise(g)
                    if g >= 1:
                        take_out(g - 1)
                take_turned(NG - 1)
                if dil:
                    log_denominators(NG // LB - 1)
                take_out(NG - 1)
                for g in range(NG - LB if dil else NG, NG):
                    dve.wait_ge(o_made, g + LB + 1)
                    take_spread(g)
                    dve.sem_inc(o_out, 1)
                if dil:
                    mix(dve, link, NG // PER_PAIR - 1)

            @block.gpsimd
            def _(pool):
                link = Chain(pool, pool_chain)
                for pair in range(NG // PER_PAIR - 1 if dil else 0):
                    mix(pool, link, pair)


def gate(nc, K, h, oT, w_in, col, tag, x_dram):
    ps = K["ps"]
    with ExitStack() as ctx:
        sc = Scope(nc, ctx, tag)
        W = split_weights(sc, 2, P, [16 * (n // 3 + 1) for n in range(KT)])
        w, raw = W["w"], W["raw"]
        x_stored, done, out_sem = sc.sem("x_stored"), sc.sem("done"), sc.sem("out")
        with nc.Block() as block:
            @block.sync
            def _(sp):
                for j in range(KT):
                    if j >= 3:
                        sp.wait_ge(W["split"], j - 2)
                    sp.dma_start(raw[:, j % 3, :, :], tiled_rows(w_in[:, col + j * P:col + (j + 1) * P])).then_inc(W["loaded"][j % 3], 16)
                for t in range(NT):
                    sp.dma_start(x_dram[t * P:(t + 1) * P, :], K["X"][:, t, :]).then_inc(x_stored, 16)
                sp.wait_ge(x_stored, 16 * NT)

            @block.tensor
            def _(pe):
                for j in range(KT):
                    pe.wait_ge(W["split"], j + 1)
                    for half in range(NH):
                        u = 2 * j + half
                        if u >= 8:
                            pe.wait_ge(out_sem, u - 7)
                        cols = slice(half * HALF, (half + 1) * HALF)
                        for k in range(KT):
                            mm = multiply_split(pe, ps[:, u % 8, :], (w[:, j % 2, 0, k, :], w[:, j % 2, 1, k, :]), (h[:, 0, k, cols], h[:, 1, k, cols]),
                                                k == 0, k == KT - 1)
                        mm.then_inc(done, 1)
                    pe.wait_ge(done, 2 * j + 2)
                    pe.sem_inc(W["free"], 1)

            @block.scalar
            def _(act):
                high_weights(act, W, 0)
                high_weights(act, W, 1)
                for u in range(2 * KT):
                    act.wait_ge(done, u + 1)
                    if u % 2 == 1 and u // 2 + 2 < KT:
                        high_weights(act, W, u // 2 + 2)
                    act.activation(oT[:, u // 2, (u % 2) * HALF:(u % 2 + 1) * HALF], ps[:, u % 8, :], ACT.Silu).then_inc(out_sem, 1)

            @block.vector
            def _(dve):
                for n in range(KT):
                    low_weights(dve, W, n)


def latents(nc, K, C, h, w_in, q_norm, kv_norm, positions, inv_freq):
    ps, ident = K["ps"], K["ident"]
    with ExitStack() as ctx:
        sc = Scope(nc, ctx, "lat")
        raw = sc.sb("raw", [P, 2, C_LAT])
        w = sc.sb("w", [P, 2, KT, C_LAT], F32R)
        ck = K["X"][:, :, 0:C_LAT]
        sq = sc.sb("sq", [P, C_QR])
        kp = sc.sb("kp", [P, NT, C_QK])
        gq, gkv = sc.sb("gq", [P, QR_T]), sc.sb("gkv", [P, 1])
        ss, var, std, rs = [sc.sb(n, [P, 2, NT]) for n in ("ss", "var", "std", "rs")]
        pos_i, pos = sc.sb("pos_i", [P, NT], I32), sc.sb("pos", [P, NT])
        fr = sc.sb("fr", [P, ROPE_HALF])
        ang, turns, red, mag = [sc.sb(n, [P, NT, ROPE_HALF]) for n in ("ang", "turns", "red", "mag")]
        ra, rb = [sc.sb(n, [P, NT, ROPE_HALF]) for n in ("ra", "rb")]
        loaded, made, copied, summed, var_ready, std_ready, ang_ready, tables, scaled, roped, turned, chain, out_act, out_dve = [sc.sem(n) for n in
            ("loaded", "made", "copied", "summed", "var_ready", "std_ready", "ang_ready", "tables", "scaled", "roped", "turned", "chain", "out_act", "out_dve")]
        cs, sn = C["cos"], C["sin"]
        raw_loaded, w_high, w_split = [sc.sem("raw0"), sc.sem("raw1")], sc.sem("w_high"), sc.sem("w_split")
        n_loads = 5
        with nc.Block() as block:
            @block.sync
            def _(sp):
                for k in range(KT):
                    if k >= 2:
                        sp.wait_ge(w_split, k - 1)
                    sp.dma_start(raw[:, k % 2, :], w_in[k * P:(k + 1) * P, 0:C_LAT]).then_inc(raw_loaded[k % 2], 16)
                sp.dma_start(pos_i[:, :], positions.rearrange("(t p) -> p t", p=P)).then_inc(loaded, 16)
                sp.dma_start(fr[:, :], inv_freq.partition_broadcast(P)).then_inc(loaded, 16)
                sp.dma_start(gq[:, :], q_norm.rearrange("(k p) -> p k", p=P)).then_inc(loaded, 16)
                sp.dma_start(gkv[:, :], kv_norm.rearrange("(k p) -> p k", p=P)).then_inc(loaded, 16)
                sp.dma_start(C["wkv"][:, :], C["w_kvb"]).then_inc(loaded, 16)

            @block.tensor
            def _(pe):
                for t in range(NT):
                    cols = slice(t * P, (t + 1) * P)
                    for k in range(KT):
                        if t == 0:
                            pe.wait_ge(w_split, k + 1)
                        mm = multiply_split(pe, ps[:, t, 0:C_LAT], (h[:, 0, k, cols], h[:, 1, k, cols]), (w[:, 0, k, :], w[:, 1, k, :]), k == 0, k == KT - 1)
                    mm.then_inc(made, 1)
                pe.wait_ge(copied, NT)
                pe.wait_ge(roped, 1)
                for t in range(NT):
                    pe.wait_ge(scaled, 2 * t + 2)
                    for j in range(3):
                        pe.transpose(ps[:, t, j * P:(j + 1) * P], ck[:, t, j * P:(j + 1) * P], ident[:, :])
                    pe.transpose(ps[0:C_QK, t, 3 * P:4 * P], kp[:, t, :], ident[:, :]).then_inc(turned, 1)

            @block.scalar
            def _(act):
                for k in range(KT):
                    act.wait_ge(raw_loaded[k % 2], 16 * (k // 2 + 1))
                    act.activation(w[:, 0, k, :], raw[:, k % 2, :], ACT.Copy).then_inc(w_high, 1)
                act.wait_ge(ang_ready, 1)
                act.activation(sn[:, :, :], red[:, :, :], ACT.Sin).then_inc(tables, 1)
                act.activation(cs[:, :, :], mag[:, :, :], ACT.Sin).then_inc(tables, 1)
                for t in range(NT):
                    act.wait_ge(made, t + 1)
                    act.activation(ck[:, t, :], ps[:, t, 0:C_LAT], ACT.Copy).then_inc(copied, 1)
                    act.wait_ge(copied, t + 1)
                    if t:
                        act.wait_ge(summed, 2 * t)
                    act.activation(sq[:, :], ck[:, t, 0:C_QR], ACT.Square, accum_out=ss[:, 0, t:t + 1]).then_inc(summed, 1)
                    act.wait_ge(summed, 2 * t + 1)
                    act.activation(sq[:, 0:C_KVR], ck[:, t, C_QR:C_QR + C_KVR], ACT.Square, accum_out=ss[:, 1, t:t + 1]).then_inc(summed, 1)
                act.wait_ge(var_ready, 1)
                act.activation(std[:, :, :], var[:, :, :], ACT.Sqrt).then_inc(std_ready, 1)
                for t in range(NT):
                    act.wait_ge(turned, t + 1)
                    for j in range(2):
                        act.activation(C["cqT"][:, j, t * P:(t + 1) * P], ps[:, t, j * P:(j + 1) * P], ACT.Copy, scale=gq[:, j:j + 1]).then_inc(out_act, 1)

            @block.vector
            def _(dve):
                link = Chain(dve, chain)
                dve.memset(kp[:, :, 0:C_NOPE], 0.0).then_inc(chain, 1)
                link.n = 1
                for k in range(KT):
                    dve.wait_ge(w_high, k + 1)
                    low_part(dve, w[:, 1, k, :], raw[:, k % 2, :], w[:, 0, k, :]).then_inc(w_split, 1)
                dve.wait_ge(loaded, 16 * n_loads)
                link(dve.tensor_copy(pos[:, :], pos_i[:, :]))
                link(dve.tensor_tensor(ang[:, :, :], pos[:, :].rearrange("p (t a) -> p t a", a=1).to_broadcast([P, NT, ROPE_HALF]),
                                       fr[:, :].rearrange("p (a f) -> p a f", a=1).to_broadcast([P, NT, ROPE_HALF]), ALU.mult))
                link(dve.tensor_scalar(turns[:, :, :], ang[:, :, :], 1.0 / TWO_PI, None, ALU.mult))
                link(dve.tensor_scalar(turns[:, :, :], turns[:, :, :], ROUND, None, ALU.add))
                link(dve.tensor_scalar(turns[:, :, :], turns[:, :, :], ROUND, None, ALU.subtract))
                link(dve.scalar_tensor_tensor(out=red[:, :, :], in0=turns[:, :, :], scalar=-TWO_PI_1, in1=ang[:, :, :], op0=ALU.mult, op1=ALU.add))
                link(dve.scalar_tensor_tensor(out=red[:, :, :], in0=turns[:, :, :], scalar=-TWO_PI_2, in1=red[:, :, :], op0=ALU.mult, op1=ALU.add))
                link(dve.scalar_tensor_tensor(out=red[:, :, :], in0=turns[:, :, :], scalar=-TWO_PI_3, in1=red[:, :, :], op0=ALU.mult, op1=ALU.add))
                link(dve.tensor_scalar(red[:, :, :], red[:, :, :], PI_BELOW, -PI_BELOW, ALU.min, ALU.max))
                link(dve.scalar_tensor_tensor(out=mag[:, :, :], in0=red[:, :, :], scalar=-1.0, in1=red[:, :, :], op0=ALU.mult, op1=ALU.max))
                dve.tensor_scalar(mag[:, :, :], mag[:, :, :], -1.0, math.pi / 2, ALU.mult, ALU.add).then_inc(ang_ready, 1)
                dve.wait_ge(copied, NT)
                dve.wait_ge(tables, 2)
                t1, t2 = ck[:, :, C_QR + C_KVR:C_QR + C_KVR + ROPE_HALF], ck[:, :, C_QR + C_KVR + ROPE_HALF:C_LAT]
                link(dve.tensor_tensor(ra[:, :, :], t1, cs[:, :, :], ALU.mult))
                link(dve.tensor_tensor(rb[:, :, :], t2, sn[:, :, :], ALU.mult))
                link(dve.tensor_tensor(kp[:, :, C_NOPE:C_NOPE + ROPE_HALF], ra[:, :, :], rb[:, :, :], ALU.subtract))
                link(dve.tensor_tensor(ra[:, :, :], t1, sn[:, :, :], ALU.mult))
                link(dve.tensor_tensor(rb[:, :, :], t2, cs[:, :, :], ALU.mult))
                dve.tensor_tensor(kp[:, :, C_NOPE + ROPE_HALF:C_QK], ra[:, :, :], rb[:, :, :], ALU.add).then_inc(roped, 1)
                dve.wait_ge(summed, 2 * NT)
                link(dve.tensor_scalar(var[:, 0, :], ss[:, 0, :], 1.0 / C_QR, EPS, ALU.mult, ALU.add))
                dve.tensor_scalar(var[:, 1, :], ss[:, 1, :], 1.0 / C_KVR, EPS, ALU.mult, ALU.add).then_inc(var_ready, 1)
                dve.wait_ge(std_ready, 1)
                link(dve.reciprocal(rs[:, :, :], std[:, :, :]))
                for t in range(NT):
                    dve.tensor_scalar(ck[:, t, 0:C_QR], ck[:, t, 0:C_QR], rs[:, 0, t:t + 1], None, ALU.mult).then_inc(scaled, 1)
                    dve.tensor_scalar(ck[:, t, C_QR:C_QR + C_KVR], ck[:, t, C_QR:C_QR + C_KVR], rs[:, 1, t:t + 1], None, ALU.mult).then_inc(scaled, 1)
                for t in range(NT):
                    dve.wait_ge(turned, t + 1)
                    dve.wait_ge(out_act, 2 * (t + 1))
                    cols = slice(t * P, (t + 1) * P)
                    dve.tensor_scalar(C["ckvT"][:, cols], ps[:, t, 2 * P:3 * P], gkv[:, 0:1], None, ALU.mult).then_inc(out_dve, 1)
                    for slot in range(2):
                        dve.tensor_copy(C["kT"][C_NOPE:C_QK, slot, cols], ps[C_NOPE:C_QK, t, 3 * P:4 * P]).then_inc(out_dve, 1)


def latent_queries(nc, K, C, w_qb):
    ps, ident = K["ps"], K["ident"]
    W = C_HEADS * C_QK
    with ExitStack() as ctx:
        sc = Scope(nc, ctx, "lq")
        wq = sc.sb("wq", [P, QR_T, W])
        qt = sc.sb("qt", [P, 2, C_HEADS, C_QK])
        ra, rb, rc = [sc.sb(n, [P, C_HEADS, ROPE_HALF]) for n in ("ra", "rb", "rc")]
        loaded, q_made, q_out, v_made, v_out, roped, turned, out_act, out_dve, chain = [sc.sem(n) for n in
            ("loaded", "q_made", "q_out", "v_made", "v_out", "roped", "turned", "out_act", "out_dve", "chain")]
        with nc.Block() as block:
            @block.sync
            def _(sp):
                sp.dma_start(wq[:, :, :], tiled_rows(w_qb)).then_inc(loaded, 16)

            @block.tensor
            def _(pe):
                def turn(t, b):
                    pe.wait_ge(roped, t + 1)
                    for n in range(2):
                        u = 2 * t + b
                        if n == 0 and u:
                            pe.wait_ge(out_act, u)
                            pe.wait_ge(out_dve, u)
                        for j in range(4):
                            mm = pe.transpose(ps[0:C_QK, 6 + n, j * P:(j + 1) * P], qt[:, t % 2, 8 * b + 4 * n + j, :], ident[:, :])
                    mm.then_inc(turned, 1)

                pe.wait_ge(loaded, 16)
                wv = C["wkv"][:, :].rearrange("p (h x) -> p h x", x=C_NOPE + C_V)
                for t in range(NT):
                    cols = slice(t * P, (t + 1) * P)
                    if t:
                        pe.wait_ge(q_out, t)
                    for n in range(3):
                        for k in range(QR_T):
                            mm = pe.matmul(ps[:, n, :], C["cqT"][:, k, cols], wq[:, k, n * HALF:(n + 1) * HALF], start=(k == 0), stop=(k == QR_T - 1))
                    mm.then_inc(q_made, 1)
                    if t:
                        turn(t - 1, 0)
                        pe.wait_ge(v_out, t)
                    for n in range(2):
                        mm = pe.matmul(ps[:, 4 + n, :], C["ckvT"][:, cols], wv[:, 8 * n:8 * n + 8, C_NOPE:], start=True, stop=True)
                    mm.then_inc(v_made, 1)
                    if t:
                        turn(t - 1, 1)
                turn(NT - 1, 0)
                turn(NT - 1, 1)

            def out(act, t, b):
                act.wait_ge(turned, 2 * t + b + 1)
                dst = C["qT"](8 * b)
                act.activation(dst[0:C_QK, 0:4, t * P:(t + 1) * P], ps[0:C_QK, 6, :].rearrange("p (h t) -> p h t", t=P), ACT.Copy).then_inc(out_act, 1)

            @block.scalar
            def _(act):
                for t in range(NT):
                    act.wait_ge(q_made, t + 1)
                    if t >= 2:
                        act.wait_ge(turned, 2 * (t - 1))
                    flat = qt[:, t % 2, :, :].rearrange("p h x -> p (h x)")
                    for n in range(3):
                        i = act.activation(flat[:, n * HALF:(n + 1) * HALF], ps[:, n, :], ACT.Copy)
                    i.then_inc(q_out, 1)
                    if t:
                        out(act, t - 1, 0)
                    act.wait_ge(v_made, t + 1)
                    for n in range(2):
                        i = act.activation(C["v"][:, t, n * HALF:(n + 1) * HALF], ps[:, 4 + n, :], ACT.Copy)
                    i.then_inc(v_out, 1)
                    if t:
                        out(act, t - 1, 1)
                out(act, NT - 1, 0)
                out(act, NT - 1, 1)

            @block.vector
            def _(dve):
                link = Chain(dve, chain)

                def outd(t):
                    for b in range(2):
                        dve.wait_ge(turned, 2 * t + b + 1)
                        dst = C["qT"](8 * b)
                        dve.tensor_copy(dst[0:C_QK, 4:8, t * P:(t + 1) * P], ps[0:C_QK, 7, :].rearrange("p (h t) -> p h t", t=P)).then_inc(out_dve, 1)

                for t in range(NT):
                    dve.wait_ge(q_out, t + 1)
                    t1, t2 = qt[:, t % 2, :, C_NOPE:C_NOPE + ROPE_HALF], qt[:, t % 2, :, C_NOPE + ROPE_HALF:]
                    cs = C["cos"][:, t:t + 1, :].to_broadcast([P, C_HEADS, ROPE_HALF])
                    sn = C["sin"][:, t:t + 1, :].to_broadcast([P, C_HEADS, ROPE_HALF])
                    link(dve.tensor_tensor(ra[:, :, :], t2, sn, ALU.mult))
                    link(dve.tensor_tensor(rb[:, :, :], t1, sn, ALU.mult))
                    link(dve.tensor_tensor(rc[:, :, :], t2, cs, ALU.mult))
                    link(dve.tensor_tensor(t1, t1, cs, ALU.mult))
                    link(dve.tensor_tensor(t1, t1, ra[:, :, :], ALU.subtract))
                    dve.tensor_tensor(t2, rb[:, :, :], rc[:, :, :], ALU.add).then_inc(roped, 1)
                    if t:
                        outd(t - 1)
                outd(NT - 1)


def latent_attention(nc, K, C, oT):
    ps, ident = K["ps"], K["ident"]
    NU = C_HEADS * NT
    with ExitStack() as ctx:
        sc = Scope(nc, ctx, "lattn")
        SB = 3
        s_sb = sc.sb("s", [P, SB, S])
        pT = [sc.sb("pT0", [P, 4, HALF]), sc.sb("pT1", [P, 8, HALF])]
        mx, nm, den, rden = [sc.sb(n, [P, 2]) for n in ("mx", "nm", "den", "rden")]
        s_made, s_masked, m_ready, p_ready, n_ready, turned, pt_out, o_made, o_out, k_made, k_out, chain = [sc.sem(n) for n in
            ("s_made", "s_masked", "m_ready", "p_ready", "n_ready", "turned", "pt_out", "o_made", "o_out", "k_made", "k_out", "chain")]

        pieces = [[(b, min(b + 4, u % NT + 1)) for b in range(0, u % NT + 1, 4)] for u in range(NU)]
        first_piece = [sum(len(p) for p in pieces[:u]) for u in range(NU + 1)]

        with nc.Block() as block:
            @block.tensor
            def _(pe):
                def keys(h):
                    for half in range(NH):
                        if 2 * h + half:
                            pe.wait_ge(k_out, 2 * h + half)
                        pe.matmul(ps[0:C_NOPE, 7, :], C["wkv"][:, h * (C_NOPE + C_V):h * (C_NOPE + C_V) + C_NOPE],
                                  C["ckvT"][:, half * HALF:(half + 1) * HALF], start=True, stop=True).then_inc(k_made, 1)

                def scores(u):
                    h, i = u // NT, u % NT
                    if i == 0:
                        pe.wait_ge(k_out, 2 * h + 2)
                    if u >= 2:
                        pe.wait_ge(p_ready, u - 1)
                    q = C["qT"](h)[0:C_QK, 0, i * P:(i + 1) * P]
                    w = (i + 1) * P
                    for n in range((w + HALF - 1) // HALF):
                        c1 = min(w, (n + 1) * HALF)
                        mm = pe.matmul(ps[:, 2 * (u % 2) + n, 0:c1 - n * HALF], q, C["kT"][0:C_QK, h % 2, n * HALF:c1], start=True, stop=True)
                    mm.then_inc(s_made, 1)

                def turn(u):
                    pe.wait_ge(n_ready, u + 1)
                    for r, (b0, b1) in enumerate(pieces[u], first_piece[u]):
                        if r >= 2:
                            pe.wait_ge(pt_out, r - 1)
                        for b in range(b0, b1):
                            mm = pe.transpose(ps[:, 4 + r % 2, (b - b0) * P:(b - b0 + 1) * P], s_sb[:, u % SB, b * P:(b + 1) * P], ident[:, :])
                        mm.then_inc(turned, 1)

                def values(g):
                    h, half = g // 2, g % 2
                    pe.wait_ge(pt_out, first_piece[4 * (g + 1)])
                    if g:
                        pe.wait_ge(o_out, g)
                    orow = slice((h % 2) * C_V, (h % 2 + 1) * C_V)
                    nb = 4 * (half + 1)
                    for b in range(nb):
                        q0 = max(0, b * P - half * HALF)
                        mm = pe.matmul(ps[orow, 6, q0:HALF], C["v"][:, b, h * C_V:(h + 1) * C_V], pT[half][:, b, q0:HALF],
                                       start=(b == 0), stop=(b == nb - 1), skip_group_check=True)
                    mm.then_inc(o_made, 1)

                keys(0)
                scores(0)
                scores(1)
                for u in range(NU):
                    h, i = u // NT, u % NT
                    if i == 3 and h + 1 < C_HEADS:
                        keys(h + 1)
                    if i == 7:
                        values(2 * h)
                    if i == 1 and h:
                        values(2 * h - 1)
                    if u + 2 < NU:
                        scores(u + 2)
                    turn(u)
                values(NU // 4 - 1)

            @block.scalar
            def _(act):
                def keys_out(h):
                    for half in range(NH):
                        act.wait_ge(k_made, 2 * h + half + 1)
                        act.activation(C["kT"][0:C_NOPE, h % 2, half * HALF:(half + 1) * HALF], ps[0:C_NOPE, 7, :], ACT.Copy).then_inc(k_out, 1)

                def probabilities(u):
                    w = (u % NT + 1) * P
                    act.wait_ge(m_ready, u + 1)
                    src = ps[:, 2 * (u % 2):2 * (u % 2) + 2, :].rearrange("p a n -> p (a n)")
                    act.activation(s_sb[:, u % SB, 0:w], src[:, 0:w], ACT.Exp, scale=C_SCALE, bias=nm[:, u % 2:u % 2 + 1],
                                   accum_out=den[:, u % 2:u % 2 + 1]).then_inc(p_ready, 1)

                keys_out(0)
                probabilities(0)
                for u in range(NU):
                    h, i = u // NT, u % NT
                    if i == 3 and h + 1 < C_HEADS:
                        keys_out(h + 1)
                    if u + 1 < NU:
                        if u + 1 >= SB:
                            act.wait_ge(turned, first_piece[u + 2 - SB])
                        probabilities(u + 1)
                    half = i // 4
                    if i % 4 == 0:
                        g = u // 4
                        if g >= 2:
                            act.wait_ge(o_made, g - 1)
                    for r, (b0, b1) in enumerate(pieces[u], first_piece[u]):
                        act.wait_ge(turned, r + 1)
                        src = ps[:, 4 + r % 2, :].rearrange("p (b t) -> p b t", t=P)
                        act.activation(pT[half][:, b0:b1, (i % 4) * P:(i % 4 + 1) * P], src[:, 0:b1 - b0, :], ACT.Copy).then_inc(pt_out, 1)

            @block.vector
            def _(dve):
                link = Chain(dve, chain)

                def maxima(u):
                    i = u % NT
                    w = (i + 1) * P
                    dve.wait_ge(s_made, u + 1)
                    src = ps[:, 2 * (u % 2):2 * (u % 2) + 2, :].rearrange("p a n -> p (a n)")
                    diag = src[:, i * P:w]
                    link(dve.tensor_tensor(diag, diag, K["neg_after"][:, :], ALU.add))
                    link(dve.tensor_reduce(mx[:, u % 2:u % 2 + 1], src[:, 0:w], AX.X, ALU.max))
                    dve.tensor_scalar(nm[:, u % 2:u % 2 + 1], mx[:, u % 2:u % 2 + 1], -C_SCALE, None, ALU.mult).then_inc(m_ready, 1)

                def normalise(u):
                    w = (u % NT + 1) * P
                    dve.wait_ge(p_ready, u + 1)
                    link(dve.reciprocal(rden[:, u % 2:u % 2 + 1], den[:, u % 2:u % 2 + 1]))
                    dve.tensor_scalar(s_sb[:, u % SB, 0:w], s_sb[:, u % SB, 0:w], rden[:, u % 2:u % 2 + 1], None, ALU.mult).then_inc(n_ready, 1)

                def take_out(g):
                    h, half = g // 2, g % 2
                    dve.wait_ge(o_made, g + 1)
                    orow = slice((h % 2) * C_V, (h % 2 + 1) * C_V)
                    dst = oT[orow, h // 2, half * HALF:(half + 1) * HALF]
                    dve.tensor_tensor(dst, dst, ps[orow, 6, :], ALU.mult).then_inc(o_out, 1)

                maxima(0)
                for u in range(NU):
                    if u + 1 < NU:
                        maxima(u + 1)
                    normalise(u)
                    if u % NT == 7:
                        take_out(2 * (u // NT))
                    if u % NT == 2 and u > NT:
                        take_out(2 * (u // NT) - 1)
                take_out(NU // 4 - 1)


def build(nc, A, out, invcnt, onehot, inv_freq):
    with ExitStack() as ctx:
        def sb(name, shape, dt=F32):
            return ctx.enter_context(nc.sbuf_tensor(name, shape, dt))

        ctx.enter_context(nc.allow_non_contiguous_dma(reason="gains and taps of one element a partition"))
        K = {
            "X": sb("X", [P, NT, D]), "ss": sb("ss", [P, NT]), "ident": sb("ident", [P, P]), "ones": sb("ones", [P, P]),
            "neg_after": sb("neg_after", [P, P]), "neg_before": sb("neg_before", [P, P]), "earlier": sb("earlier", [P, P]),
            "sel_neg": sb("sel_neg", [HEADS, HEADS, P]), "sel_one": sb("sel_one", [HEADS, HEADS, P]),
            "ps": ctx.enter_context(nc.psum_tensor("ps", [P, 8, HALF], F32)),
        }
        y_dram = nc.dram_tensor("y_rows", [SLOTS_B * P, D], F32).ap()
        make_constants(nc, K)
        load_x(nc, K, A["x"][0])
        w_in = A["w_in"][0]
        with ExitStack() as mctx:
            K["hT"] = K["X"]
            norm_transpose(nc, K, A["g_mix"][0], "n1", in_place=True)
            def msb(name, shape, dt=F32):
                return mctx.enter_context(nc.sbuf_tensor("mix_" + name, shape, dt))
            M = {"yT": msb("yT", [P, 4, S]), "hmT": msb("hmT", [P, HEADS, S]), "ghead": msb("ghead", [P, HEADS]),
                 "g_head_dram": A["g_head"][0]}
            with ExitStack() as ictx:
                def isb(name, shape, dt=F32):
                    return ictx.enter_context(nc.sbuf_tensor("mixin_" + name, shape, dt))
                M.update({"qT": isb("qT", [P, HEADS, S]), "kT": isb("kT", [P, HEADS, S]), "og": isb("og", [P, HEADS, S]),
                          "v": isb("v", [P, NT, HEADS, DH + 1]), "U": isb("U", [HEADS, NC, P]),
                          "G": isb("G", [HEADS, NC, P]), "SP": isb("SP", [P, HEADS, NC])})
                M["R"] = isb("R", [P, S])
                M["RT"] = isb("RT", [P, NC, P])
                M["dT"] = M["hmT"]
                mixer_projections(nc, K, M, w_in, A["b_if"][0], A["conv_q"][0], A["conv_k"][0], A["w_pool"][0], A["pool_scale"][0], invcnt)
                mlstm(nc, K, M)
            mixer_merge(nc, K, M, K["hT"], w_in, A["w_br_a"][0], A["w_br_b"][0], K["X"], y_dram)
        project_add(nc, K, K["X"], A["w_out"][0], "wout", x_dram=A["x"][0], over_x=True)
        with ExitStack() as ectx:
            def esb(name, shape, dt=F32):
                return ectx.enter_context(nc.sbuf_tensor("routed_" + name, shape, dt))
            h_dram = nc.dram_tensor("h_rows", [S, D], F32).ap()
            slot_tok = nc.dram_tensor("slot_tok", [SLOTS_B * P, 1], I32).ap()
            R = {"idx": esb("idx", [P, SLOTS_B], I32), "dest": esb("dest", [P, TOP_K, NT], I32), "gate": esb("gate", [P, TOP_K, NT]),
                 "block_e": esb("block_e", [1, SLOTS_B], I32), "n_blocks": esb("n_blocks", [1, 1], I32)}
            with nc.sbuf_tensor("hT_moe", [P, KT, S], F32) as hT:
                K["hT"] = hT
                norm_transpose(nc, K, A["g_ffn"][0], "n2", h_dram)
                route(nc, K, R, A["w_rg"][0], A["b_rg"][0], A["w_re"][0], A["b_re"][0], slot_tok)
            experts(nc, K, R, h_dram, y_dram, A["w_e_gate"][0], A["w_e_up"][0], A["w_e_down"][0])
            combine(nc, K, R, y_dram)
        x3_dram = nc.dram_tensor("x3_rows", [S, D], F32).ap()
        norm_rows(nc, K, A["g_final"], "nf", x3_dram)
        with ExitStack() as actx:
            vb_dram = nc.dram_tensor("vb_rows", [S, B_WIDTH], F32).ap()
            G_dram = nc.dram_tensor("bias_strips", [A_HEADS + B_HEADS, len(DILATIONS), BAND], F32).ap()
            oT = actx.enter_context(nc.sbuf_tensor("ab_oT", [P, KT, S], F32))
            B = {"qb": K["X"][:, 0:4, :], "kb": K["X"][:, 4:8, :]}
            w_ab = A["ab_w_in_2"][0]
            with ExitStack() as a1:
                B["qa"] = a1.enter_context(nc.sbuf_tensor("ab_qa", [P, 4, S], F32))
                B["ka"] = a1.enter_context(nc.sbuf_tensor("ab_ka", [P, 1, S], F32))
                B["va"] = a1.enter_context(nc.sbuf_tensor("ab_va", [P, NT, P], F32))
                with nc.sbuf_tensor("ab_h", [P, 2, KT, S], F32R) as h:
                    norm_transpose(nc, K, A["norm_w_2"][0], "n3", halves=h)
                    ab_projections(nc, K, B, h, oT, w_ab, vb_dram)
                T = {"A": a1.enter_context(nc.sbuf_tensor("ab_biasA", [P, A_HEADS, 2 * P], F32))}
                bias_tables(nc, K, T, G_dram, A["rel_bias_2"], onehot, "A")
                banded_attention(nc, K, B, T, oT, "A", None, A["ab_sinks_2"][0])
            with ExitStack() as a2:
                T = {"B0": a2.enter_context(nc.sbuf_tensor("ab_biasB0", [P, B_HEADS, 2 * P], F32)),
                     "B1": a2.enter_context(nc.sbuf_tensor("ab_biasB1", [P, B_HEADS, 2 * P], F32)),
                     "B2": a2.enter_context(nc.sbuf_tensor("ab_biasB2", [P, B_HEADS, 64], F32))}
                bias_tables(nc, K, T, G_dram, A["rel_bias_2"], onehot, "B")
                banded_attention(nc, K, B, T, oT, "B", vb_dram, None)
            project_add(nc, K, oT, A["ab_w_out_2"][0], "abo", x_dram=x3_dram)
        with ExitStack() as cctx:
            x4_dram = nc.dram_tensor("x4_rows", [S, D], F32).ap()
            w_c = A["c_w_in_2"][0]
            oT = cctx.enter_context(nc.sbuf_tensor("c_oT", [P, KT, S], F32))
            with ExitStack() as qctx:
                def qsb(name, shape):
                    return qctx.enter_context(nc.sbuf_tensor("c_" + name, shape, F32))
                C = {"ckvT": qsb("ckvT", [P, S]), "kT": qsb("kT", [C_QK, 2, S]), "wkv": qsb("wkv", [P, C_HEADS * (C_NOPE + C_V)]),
                     "w_kvb": A["c_w_kvb_2"][0], "cos": qsb("cos", [P, NT, ROPE_HALF]), "sin": qsb("sin", [P, NT, ROPE_HALF]),
                     "cqT": qsb("cqT", [P, QR_T, S]),
                     "v": K["X"]}
                with nc.sbuf_tensor("c_h", [P, 2, KT, S], F32R) as h:
                    norm_transpose(nc, K, A["norm_w_2"][1], "n4", halves=h)
                    gate(nc, K, h, oT, w_c, C_LAT, "cz", x4_dram)
                    latents(nc, K, C, h, w_c, A["c_q_norm_2"][0], A["c_kv_norm_2"][0], A["positions_2"][0], inv_freq)
                q = qsb("q", [C_QK, C_HEADS, S])
                C["qT"] = lambda h: q[:, h:, :]
                latent_queries(nc, K, C, A["c_w_qb_2"][0])
                latent_attention(nc, K, C, oT)
            project_add(nc, K, oT, A["c_w_out_2"][0], "co", x4_dram)
        norm_rows(nc, K, A["final_norm_2"], "nout", out, last=True)


_INS = ["x", "g_mix", "w_in", "b_if", "conv_q", "conv_k", "g_head", "w_pool", "pool_scale", "w_br_a", "w_br_b", "w_out",
        "g_ffn", "w_rg", "b_rg", "w_re", "b_re", "w_e_gate", "w_e_up", "w_e_down", "g_final", "positions_2", "norm_w_2",
        "rel_bias_2", "ab_w_in_2", "ab_sinks_2", "ab_w_out_2", "c_w_in_2", "c_q_norm_2", "c_w_qb_2", "c_kv_norm_2",
        "c_w_kvb_2", "c_w_out_2", "final_norm_2"]


def kernel(**inputs):
    import numpy as _np
    import concourse.bacc as _bacc
    from concourse import mybir as _mybir
    from concourse.bass_utils import run_bass_kernel_spmd as _run

    nc = _bacc.Bacc("TRN2", target_bir_lowering=False, num_devices=1)
    arrays, aps = {}, {}

    def give(name, a):
        arrays[f"in_{name}_dram"] = a
        return nc.dram_tensor(f"in_{name}_dram", a.shape, _mybir.dt.from_np(a.dtype), kind="ExternalInput").ap()

    for name in _INS:
        aps[name] = give(name, _np.ascontiguousarray(inputs[name]))
    invcnt, onehot, inv_freq = [give(n, f()) for n, f in
                                (("window_reciprocals", window_reciprocals), ("bucket_onehot", bucket_onehot),
                                 ("inverse_frequencies", inverse_frequencies))]
    out = nc.dram_tensor("out_0_dram", (S, D), _mybir.dt.float32, kind="ExternalOutput").ap()
    build(nc, aps, out, invcnt, onehot, inv_freq)
    r = _run(nc, [arrays], core_ids=[0])
    return r.results[0]["out_0_dram"].reshape(1, S, D)
```
